# Optimizing a Trainium2 kernel written in Bass

```python
import math
import jax
import jax.numpy as jnp
from jax import lax
import numpy as np

D_MODEL = 1024
BATCH = 1
SEQ = 256
DEPTH = 2

N_A = DEPTH // 2
N_B = DEPTH - N_A
S5_GROUP = 16
S5_WIDTH = D_MODEL
S5_GROUPS = S5_WIDTH // S5_GROUP
S5_STATE = 64
HEAD_DIM = 64
N_HEADS = D_MODEL // HEAD_DIM
N_KV_HEADS = 4
Q_PER_KV = N_HEADS // N_KV_HEADS
WINDOW = 128
ATTN_BLOCK = 128
ROPE_THETA = 10000.0
PEER_HEADS = 8
PEER_KEY_DIM = 128
PEER_HALF = PEER_KEY_DIM // 2
PEER_N_KEYS = 128
PEER_N_EXPERTS = PEER_N_KEYS * PEER_N_KEYS
PEER_TOPK = 16
PEER_TOKEN_BLOCK = 128
N_COND = 6 * DEPTH + 4
RMS_EPS = 1e-6
NEG_INF = -1e30

kernel_name = "yoco_s5_swa_sink_peer_adaln"

def rmsnorm(x, g):
    x32 = x.astype(jnp.float32)
    y = x32 * lax.rsqrt(jnp.mean(x32 * x32, axis=-1, keepdims=True) + RMS_EPS)
    return (y * g.astype(jnp.float32)).astype(x.dtype)

def modulate(h, shift, scale):
    return h * (1 + scale[:, None, :]) + shift[:, None, :]

def rope_tables(positions):
    inv_freq = ROPE_THETA ** (-jnp.arange(0, HEAD_DIM, 2, dtype=jnp.float32) / HEAD_DIM)
    ang = positions.astype(jnp.float32)[..., None] * inv_freq
    return jnp.cos(ang)[:, :, None, :], jnp.sin(ang)[:, :, None, :]

def apply_rope(t, cos, sin):
    cos = cos.astype(t.dtype)
    sin = sin.astype(t.dtype)
    t1, t2 = jnp.split(t, 2, axis=-1)
    return jnp.concatenate([t1 * cos - t2 * sin, t2 * cos + t1 * sin], axis=-1)

def s5_discretize(a_re, a_im, log_dt, b_re, b_im):
    a_re = a_re.astype(jnp.float32)
    a_im = a_im.astype(jnp.float32)
    b_re = b_re.astype(jnp.float32)
    b_im = b_im.astype(jnp.float32)
    dt = jnp.exp(log_dt.astype(jnp.float32))[:, None]
    mag = jnp.exp(a_re * dt)
    lb_re = mag * jnp.cos(a_im * dt)
    lb_im = mag * jnp.sin(a_im * dt)
    nr = lb_re - 1.0
    ni = lb_im
    den = a_re * a_re + a_im * a_im
    coef_re = (nr * a_re + ni * a_im) / den
    coef_im = (ni * a_re - nr * a_im) / den
    bb_re = coef_re[..., None] * b_re - coef_im[..., None] * b_im
    bb_im = coef_re[..., None] * b_im + coef_im[..., None] * b_re
    return lb_re, lb_im, bb_re, bb_im

def s5_scan_one(u, lb_re, lb_im, bb_re, bb_im, c_re, c_im, d):
    bu_re = jnp.einsum('gpc,sgc->sgp', bb_re, u)
    bu_im = jnp.einsum('gpc,sgc->sgp', bb_im, u)
    a_re = jnp.broadcast_to(lb_re, bu_re.shape)
    a_im = jnp.broadcast_to(lb_im, bu_im.shape)

    def combine(e1, e2):
        a1r, a1i, b1r, b1i = e1
        a2r, a2i, b2r, b2i = e2
        return (a2r * a1r - a2i * a1i,
                a2r * a1i + a2i * a1r,
                a2r * b1r - a2i * b1i + b2r,
                a2r * b1i + a2i * b1r + b2i)

    _, _, xr, xi = lax.associative_scan(combine, (a_re, a_im, bu_re, bu_im), axis=0)
    y = jnp.einsum('gcp,sgp->sgc', c_re, xr) - jnp.einsum('gcp,sgp->sgc', c_im, xi)
    return y + d * u

def s5_mixer(h, w_in, a_re, a_im, log_dt, b_re, b_im, c_re, c_im, d, w_glu, b_glu, w_out):
    B, S, _ = h.shape
    u = (h @ w_in).astype(jnp.float32).reshape(B, S, S5_GROUPS, S5_GROUP)
    lb_re, lb_im, bb_re, bb_im = s5_discretize(a_re, a_im, log_dt, b_re, b_im)
    c_re32 = c_re.astype(jnp.float32)
    c_im32 = c_im.astype(jnp.float32)
    d32 = d.astype(jnp.float32)
    y = lax.map(lambda ub: s5_scan_one(ub, lb_re, lb_im, bb_re, bb_im, c_re32, c_im32, d32), u)
    y = jax.nn.gelu(y.reshape(B, S, S5_WIDTH))
    y = y * jax.nn.sigmoid(y @ w_glu.astype(jnp.float32) + b_glu.astype(jnp.float32))
    return (y.astype(h.dtype) @ w_out).astype(h.dtype)

def shared_kv(x, g, shift, scale, w_kv, cos, sin):
    B, S, _ = x.shape
    h = modulate(rmsnorm(x, g), shift, scale)
    kv = h @ w_kv
    k, v = jnp.split(kv, 2, axis=-1)
    k = apply_rope(k.reshape(B, S, N_KV_HEADS, HEAD_DIM), cos, sin)
    v = v.reshape(B, S, N_KV_HEADS, HEAD_DIM)
    return k, v

def window_attention(h, k, v, w_q, sinks, w_o, cos, sin):
    B, S, _ = h.shape
    nb = S // ATTN_BLOCK
    q = apply_rope((h @ w_q).reshape(B, S, N_HEADS, HEAD_DIM), cos, sin)
    q = q.reshape(B, nb, ATTN_BLOCK, N_KV_HEADS, Q_PER_KV, HEAD_DIM)

    def band(t):
        tp = jnp.pad(t, ((0, 0), (ATTN_BLOCK, 0), (0, 0), (0, 0)))
        tp = tp.reshape(B, nb + 1, ATTN_BLOCK, N_KV_HEADS, HEAD_DIM)
        return jnp.concatenate([tp[:, :-1], tp[:, 1:]], axis=2)

    kb = band(k)
    vb = band(v)
    qi = jnp.arange(ATTN_BLOCK)[:, None]
    kj = jnp.arange(2 * ATTN_BLOCK)[None, :]
    diff = qi + ATTN_BLOCK - kj
    k_abs = (jnp.arange(nb)[:, None, None] - 1) * ATTN_BLOCK + kj[None]
    mask = (diff >= 0)[None] & (diff < WINDOW)[None] & (k_abs >= 0)
    s = jnp.einsum('bnqkgd,bnjkd->bnkgqj', q, kb).astype(jnp.float32) * (HEAD_DIM ** -0.5)
    s = jnp.where(mask[None, :, None, None, :, :], s, NEG_INF)
    sink = sinks.astype(jnp.float32).reshape(N_KV_HEADS, Q_PER_KV)[None, None, :, :, None, None]
    m = jnp.maximum(jnp.max(s, axis=-1, keepdims=True), sink)
    p = jnp.exp(s - m)
    p = p / (jnp.sum(p, axis=-1, keepdims=True) + jnp.exp(sink - m))
    o = jnp.einsum('bnkgqj,bnjkd->bnqkgd', p.astype(vb.dtype), vb)
    return o.reshape(B, S, N_HEADS * HEAD_DIM) @ w_o

def peer(h, w_q, sub_keys, u_tab, v_tab):
    B, S, D = h.shape
    T = B * S
    xt = h.reshape(T, D)
    q = (xt @ w_q).reshape(T, PEER_HEADS, 2, PEER_HALF)
    sc = jnp.einsum('thpd,hpnd->thpn', q, sub_keys).astype(jnp.float32)
    s_half, i_half = lax.top_k(sc, PEER_TOPK)
    cand = s_half[:, :, 0, :, None] + s_half[:, :, 1, None, :]
    cand_id = i_half[:, :, 0, :, None] * PEER_N_KEYS + i_half[:, :, 1, None, :]
    cand = cand.reshape(T, PEER_HEADS, PEER_TOPK * PEER_TOPK)
    cand_id = cand_id.reshape(T, PEER_HEADS, PEER_TOPK * PEER_TOPK)
    top_s, top_pos = lax.top_k(cand, PEER_TOPK)
    ids = jnp.take_along_axis(cand_id, top_pos, axis=-1)
    gates = jax.nn.softmax(top_s, axis=-1).astype(h.dtype)
    nblk = T // PEER_TOKEN_BLOCK
    ids = ids.reshape(nblk, PEER_TOKEN_BLOCK, PEER_HEADS * PEER_TOPK)
    gates = gates.reshape(nblk, PEER_TOKEN_BLOCK, PEER_HEADS * PEER_TOPK)
    xb = xt.reshape(nblk, PEER_TOKEN_BLOCK, D)

    def expert_block(args):
        xc, idc, gc = args
        act = jax.nn.gelu(jnp.einsum('td,tkd->tk', xc, u_tab[idc])) * gc
        return jnp.einsum('tk,tkd->td', act, v_tab[idc])

    out = lax.map(expert_block, (xb, ids, gates))
    return out.reshape(B, S, D)

def setup_inputs(seed: int = 0) -> dict:
    key = jax.random.key(seed)
    ks = jax.random.split(key, 32)
    f32 = jnp.float32
    B, S, D = BATCH, SEQ, D_MODEL

    def nrm(k, shape, s):
        return jax.random.normal(k, shape, f32) * s

    G, P, C = S5_GROUPS, S5_STATE, S5_GROUP
    n = jnp.arange(P, dtype=f32)
    return {
        "x": nrm(ks[0], (B, S, D), 1.0),
        "c": nrm(ks[1], (B, D), 1.0),
        "positions": jnp.broadcast_to(jnp.arange(S, dtype=jnp.int32)[None, :], (B, S)),
        "w_cond": nrm(ks[2], (D, N_COND * D), 0.5 * D ** -0.5),
        "b_cond": nrm(ks[3], (N_COND * D,), 0.02),
        "norm_mix": 1.0 + nrm(ks[4], (DEPTH, D), 0.02),
        "norm_ffn": 1.0 + nrm(ks[5], (DEPTH, D), 0.02),
        "s5_w_in": nrm(ks[6], (N_A, D, S5_WIDTH), D ** -0.5),
        "s5_a_re": -0.5 + nrm(ks[7], (N_A, G, P), 0.01),
        "s5_a_im": math.pi * n + nrm(ks[8], (N_A, G, P), 0.01),
        "s5_log_dt": jax.random.uniform(ks[9], (N_A, G), f32, math.log(1e-3), math.log(1e-1)),
        "s5_b_re": nrm(ks[10], (N_A, G, P, C), (2 * C) ** -0.5),
        "s5_b_im": nrm(ks[11], (N_A, G, P, C), (2 * C) ** -0.5),
        "s5_c_re": nrm(ks[12], (N_A, G, C, P), P ** -0.5),
        "s5_c_im": nrm(ks[13], (N_A, G, C, P), P ** -0.5),
        "s5_d": nrm(ks[14], (N_A, G, C), 1.0),
        "s5_w_glu": nrm(ks[15], (N_A, S5_WIDTH, S5_WIDTH), S5_WIDTH ** -0.5),
        "s5_b_glu": nrm(ks[16], (N_A, S5_WIDTH), 0.02),
        "s5_w_out": nrm(ks[17], (N_A, S5_WIDTH, D), S5_WIDTH ** -0.5),
        "kv_norm": 1.0 + nrm(ks[18], (D,), 0.02),
        "w_kv": nrm(ks[19], (D, 2 * N_KV_HEADS * HEAD_DIM), D ** -0.5),
        "attn_w_q": nrm(ks[20], (N_B, D, N_HEADS * HEAD_DIM), D ** -0.5),
        "attn_sinks": nrm(ks[21], (N_B, N_HEADS), 0.5),
        "attn_w_o": nrm(ks[22], (N_B, N_HEADS * HEAD_DIM, D), (N_HEADS * HEAD_DIM) ** -0.5),
        "peer_w_q": nrm(ks[23], (DEPTH, D, PEER_HEADS * PEER_KEY_DIM), D ** -0.5),
        "peer_sub_keys": nrm(ks[24], (DEPTH, PEER_HEADS, 2, PEER_N_KEYS, PEER_HALF), PEER_HALF ** -0.5),
        "peer_u": nrm(ks[25], (DEPTH, PEER_N_EXPERTS, D), D ** -0.5),
        "peer_v": nrm(ks[26], (DEPTH, PEER_N_EXPERTS, D), 1.0),
        "final_norm": 1.0 + nrm(ks[27], (D,), 0.02),
    }

def reference(x, c, positions, w_cond, b_cond, norm_mix, norm_ffn, s5_w_in, s5_a_re, s5_a_im,
              s5_log_dt, s5_b_re, s5_b_im, s5_c_re, s5_c_im, s5_d, s5_w_glu, s5_b_glu, s5_w_out,
              kv_norm, w_kv, attn_w_q, attn_sinks, attn_w_o, peer_w_q, peer_sub_keys, peer_u,
              peer_v, final_norm):
    B = x.shape[0]
    cond = (jax.nn.silu(c.astype(jnp.float32)) @ w_cond.astype(jnp.float32)
            + b_cond.astype(jnp.float32)).astype(x.dtype).reshape(B, N_COND, D_MODEL)
    cos, sin = rope_tables(positions)
    k_sh = None
    v_sh = None
    for i in range(DEPTH):
        m = cond[:, 6 * i:6 * i + 6]
        h = modulate(rmsnorm(x, norm_mix[i]), m[:, 0], m[:, 1])
        if i < N_A:
            a = i
            y = s5_mixer(h, s5_w_in[a], s5_a_re[a], s5_a_im[a], s5_log_dt[a], s5_b_re[a], s5_b_im[a],
                         s5_c_re[a], s5_c_im[a], s5_d[a], s5_w_glu[a], s5_b_glu[a], s5_w_out[a])
        else:
            b = i - N_A
            y = window_attention(h, k_sh, v_sh, attn_w_q[b], attn_sinks[b], attn_w_o[b], cos, sin)
        x = x + m[:, 2][:, None, :] * y
        h = modulate(rmsnorm(x, norm_ffn[i]), m[:, 3], m[:, 4])
        x = x + m[:, 5][:, None, :] * peer(h, peer_w_q[i], peer_sub_keys[i], peer_u[i], peer_v[i])
        if i == N_A - 1:
            k_sh, v_sh = shared_kv(x, kv_norm, cond[:, 6 * DEPTH], cond[:, 6 * DEPTH + 1], w_kv, cos, sin)
    return modulate(rmsnorm(x, final_norm), cond[:, 6 * DEPTH + 2], cond[:, 6 * DEPTH + 3])


_drawn_inputs = setup_inputs


def setup_inputs(seed=0):
    import zlib

    import numpy as np

    out = dict(_drawn_inputs(seed))
    spreads = {}
    factors = {'norm_mix': 3.529,
     's5_a_re': 22.349,
     's5_b_glu': 5.266,
     'kv_norm': 7.239,
     'attn_sinks': 64.0,
     'final_norm': 9.979}
    for name, (base, spread) in spreads.items():
        noise = np.random.default_rng([zlib.crc32(name.encode()), seed]).standard_normal(out[name].shape)
        drawn = base * np.exp(spread * noise) if base else spread * noise
        out[name] = jnp.asarray(drawn.astype(out[name].dtype))
    for name, factor in factors.items():
        out[name] = (out[name] * factor).astype(out[name].dtype)
    return out
```

```python
from contextlib import ExitStack

import concourse.bass as bass
from concourse import mybir
import numpy as np

F32 = mybir.dt.float32
F32R = mybir.dt.float32r
I32 = mybir.dt.int32
U32 = mybir.dt.uint32
ALU = mybir.AluOpType
ACT = mybir.ActivationFunctionType
AX = mybir.AxisListType

P = 128
D = 1024
KC = D // P
T = 256
TB = T // P
EB = 128
HALF = EB // 2
HEADS = 8
TOPK = 16
PAIRS = 32
SLOTS = 4
TWO_PI = 6.283185307179586
MAGIC = 12582912.0
MAGIC15 = 12582912.0 / 32768.0
NEG = -1e30

STREAM = [("cond_a", 16, 0), ("w_in", 8, 0), ("cond_b", 112, 0), ("w_glu", 8, 0), ("w_out", 8, 0),
          ("peer_q0", 8, 0), ("u0", 128, 1), ("v0", 128, 1),
          ("w_kv", 4, 0), ("attn_q", 8, 0), ("w_o", 8, 0),
          ("peer_q1", 8, 0), ("u1", 128, 1), ("v1", 128, 1)]


def positions_in_stream():
    at, n, plain, split = {}, 0, 0, 0
    for name, count, is_split in STREAM:
        at[name] = (n, plain, split)
        n += count
        plain += 0 if is_split else count
        split += count if is_split else 0
    return at


AT = positions_in_stream()


class Steps:

    def __init__(self, eng, sem):
        self.eng, self.sem, self.n = eng, sem, 0

    def add(self, ins):
        ins.then_inc(self.sem, 1)
        self.n += 1

    def sync(self):
        self.eng.wait_ge(self.sem, self.n)


def rounds(eng, n, body):
    body(0, True, False)
    with eng.Fori(1, n - 1) as r:
        body(r, False, False)
    body(n - 1, False, True)


def build(nc, x_t, c_col, b_cond, norms, ident_d, iota_d, time_d, w_cond, w_in, w_glu, w_out,
          s5_lam, s5_b, s5_c, s5_d, b_glu, peer_wq, keys_d, u_tab, v_tab,
          w_kv, attn_wq, w_o, sinks_d, pos_d, masks_d, rot_d, freq_d, out_t):
    ctx = ExitStack()
    with ctx:
        def sb(name, shape, dt=F32, c=ctx):
            return c.enter_context(nc.sbuf_tensor(name, shape, dt))

        def sem(name):
            return ctx.enter_context(nc.semaphore(name))

        xT = sb("xT", [P, KC, T])
        ident = sb("ident", [P, P])
        ones = sb("ones", [P, P])
        zeros = sb("zeros", [P, P])
        iota = sb("iota", [P, P])
        cond = sb("cond", [P, P])
        bcond = sb("bcond", [P, P])
        norm_sb = sb("norm_sb", [P, 6, KC])
        gs = sb("gs", [P, 6, KC])
        c_sb = sb("c_sb", [P, KC])
        silu_c = sb("silu_c", [P, KC])
        eps_sb = sb("eps_sb", [P, 2])
        big = sb("big", [P, EB * T])
        ring = sb("ring", [P, SLOTS, KC, P])
        HB = big[:, :].rearrange("p (i t) -> p i t", t=T)

        def area(at, *shape, dt=None):
            n = 1
            for s in shape:
                n *= s
            v = big[:, at:at + n]
            if dt is not None:
                v = v.bitcast(dt)
            if len(shape) == 2:
                return v.rearrange("p (a b) -> p a b", a=shape[0])
            if len(shape) == 3:
                return v.rearrange("p (a b c) -> p a b c", a=shape[0], b=shape[1])
            if len(shape) == 4:
                return v.rearrange("p (a b c d) -> p a b c d", a=shape[0], b=shape[1], c=shape[2])
            return v

        sq = area(0, KC, T)
        std = area(2048, T)
        rstd = area(2304, T)
        hT = area(16384, KC, T)
        cosT = area(0, PAIRS, T)
        sinT = area(8192, PAIRS, T)
        uT = area(18432, KC, T)
        bbt = area(20480, KC, 2, P)
        c_re = area(22528, PAIRS, 32)
        c_im = area(23552, PAIRS, 32)
        c_nre = area(24576, PAIRS, 32)
        b_re = area(25600, PAIRS, 32)
        b_im = area(26624, PAIRS, 32)
        bb_re = area(27648, PAIRS, 32)
        bb_im = area(28672, PAIRS, 32)
        yT = area(29696, KC, T)
        gl = area(20480, KC, T)
        y2 = area(16384, KC, T)
        sig = area(18432, KC, T)
        SC = [area(18432, HEADS, 2, P), area(20480, HEADS, 2, P)]
        CAND = area(22528, HEADS, TOPK, TOPK)
        EQ = area(24576, HEADS, TOPK, TOPK)
        KEYS = area(26624, HEADS, 2 * P)
        qT = area(28672, KC, T)
        r_at = 30720
        v_top = area(r_at, HEADS, 2, TOPK)
        ix_u = area(r_at + 256, HEADS, 2, TOPK, dt=U32)
        ix_f = area(r_at + 512, HEADS, 2, TOPK)
        t_top = area(r_at + 768, HEADS, TOPK)
        pos_u = area(r_at + 896, HEADS, TOPK, dt=U32)
        ab_u = area(r_at + 1024, 2, HEADS, TOPK, dt=U32)
        ab_f = area(r_at + 1280, 2, HEADS, TOPK)
        route = [area(2560, 3, HEADS, TOPK), area(2944, 3, HEADS, TOPK)]
        route = [area(r_at + 1536, 3, HEADS, TOPK), None]
        gsum = sb("gsum", [P, HEADS])
        route[1] = sb("route1", [P, 3, HEADS, TOPK])
        hkv = area(4096, KC, T)
        rcos = area(6144, T)
        rsin = area(6400, T)
        rtmp = area(6656, 4, T)
        pos_i = area(7680, T, dt=I32)
        qraw = area(18432, KC, T)
        qrot = area(20480, KC, T)
        kraw = area(22528, 2, T)
        krot = area(23040, 2, T)
        kdup = area(23552, 4, T)
        vN = area(24576, TB, T)
        oT = area(25088, KC, T)
        s_sb = [area(27136, 2, 2, T), area(28160, 2, 2, T)]
        pT = [area(29184, 2, 4, P), area(30208, 2, 4, P)]
        masks = area(31232, T)
        rot = area(31488, P)
        sinks = area(31616, 4, 4)
        freq = area(31632, 1)
        rowm = area(31648, 4)
        nrowm = area(31652, 4)
        rsum = area(31656, 4)
        esink = area(31660, 4)
        ropet = area(31744, 2, T)

        s5_mem = ExitStack()
        lam = sb("lam", [P, 3, PAIRS], c=s5_mem)
        dcol = sb("dcol", [P, KC], c=s5_mem)
        bglu = sb("bglu", [P, KC], c=s5_mem)
        tt = sb("tt", [P, T], c=s5_mem)
        sm = sb("sm", [P, 24, PAIRS], c=s5_mem)
        ang = sb("ang", [P, 4, T], c=s5_mem)
        bu = sb("bu", [P, 2, 2, T], c=s5_mem)
        m1 = sb("m1", [P, 2, 2, T], c=s5_mem)
        m2 = sb("m2", [P, 2, 2, T], c=s5_mem)
        wz = sb("wz", [P, 2, T], c=s5_mem)
        zz = sb("zz", [P, 2, 2, T], c=s5_mem)
        p1 = sb("p1", [P, 2, 2, T], c=s5_mem)
        p2 = sb("p2", [P, 2, 2, T], c=s5_mem)
        bbtmp = sb("bbtmp", [P, PAIRS, 32], c=s5_mem)
        s5_mem.close()
        h_hi = sb("h_hi", [P, KC, T], F32R)
        h_lo = sb("h_lo", [P, KC, T], F32R)
        w_hi = sb("w_hi", [P, 2, KC, P], F32R)
        w_lo = sb("w_lo", [P, 2, KC, P], F32R)
        a_hi = sb("a_hi", [P, 2, T], F32R)
        a_lo = sb("a_lo", [P, 2, T], F32R)
        eq_a = sb("eq_a", [P, 2, 4, HALF])
        one_hi = sb("one_hi", [P, 2, 4, HALF], F32R)
        one_lo = sb("one_lo", [P, 2, 4, HALF], F32R)
        one_b = sb("one_b", [P, 2, 4, P], F32R)
        i0T = sb("i0T", [P, T])
        i1T = sb("i1T", [P, T])
        g_hi = sb("g_hi", [P, T])
        g_lo = sb("g_lo", [P, T])

        bank = [ctx.enter_context(nc.psum_tensor(f"bank{i}", [P, 512], F32)) for i in range(8)]

        s_const = sem("s_const")
        s_s5in = sem("s_s5in")
        s_slot = [sem(f"s_slot{i}") for i in range(SLOTS)]
        s_plain = sem("s_plain")
        s_hi = sem("s_hi")
        s_lo = sem("s_lo")
        s_split = sem("s_split")
        s_evac = sem("s_evac")
        s_dve = sem("s_dve")
        s_act = sem("s_act")
        s_ones = sem("s_ones")
        s_silu = sem("s_silu")
        s_sq = sem("s_sq")
        s_ms = sem("s_ms")
        s_var = sem("s_var")
        s_std = sem("s_std")
        s_hn = sem("s_hn")
        s_h = sem("s_h")
        s_x = sem("s_x")
        s_ang = sem("s_ang")
        s_trig = sem("s_trig")
        s_trig0 = sem("s_trig0")
        s_rho = sem("s_rho")
        s_cneg = sem("s_cneg")
        s_bb = sem("s_bb")
        s_bbt = sem("s_bbt")
        s_bbev = sem("s_bbev")
        s_bu = sem("s_bu")
        s_buev = sem("s_buev")
        s_m1 = sem("s_m1")
        s_m2 = sem("s_m2")
        s_z = sem("s_z")
        s_p1 = sem("s_p1")
        s_p2 = sem("s_p2")
        s_y = sem("s_y")
        s_yev = sem("s_yev")
        s_gl = sem("s_gl")
        s_sig = sem("s_sig")
        s_y2 = sem("s_y2")
        s_keys = sem("s_keys")
        s_hhi = sem("s_hhi")
        s_hlo = sem("s_hlo")
        s_sc = sem("s_sc")
        s_scev = sem("s_scev")
        s_gsub = sem("s_gsub")
        s_gexp = sem("s_gexp")
        s_route = sem("s_route")
        s_rt = sem("s_rt")
        s_rtev = sem("s_rtev")
        s_eqa = sem("s_eqa")
        s_oneb = sem("s_oneb")
        s_onea = sem("s_onea")
        s_gmm = sem("s_gmm")
        s_gev = sem("s_gev")
        s_ahi = sem("s_ahi")
        s_alo = sem("s_alo")
        s_attin = sem("s_attin")
        s_rang = sem("s_rang")
        s_rtrig = sem("s_rtrig")
        s_rmm = sem("s_rmm")
        s_rope = sem("s_rope")
        s_kdup = sem("s_kdup")
        s_s = sem("s_s")
        s_sm = sem("s_sm")
        s_p = sem("s_p")
        s_pn = sem("s_pn")
        s_pt = sem("s_pt")
        s_ptev = sem("s_ptev")
        s_o = sem("s_o")
        s_oev = sem("s_oev")
        s_out = sem("s_out")

        SOURCE = {"w_in": w_in, "w_glu": w_glu, "w_out": w_out, "w_kv": w_kv, "attn_q": attn_wq,
                  "w_o": w_o, "peer_q0": peer_wq[0], "peer_q1": peer_wq[1],
                  "u0": u_tab[0], "v0": v_tab[0], "u1": u_tab[1], "v1": v_tab[1],
                  "cond_a": w_cond[0:16], "cond_b": w_cond[16:128]}
        PROJ = {}
        made = 0
        for name, count, _ in STREAM:
            if name[0] != "v" and not name.startswith("cond"):
                PROJ[name] = made
                made += count

        NORM_STATS = 5
        MIX0, FFN0, KVN, MIX1, FFN1, FINAL = range(6)
        SCALE = [1, 4, 13, 7, 10, 15]
        SHIFT = [0, 3, 12, 6, 9, 14]

        def vec(n, ch):
            return cond[:, n * KC + ch:n * KC + ch + 1]

        block = ctx.enter_context(nc.Block())

        @block.sync
        def _(sp):
            prev = None
            for name, count, is_split in STREAM:
                n0, plain0, split0 = AT[name]
                src = SOURCE[name]

                def load(r, j, freed, by_split):
                    if freed is not None:
                        sp.wait_ge(s_lo if by_split else s_plain, freed)
                    blk = src[r * SLOTS + j] if isinstance(r, int) else \
                        src[bass.ds(r * SLOTS + j, 1)].rearrange("a p n -> p (a n)")
                    sp.dma_start(ring[:, j].rearrange("p a b -> p (a b)"), blk).then_inc(s_slot[j], 16)

                for j in range(SLOTS):
                    if prev is None:
                        load(0, j, None, 0)
                    else:
                        before = split0 if prev[2] else plain0
                        load(0, j, before - SLOTS + j + 1, prev[2])
                first = split0 if is_split else plain0
                if count // SLOTS > 2:
                    with sp.Fori(1, count // SLOTS) as r:
                        for j in range(SLOTS):
                            load(r, j, r * SLOTS + (first - SLOTS + j + 1), is_split)
                else:
                    for r in range(1, count // SLOTS):
                        for j in range(SLOTS):
                            load(r, j, first + (r - 1) * SLOTS + j + 1, is_split)
                prev = (name, count, is_split)
            sp.wait_ge(s_h, 8 * 6)
            sp.dma_start(out_t, hT).then_inc(s_out, 16)
            sp.wait_ge(s_out, 16)

        @block.gpsimd
        def _(pool):
            nc.gpsimd.memset(ones[:], 1.0).then_inc(s_ones, 1)
            nc.gpsimd.memset(zeros[:], 0.0).then_inc(s_ones, 1)
            nc.gpsimd.memset(eps_sb[:, 0:1], TWO_PI / 4).then_inc(s_ones, 1)

            def bc(table, pr):
                return table[:, pr:pr + 1, :].broadcast_to([P, 2, T])

            def m2_of(pr, k, first2):
                pool.wait_ge(s_buev, pr + 1)
                if not first2:
                    pool.wait_ge(s_z, pr - 1)
                nc.gpsimd.tensor_tensor(m2[:, k], bu[:, k], bc(sinT, pr), ALU.mult).then_inc(s_m2, 1)

            pool.wait_ge(s_trig, 8)
            m2_of(0, 0, True)

            def s5_round(ch, first, last):
                for q in range(4):
                    pr = ch * 4 + q
                    if not (last and q == 3):
                        m2_of(pr + 1, (q + 1) % 2, first and q == 0)
                    pool.wait_ge(s_z, pr + 1)
                    if not (first and q < 2):
                        pool.wait_ge(s_y, pr - 1)
                    nc.gpsimd.tensor_tensor(p2[:, q % 2], zz[:, q % 2], bc(sinT, pr), ALU.mult)\
                        .then_inc(s_p2, 1)

            for ch in range(KC):
                s5_round(ch, ch == 0, ch == KC - 1)

            for layer in range(2):
                su = AT[f"u{layer}"][2]
                with pool.Fori(0, HALF // SLOTS) as r:
                    for j in range(SLOTS):
                        pool.wait_ge(s_hi, r * SLOTS + (su + j + 1))
                        nc.gpsimd.tensor_tensor(w_lo[:, j % 2], ring[:, j], w_hi[:, j % 2].bitcast(F32),
                                                ALU.subtract).then_inc(s_lo, 1)

                def gates(group, k, g, first2):
                    pool.wait_ge(s_eqa, group + 1)
                    if not first2:
                        pool.wait_ge(s_gmm, group - 1)
                    for part, out in ((g_hi, one_hi), (g_lo, one_lo)):
                        tok = part[:, g * 4:g * 4 + 4] if isinstance(g, int) else part[:, bass.ds(g * 4, 4)]
                        nc.gpsimd.tensor_tensor(out[:, k], eq_a[:, k],
                                                tok.unsqueeze(2).broadcast_to([P, 4, HALF]), ALU.mult)\
                            .then_inc(s_onea, 1)

                base = 2 * HALF * layer

                def u2(r, first, last):
                    for j in range(SLOTS):
                        g = r * SLOTS + j
                        gates(base + g, j % 2, g, first and j < 2 and layer == 0)

                rounds(pool, HALF // SLOTS, u2)

                def a_low(v, k):
                    pool.wait_ge(s_ahi, EB * layer + v + 1)
                    src = HB[:, v, :] if isinstance(v, int) else HB[:, bass.ds(v, 1), :].rearrange("p a t -> p (a t)")
                    nc.gpsimd.tensor_tensor(a_lo[:, k], src, a_hi[:, k].bitcast(F32), ALU.subtract)\
                        .then_inc(s_alo, 1)

                gates(base + HALF, 0, 0, False)

                def v1(r, first, last):
                    for j in range(SLOTS):
                        g = r * SLOTS + j
                        a_low(g, j % 2)
                        if not (last and j == 3):
                            gates(base + HALF + g + 1, (j + 1) % 2, g + 1, False)

                rounds(pool, HALF // SLOTS, v1)
                with pool.Fori(0, HALF // SLOTS) as r:
                    for j in range(SLOTS):
                        a_low(r * SLOTS + (HALF + j), j % 2)

        @block.scalar
        def _(act):
            for dst, src in ((c_sb[:], c_col), (xT[:], x_t), (bcond[:], b_cond), (norm_sb[:], norms),
                             (ident[:], ident_d), (iota[:], iota_d)):
                act.dma_start(dst, src).then_inc(s_const, 16)
            for dst, src in ((lam[:], s5_lam), (tt[:], time_d), (b_re, s5_b[:, 0]), (b_im, s5_b[:, 1]),
                             (c_re, s5_c[:, 0]), (c_im, s5_c[:, 1]), (dcol[:], s5_d), (bglu[:], b_glu)):
                act.dma_start(dst, src).then_inc(s_s5in, 16)

            act.wait_ge(s_const, 96)
            nc.scalar.activation(silu_c[:], c_sb[:], ACT.Silu).then_inc(s_silu, 1)
            act.wait_ge(s_s5in, 128)
            nc.scalar.activation(sm[:, 0], lam[:, 2], ACT.Exp).then_inc(s_act, 1)
            act.wait_ge(s_rho, 1)
            nc.scalar.activation(sm[:, 2], sm[:, 1], ACT.Exp).then_inc(s_act, 1)
            act.wait_ge(s_rho, 2)
            act.wait_ge(s_ones, 3)
            nc.scalar.activation(sm[:, 4], sm[:, 3], ACT.Sin, scale=TWO_PI).then_inc(s_trig0, 1)
            nc.scalar.activation(sm[:, 5], sm[:, 3], ACT.Abs).then_inc(s_act, 1)
            act.wait_ge(s_act, 3)
            nc.scalar.activation(sm[:, 6], sm[:, 5], ACT.Sin, scale=-TWO_PI, bias=eps_sb[:, 0:1])\
                .then_inc(s_trig0, 1)
            nc.scalar.mul(c_nre, c_re, -1.0).then_inc(s_cneg, 1)
            nc.scalar.mul(c_im, c_im, -1.0).then_inc(s_cneg, 1)
            for ch in range(KC):
                act.wait_ge(s_bbt, ch + 1)
                nc.scalar.copy(bbt[:, ch].rearrange("p a b -> p (a b)"),
                               bank[4 + ch % 2][:, 0:256]).then_inc(s_bbev, 1)

            def squares(k, x_count):
                if x_count:
                    act.wait_ge(s_x, x_count)
                for half in range(2):
                    nc.scalar.activation(sq[:, half * 4:half * 4 + 4], xT[:, half * 4:half * 4 + 4],
                                         ACT.Square).then_inc(s_sq, 1)

            def root(k):
                act.wait_ge(s_var, k + 1)
                nc.scalar.activation(std, rstd, ACT.Sqrt).then_inc(s_std, 1)

            def shifts(which, dst, n):
                for ch in range(KC):
                    act.wait_ge(s_hn, 8 * n + ch + 1)
                    nc.scalar.activation(dst[:, ch], dst[:, ch], ACT.Identity, bias=vec(SHIFT[which], ch))\
                        .then_inc(s_h, 1)

            def evacuate(name, m, dst):
                act.wait_ge(s_plain, AT[name][1] + m + 1)
                nc.scalar.copy(dst, bank[m % 2][:, 0:T]).then_inc(s_evac, 1)

            squares(0, 0)
            root(0)
            shifts(MIX0, hT, 0)
            for g in range(4):
                act.wait_ge(s_ang, 8 * g + 8)
                part = slice(8 * g, 8 * g + 8)
                nc.scalar.activation(cosT[:, part], sinT[:, part], ACT.Abs).then_inc(s_act, 1)
                act.wait_ge(s_act, 4 + g)
                nc.scalar.activation(cosT[:, part], cosT[:, part], ACT.Sin, scale=-TWO_PI,
                                     bias=eps_sb[:, 0:1]).then_inc(s_trig, 1)
                nc.scalar.activation(sinT[:, part], sinT[:, part], ACT.Sin, scale=TWO_PI).then_inc(s_trig, 1)
            for m in range(8):
                evacuate("w_in", m, uT[:, m])

            def bu_round(ch, first, last):
                for q in range(4):
                    pr = ch * 4 + q
                    act.wait_ge(s_bu, pr + 1)
                    if not (first and q < 2):
                        act.wait_ge(s_m1, pr - 1)
                        act.wait_ge(s_m2, pr - 1)
                    nc.scalar.copy(bu[:, q % 2].rearrange("p a b -> p (a b)"), bank[2 + q][:, :])\
                        .then_inc(s_buev, 1)

            rounds(act, KC, bu_round)
            act.wait_ge(s_yev, 8)
            nc.scalar.activation(gl, yT, ACT.Gelu_apprx_tanh).then_inc(s_gl, 1)
            for m in range(8):
                act.wait_ge(s_plain, AT["w_glu"][1] + m + 1)
                nc.scalar.activation(sig[:, m], bank[m % 2][:, 0:T], ACT.Sigmoid, bias=bglu[:, m:m + 1])\
                    .then_inc(s_evac, 1)

            def peer(layer):
                act.wait_ge(s_h, 8 * (2 + 3 * layer))
                act.dma_start(KEYS, keys_d[layer]).then_inc(s_keys, 16)
                nc.scalar.copy(h_hi[:], hT).then_inc(s_hhi, 1)
                for m in range(8):
                    evacuate(f"peer_q{layer}", m, qT[:, m])
                for tb in range(TB):
                    for b in range(4):
                        act.wait_ge(s_sc, 8 * layer + 4 * tb + b + 1)
                        nc.scalar.copy(SC[tb][:, 2 * b:2 * b + 2], bank[2 + b][:, :]
                                       .rearrange("p (a b c) -> p a b c", a=2, b=2)).then_inc(s_scev, 1)
                n0, _, s0 = AT[f"u{layer}"]

                def hi(r, j, off):
                    jj = (j + off) % 4
                    rr = (j + off) // 4
                    act.wait_ge(s_slot[jj], r * 16 + ((n0 // 4 + rr + 1) * 16))
                    if not (layer == 0 and isinstance(r, int) and r * 4 + j + off < 2):
                        act.wait_ge(s_split, r * 4 + (s0 + j + off - 1))
                    nc.scalar.copy(w_hi[:, jj % 2], ring[:, jj]).then_inc(s_hi, 1)

                hi(0, 0, 0)
                hi(0, 1, 0)
                ix = {0: None}

                def exp_gates(tb):
                    act.wait_ge(s_gsub, 2 * layer + tb + 1)
                    dst = route[tb][:, 2]
                    nc.scalar.activation(dst, dst, ACT.Exp).then_inc(s_gexp, 1)

                def gelu(r, j, half):
                    act.wait_ge(s_split, r * 4 + (s0 + half * HALF + j + 1))
                    row = r * 4 + (half * HALF + j)
                    dst = HB[:, row, :] if isinstance(row, int) else \
                        HB[:, bass.ds(row, 1), :].rearrange("p a t -> p (a t)")
                    nc.scalar.activation(dst, bank[j % 2][:, 0:T], ACT.Gelu_apprx_tanh).then_inc(s_evac, 1)

                def u_round(half):
                    def body(r, first, last):
                        for j in range(SLOTS):
                            hi(r + half * (HALF // 4), j, 2)
                            gelu(r, j, half)
                    return body

                n1 = HALF // SLOTS
                with act.Fori(0, 7) as r:
                    u_round(0)(r, False, False)
                exp_gates(0)
                with act.Fori(7, 13) as r:
                    u_round(0)(r, False, False)
                exp_gates(1)
                with act.Fori(13, n1) as r:
                    u_round(0)(r, False, False)
                with act.Fori(0, n1) as r:
                    u_round(1)(r, False, False)

                def a_high(v, k):
                    src = HB[:, v, :] if isinstance(v, int) else HB[:, bass.ds(v, 1), :].rearrange("p a t -> p (a t)")
                    nc.scalar.copy(a_hi[:, k], src).then_inc(s_ahi, 1)

                act.wait_ge(s_gev, 2 * HALF * layer + HALF)
                a_high(0, 0)
                a_high(1, 1)

                def v_round(half):
                    def body(r, first, last):
                        for j in range(SLOTS):
                            final = last and half == 1 and j >= 2
                            if not final:
                                hi(r + (2 + half) * (HALF // 4), j, 2)
                                if half == 0 and last and j == 2:
                                    act.wait_ge(s_gev, 2 * HALF * layer + 2 * HALF)
                                act.wait_ge(s_alo, r * 4 + (EB * layer + half * HALF + j + 1))
                                a_high(r * 4 + (half * HALF + j + 2), j % 2)
                    return body

                rounds(act, n1, v_round(0))
                rounds(act, n1, v_round(1))

            squares(1, 8)
            root(1)
            shifts(FFN0, hT, 1)
            peer(0)

            squares(2, 16)
            for dst, src in ((masks, masks_d), (rot, rot_d), (sinks, sinks_d), (freq, freq_d), (pos_i, pos_d)):
                act.dma_start(dst, src).then_inc(s_attin, 16)
            root(2)
            shifts(KVN, hkv, 2)
            shifts(MIX1, hT, 3)
            for m in range(2):
                evacuate("w_kv", m, kraw[:, m])
            for m in range(2):
                act.wait_ge(s_plain, AT["w_kv"][1] + 2 + m + 1)
                nc.scalar.copy(vN[:, :, m * P:(m + 1) * P],
                               bank[m % 2][:, 0:T].rearrange("p (a b) -> p a b", a=2)).then_inc(s_evac, 1)
            act.wait_ge(s_rang, 1)
            nc.scalar.activation(rsin, rtmp[:, 0], ACT.Sin).then_inc(s_rtrig, 1)
            nc.scalar.activation(rtmp[:, 1], rtmp[:, 0], ACT.Abs).then_inc(s_act, 1)
            act.wait_ge(s_act, 8)
            nc.scalar.activation(rcos, rtmp[:, 1], ACT.Sin, scale=-1.0, bias=eps_sb[:, 0:1]).then_inc(s_rtrig, 1)
            for m in range(8):
                evacuate("attn_q", m, qraw[:, m])
                if m == 3:
                    act.wait_ge(s_rope, 2)
                    for src in range(2):
                        for dst in range(2):
                            act.dma_start(kdup[64 * dst:64 * dst + 64, src::2, :],
                                          krot[64 * src:64 * src + 64, :, :]).then_inc(s_kdup, 16)
            for s in range(9):
                if s < 8:
                    tb = s // 4
                    k0, nk = (P, P) if tb == 0 else (0, T)
                    act.wait_ge(s_sm, s + 1)
                    for r in range(2):
                        for mm in range(2):
                            head = 2 * r + mm
                            view = s_sb[s % 2][:, r, mm, k0:k0 + nk]
                            nc.scalar.activation(view, view, ACT.Exp, bias=nrowm[:, head:head + 1],
                                                 accum_out=rsum[:, head:head + 1]).then_inc(s_p, 1)
                    nc.scalar.activation(esink, esink, ACT.Exp).then_inc(s_p, 1)
                if s >= 1:
                    ps = s - 1
                    ptb, kv = ps // 4, ps % 4
                    for kb in range(1 - ptb, 2):
                        n_before = ps if ps < 4 else 4 + 2 * (ps - 4)
                        n_this = n_before + (kb if ptb else 0) + 1
                        act.wait_ge(s_pt, n_this)
                        nc.scalar.copy(pT[ps % 2][:, kb], bank[6 + kb][:, :]
                                       .rearrange("p (a b) -> p a b", a=4)).then_inc(s_ptev, 1)
                    act.wait_ge(s_o, ps + 1)
                    nc.scalar.copy(oT[:, 2 * kv:2 * kv + 2, ptb * P:ptb * P + P],
                                   bank[ps % 2][:, 256:512].rearrange("p (a b) -> p a b", a=2))\
                        .then_inc(s_oev, 1)
            squares(3, 24)
            root(3)
            shifts(FFN1, hT, 4)
            peer(1)
            squares(4, 32)
            root(4)
            shifts(FINAL, hT, 5)

        @block.vector
        def _(dve):
            v = nc.vector
            st = Steps(dve, s_dve)

            def do(ins):
                st.add(ins)
                st.sync()

            def scales(which):
                st.add(v.scalar_tensor_tensor(gs[:, which], cond[:, SCALE[which] * KC:SCALE[which] * KC + KC], 1.0,
                                              norm_sb[:, which], ALU.add, ALU.mult))

            def stats(k):
                dve.wait_ge(s_ms, k + 1)
                v.tensor_scalar(rstd, bank[0][:, 0:T], 1.0 / D, 1e-6, ALU.mult, ALU.add).then_inc(s_var, 1)
                dve.wait_ge(s_std, k + 1)
                do(v.reciprocal(rstd, std))

            def normalise(which, dst):
                for ch in range(KC):
                    v.scalar_tensor_tensor(dst[:, ch], xT[:, ch], gs[:, which, ch:ch + 1], rstd,
                                           ALU.mult, ALU.mult).then_inc(s_hn, 1)

            def residual(name, gate, m):
                dve.wait_ge(s_plain, AT[name][1] + m + 1)
                v.scalar_tensor_tensor(xT[:, m], bank[m % 2][:, 0:T], vec(gate, m), xT[:, m],
                                       ALU.mult, ALU.add).then_inc(s_x, 1)

            dve.wait_ge(s_s5in, 128)
            dve.wait_ge(s_act, 1)
            a_re, a_im = lam[:, 0], lam[:, 1]
            v.tensor_tensor(sm[:, 1], a_re, sm[:, 0], ALU.mult).then_inc(s_rho, 1)
            theta, th, tl, acc, n, rl, rh = (sm[:, i] for i in range(7, 14))
            t1, t2 = sm[:, 14], sm[:, 15]
            do(v.tensor_tensor(theta, a_im, sm[:, 0], ALU.mult))
            inv = 1.0 / TWO_PI
            i1 = float(np.float32(np.round(inv * 2.0 ** 14) / 2.0 ** 14))
            i2 = float(np.float32(inv - i1))
            do(v.tensor_scalar(t1, theta, 4097.0, None, ALU.mult))
            do(v.tensor_tensor(t2, t1, theta, ALU.subtract))
            do(v.tensor_tensor(th, t1, t2, ALU.subtract))
            do(v.tensor_tensor(tl, theta, th, ALU.subtract))
            st.add(v.tensor_scalar(th, th, i1, None, ALU.mult))
            st.add(v.tensor_scalar(tl, tl, i1, None, ALU.mult))
            do(v.tensor_scalar(t1, theta, i2, None, ALU.mult))
            do(v.tensor_tensor(tl, tl, t1, ALU.add))
            do(v.tensor_tensor(acc, th, tl, ALU.add))
            do(v.tensor_scalar(n, acc, MAGIC, -MAGIC, ALU.add, ALU.add))
            do(v.tensor_tensor(th, th, n, ALU.subtract))
            do(v.tensor_tensor(acc, th, tl, ALU.add))
            do(v.tensor_scalar(rh, acc, MAGIC15, -MAGIC15, ALU.add, ALU.add))
            do(v.tensor_tensor(rl, th, rh, ALU.subtract))
            do(v.tensor_tensor(rl, rl, tl, ALU.add))
            v.tensor_scalar(sm[:, 3], acc, 0.49999997, -0.49999997, ALU.min, ALU.max).then_inc(s_rho, 1)
            mag, lre, lim, den, cr, ci = (sm[:, i] for i in (2, 16, 17, 18, 19, 20))
            dve.wait_ge(s_trig0, 2)
            dve.wait_ge(s_act, 2)
            do(v.tensor_tensor(lre, mag, sm[:, 6], ALU.mult))
            st.add(v.tensor_tensor(lim, mag, sm[:, 4], ALU.mult))
            st.add(v.tensor_tensor(den, a_re, a_re, ALU.mult))
            st.add(v.tensor_tensor(t1, a_im, a_im, ALU.mult))
            do(v.tensor_scalar(lre, lre, -1.0, None, ALU.add))
            do(v.tensor_tensor(den, den, t1, ALU.add))
            do(v.reciprocal(den, den))
            st.add(v.tensor_tensor(cr, lre, a_re, ALU.mult))
            st.add(v.tensor_tensor(t1, lim, a_im, ALU.mult))
            st.add(v.tensor_tensor(ci, lim, a_re, ALU.mult))
            do(v.tensor_tensor(t2, lre, a_im, ALU.mult))
            st.add(v.tensor_tensor(cr, cr, t1, ALU.add))
            do(v.tensor_tensor(ci, ci, t2, ALU.subtract))
            st.add(v.tensor_tensor(cr, cr, den, ALU.mult))
            do(v.tensor_tensor(ci, ci, den, ALU.mult))
            crb = cr.unsqueeze(2).broadcast_to([P, PAIRS, 32])
            cib = ci.unsqueeze(2).broadcast_to([P, PAIRS, 32])
            st.add(v.tensor_tensor(bb_re, b_re, crb, ALU.mult))
            st.add(v.tensor_tensor(bbtmp[:], b_im, cib, ALU.mult))
            st.add(v.tensor_tensor(bb_im, b_im, crb, ALU.mult))
            st.sync()
            v.tensor_tensor(bb_re, bb_re, bbtmp[:], ALU.subtract).then_inc(s_bb, 1)
            dve.wait_ge(s_bb, 1)
            do(v.tensor_tensor(bbtmp[:], b_re, cib, ALU.mult))
            v.tensor_tensor(bb_im, bb_im, bbtmp[:], ALU.add).then_inc(s_bb, 1)

            dve.wait_ge(s_const, 96)
            dve.wait_ge(s_plain, 16)
            do(v.tensor_tensor(cond[:, 0:16], bank[6][:, 256:272], bcond[:, 0:16], ALU.add))
            scales(MIX0)
            st.sync()
            stats(0)
            normalise(MIX0, hT)

            for pr in range(PAIRS):
                k, w = ang[:, pr % 2], ang[:, 2 + pr % 2]
                do(v.tensor_scalar(w, tt[:], acc[:, pr:pr + 1], MAGIC, ALU.mult, ALU.add))
                do(v.tensor_scalar(k, w, -MAGIC, None, ALU.add))
                do(v.scalar_tensor_tensor(w, tt[:], rh[:, pr:pr + 1], k, ALU.mult, ALU.subtract))
                do(v.scalar_tensor_tensor(k, tt[:], rl[:, pr:pr + 1], w, ALU.mult, ALU.add))
                v.tensor_scalar(sinT[:, pr], k, 0.49999997, -0.49999997, ALU.min, ALU.max).then_inc(s_ang, 1)

            def bc(table, pr):
                return table[:, bass.ds(pr, 1), :].broadcast_to([P, 2, T]) if not isinstance(pr, int) \
                    else table[:, pr:pr + 1, :].broadcast_to([P, 2, T])

            def m1_of(pr, k):
                dve.wait_ge(s_buev, pr + 1)
                v.tensor_tensor(m1[:, k], bu[:, k], bc(cosT, pr), ALU.mult).then_inc(s_m1, 1)

            dve.wait_ge(s_trig, 8)
            m1_of(0, 0)
            base = st.n
            PER = 8

            def s5_round(ch, first, last):
                for q in range(4):
                    pr = ch * 4 + q
                    k = q % 2
                    if not (last and q == 3):
                        m1_of(pr + 1, (q + 1) % 2)
                    dve.wait_ge(s_m1, pr + 1)
                    dve.wait_ge(s_m2, pr + 1)
                    v.tensor_tensor(wz[:, 0], m1[:, k, 0], m2[:, k, 1], ALU.add).then_inc(s_dve, 1)
                    v.tensor_tensor(wz[:, 1], m1[:, k, 1], m2[:, k, 0], ALU.subtract).then_inc(s_dve, 1)
                    dve.wait_ge(s_dve, ch * PER + (base + 2 * q + 2))
                    if not (first and q < 2):
                        dve.wait_ge(s_p2, pr - 1)
                    magp = mag[:, bass.ds(pr, 1)] if not isinstance(pr, int) else mag[:, pr:pr + 1]
                    magb = magp.broadcast_to([P, T])
                    v.tensor_tensor_scan(zz[:, k, 0], magb, wz[:, 0], 0.0, ALU.mult, ALU.add)
                    v.tensor_tensor_scan(zz[:, k, 1], magb, wz[:, 1], 0.0, ALU.mult, ALU.add).then_inc(s_z, 1)
                    dve.wait_ge(s_z, pr + 1)
                    if not (first and q < 2):
                        dve.wait_ge(s_y, pr - 1)
                    v.tensor_tensor(p1[:, k], zz[:, k], bc(cosT, pr), ALU.mult).then_inc(s_p1, 1)
                dve.wait_ge(s_y, ch * 4 + 4)
                col = (ch % 2) * 256 if isinstance(ch, int) else 0
                chs = slice(ch, ch + 1) if isinstance(ch, int) else bass.ds(ch, 1)
                flat = "p a t -> p (a t)"
                dcol_c = dcol[:, chs]
                v.scalar_tensor_tensor(yT[:, chs].rearrange(flat), uT[:, chs].rearrange(flat), dcol_c,
                                       bank[7][:, 0:T], ALU.mult, ALU.add).then_inc(s_yev, 1)

            rounds(dve, KC, s5_round)
            st.n = base + PER * KC
            dve.wait_ge(s_plain, AT["w_glu"][1])
            do(v.tensor_tensor(cond[:, 16:P], bank[6][:, 272:384], bcond[:, 16:P], ALU.add))
            for which in (FFN0, KVN, MIX1, FFN1, FINAL):
                scales(which)
            for m in range(8):
                dve.wait_ge(s_evac, PROJ["w_glu"] + m + 1)
                if m == 0:
                    dve.wait_ge(s_gl, 1)
                v.tensor_tensor(y2[:, m], gl[:, m], sig[:, m], ALU.mult).then_inc(s_y2, 1)
            for m in range(8):
                residual("w_out", 2, m)
            st.sync()

            def top16(src, vals, idx, n):
                for g in range(0, n, 4):
                    rows = range(g, g + 4)
                    for i in rows:
                        st.add(v.max(vals[i][:, 0:8], src[i]))
                    st.sync()
                    for i in rows:
                        st.add(v.max_index(idx[i][:, 0:8], vals[i][:, 0:8], src[i]))
                    st.sync()
                    for i in rows:
                        st.add(v.match_replace(src[i], vals[i][:, 0:8], src[i], -3.0e38))
                    st.sync()
                    for i in rows:
                        st.add(v.max(vals[i][:, 8:16], src[i]))
                    st.sync()
                    for i in rows:
                        st.add(v.max_index(idx[i][:, 8:16], vals[i][:, 8:16], src[i]))
                st.sync()

            def peer(layer):
                dve.wait_ge(s_hhi, layer + 1)
                v.tensor_tensor(h_lo[:], hT, h_hi[:].bitcast(F32), ALU.subtract).then_inc(s_hlo, 1)
                for tb in range(TB):
                    dve.wait_ge(s_scev, 8 * layer + 4 * tb + 4)
                    hp = [(h, p) for h in range(HEADS) for p in range(2)]
                    top16([SC[tb][:, h, p] for h, p in hp], [v_top[:, h, p] for h, p in hp],
                          [ix_u[:, h, p] for h, p in hp], 2 * HEADS)
                    full = [P, HEADS, TOPK, TOPK]
                    st.add(v.tensor_copy(ix_f, ix_u))
                    do(v.tensor_tensor(CAND, v_top[:, :, 0].unsqueeze(3).broadcast_to(full),
                                       v_top[:, :, 1].unsqueeze(2).broadcast_to(full), ALU.add))
                    top16([CAND[:, h].rearrange("p a b -> p (a b)") for h in range(HEADS)],
                          [t_top[:, h] for h in range(HEADS)], [pos_u[:, h] for h in range(HEADS)], HEADS)
                    st.add(v.tensor_scalar(ab_u[:, 0], pos_u, 4, None, ALU.logical_shift_right))
                    do(v.tensor_scalar(ab_u[:, 1], pos_u, 15, None, ALU.bitwise_and))
                    do(v.tensor_copy(ab_f, ab_u))
                    io = iota[:, 0:TOPK].unsqueeze(1).unsqueeze(1).broadcast_to(full)
                    for half in range(2):
                        do(v.tensor_tensor(EQ, ab_f[:, half].unsqueeze(3).broadcast_to(full), io, ALU.is_equal))
                        do(v.tensor_tensor(EQ, EQ, ix_f[:, :, half].unsqueeze(2).broadcast_to(full), ALU.mult))
                        do(v.tensor_reduce(route[tb][:, half], EQ, axis=AX.X, op=ALU.add))
                    v.tensor_tensor(route[tb][:, 2], t_top, t_top[:, :, 0:1].broadcast_to([P, HEADS, TOPK]),
                                    ALU.subtract).then_inc(s_gsub, 1)
                    dve.wait_ge(s_gexp, 2 * layer + tb + 1)
                    do(v.tensor_reduce(gsum[:], route[tb][:, 2], axis=AX.X, op=ALU.add))
                    do(v.reciprocal(gsum[:], gsum[:]))
                    v.tensor_tensor(route[tb][:, 2], route[tb][:, 2],
                                    gsum[:].unsqueeze(2).broadcast_to([P, HEADS, TOPK]), ALU.mult)\
                        .then_inc(s_route, 1)
                for tb in range(TB):
                    dve.wait_ge(s_rt, 2 * layer + tb + 1)
                    cols = slice(tb * P, tb * P + P)
                    st.add(v.tensor_copy(i0T[:, cols], bank[6 + tb][:, 0:P]))
                    st.add(v.tensor_copy(i1T[:, cols], bank[6 + tb][:, P:2 * P]))
                    do(v.tensor_copy(g_hi[:, cols].bitcast(F32R), bank[6 + tb][:, 2 * P:3 * P]))
                    v.tensor_tensor(g_lo[:, cols], bank[6 + tb][:, 2 * P:3 * P], g_hi[:, cols],
                                    ALU.subtract).then_inc(s_rtev, 1)
                dve.wait_ge(s_rtev, 2 * layer + 2)
                st.sync()
                base = 2 * HALF * layer
                su = AT[f"u{layer}"][2]

                def one_hots(group, k, g, half, first2):
                    if not first2:
                        dve.wait_ge(s_onea, 2 * (group - 1))
                        dve.wait_ge(s_gmm, group - 1)
                    for idx, out, first_key, width, s in ((i0T, eq_a, half * HALF, HALF, s_eqa),
                                                          (i1T, one_b, 0, P, s_oneb)):
                        tok = idx[:, g * 4:g * 4 + 4] if isinstance(g, int) else idx[:, bass.ds(g * 4, 4)]
                        v.tensor_tensor(out[:, k], tok.unsqueeze(2).broadcast_to([P, 4, width]),
                                        iota[:, first_key:first_key + width].unsqueeze(1)
                                        .broadcast_to([P, 4, width]), ALU.is_equal).then_inc(s, 1)

                def low(r, j, off):
                    dve.wait_ge(s_hi, r * 4 + (su + off + j + 1))
                    v.tensor_tensor(w_lo[:, j % 2], ring[:, j], w_hi[:, j % 2].bitcast(F32), ALU.subtract)\
                        .then_inc(s_lo, 1)

                def apply_gates(group, k, g, half):
                    if isinstance(g, int) and g == 0:
                        dve.wait_ge(s_evac, e_u + (half + 1) * HALF)
                    dve.wait_ge(s_gmm, group + 1)
                    rows = HB[:, half * HALF:half * HALF + HALF, :]
                    rows = rows[:, :, g * 4:g * 4 + 4] if isinstance(g, int) else rows[:, :, bass.ds(g * 4, 4)]
                    rows = rows.rearrange("p i t -> p t i")
                    v.tensor_tensor(rows, bank[6 + k][:, 0:4 * HALF].rearrange("p (t i) -> p t i", t=4),
                                    rows, ALU.mult).then_inc(s_gev, 1)

                def both(half):
                    def body(r, first, last):
                        for j in range(SLOTS):
                            g = r * SLOTS + j
                            low(r, j, HALF * (1 + half))
                            if not (last and j == 3):
                                one_hots(base + half * HALF + g + 1, (j + 1) % 2, g + 1, half,
                                         layer == 0 and half == 0 and first and j == 0)
                            elif half == 0:
                                one_hots(base + HALF, 0, 0, 1, False)
                            if not (first and j == 0):
                                apply_gates(base + half * HALF + g - 1, (j + 1) % 2, g - 1, half)
                            elif half == 1:
                                pass
                            if last and j == 3:
                                apply_gates(base + half * HALF + g, j % 2, g, half)
                    return body

                e_u = PROJ[f"u{layer}"] - 8 * (layer + 1)
                one_hots(base, 0, 0, 0, layer == 0)
                rounds(dve, HALF // SLOTS, both(0))
                rounds(dve, HALF // SLOTS, both(1))
                with dve.Fori(0, HALF // SLOTS) as r:
                    for j in range(SLOTS):
                        low(r, j, 3 * HALF)
                dve.wait_ge(s_split, su + 2 * EB)
                for ch in range(KC):
                    v.scalar_tensor_tensor(xT[:, ch], bank[2 + ch // 2][:, (ch % 2) * T:(ch % 2) * T + T],
                                           vec(6 * layer + 5, ch), xT[:, ch], ALU.mult, ALU.add).then_inc(s_x, 1)

            stats(1)
            normalise(FFN0, hT)
            dve.wait_ge(s_h, 16)
            peer(0)

            stats(2)
            normalise(KVN, hkv)
            normalise(MIX1, hT)
            dve.wait_ge(s_attin, 80)
            c1 = 6.28125
            c2 = float(np.float32(round((TWO_PI - c1) * 2.0 ** 21) / 2.0 ** 21))
            c3 = float(np.float32(TWO_PI - c1 - c2))
            do(v.tensor_copy(rtmp[:, 1], pos_i))
            do(v.tensor_scalar(rtmp[:, 1], rtmp[:, 1], freq, None, ALU.mult))
            do(v.tensor_scalar(rtmp[:, 2], rtmp[:, 1], inv, MAGIC, ALU.mult, ALU.add))
            do(v.tensor_scalar(rtmp[:, 2], rtmp[:, 2], -MAGIC, None, ALU.add))
            for cc in (c1, c2, c3):
                do(v.scalar_tensor_tensor(rtmp[:, 1], rtmp[:, 2], -cc, rtmp[:, 1], ALU.mult, ALU.add))
            v.tensor_scalar(rtmp[:, 0], rtmp[:, 1], 3.1415925, -3.1415925, ALU.min, ALU.max).then_inc(s_rang, 1)
            dve.wait_ge(s_rtrig, 2)
            for m in range(10):
                src, dst = (kraw[:, m], krot[:, m]) if m < 2 else (qraw[:, m - 2], qrot[:, m - 2])
                dve.wait_ge(s_evac, (PROJ["w_kv"] + m + 1 if m < 2 else PROJ["attn_q"] + m - 1) - 8)
                st.add(v.tensor_tensor(ropet[:, 0], src, rcos, ALU.mult))
                dve.wait_ge(s_rmm, m + 1)
                st.add(v.tensor_tensor(ropet[:, 1], bank[2 + m % 4][:, 0:T], rsin, ALU.mult))
                st.sync()
                v.tensor_tensor(dst, ropet[:, 0], ropet[:, 1], ALU.add).then_inc(s_rope, 1)
                dve.wait_ge(s_rope, m + 1)
            for s in range(8):
                tb, kv = s // 4, s % 4
                k0, nk = (P, P) if tb == 0 else (0, T)
                own = s_sb[s % 2]
                dve.wait_ge(s_s, s + 1)
                if s >= 2:
                    dve.wait_ge(s_pt, s - 1 if s < 6 else 4 + 2 * (s - 5))
                for r in range(2):
                    st.add(v.scalar_tensor_tensor(
                        own[:, r, :, k0:k0 + nk],
                        bank[2 + 2 * (s % 2) + r][:, :].rearrange("p (a b) -> p a b", a=2)[:, :, k0:k0 + nk],
                        0.125, masks[:, k0:k0 + nk].unsqueeze(1).broadcast_to([P, 2, nk]), ALU.mult, ALU.add))
                st.sync()
                flat = own[:, :, :, k0:k0 + nk]
                do(v.tensor_reduce(rowm, flat, axis=AX.X, op=ALU.max))
                do(v.tensor_tensor(rowm, rowm, sinks[:, kv], ALU.max))
                st.add(v.tensor_scalar(nrowm, rowm, -1.0, None, ALU.mult))
                st.sync()
                v.tensor_tensor(esink, sinks[:, kv], rowm, ALU.subtract).then_inc(s_sm, 1)
                dve.wait_ge(s_p, 5 * (s + 1))
                do(v.tensor_tensor(rsum, rsum, esink, ALU.add))
                do(v.reciprocal(rsum, rsum))
                v.tensor_tensor(flat, flat, rsum.rearrange("p (a b) -> p a b", a=2).unsqueeze(3)
                                .broadcast_to([P, 2, 2, nk]), ALU.mult).then_inc(s_pn, 1)
                dve.wait_ge(s_pn, s + 1)
            for m in range(8):
                residual("w_o", 8, m)
            stats(3)
            normalise(FFN1, hT)
            dve.wait_ge(s_h, 40)
            peer(1)
            stats(4)
            normalise(FINAL, hT)

        @block.tensor
        def _(pe):
            mm = nc.tensor.matmul

            def arrived(name, m):
                n = AT[name][0] + m
                pe.wait_ge(s_slot[n % 4], 16 * (n // 4 + 1))

            def cond_round(name, r):
                n0, p0, _ = AT[name]
                col0 = 256 + (16 if name == "cond_b" else 0)
                for j in range(SLOTS):
                    pe.wait_ge(s_slot[j], r * 16 + (16 * (n0 // 4 + 1)))
                    out = bank[6][:, bass.ds(r * 4 + (col0 + j), 1)] if not isinstance(r, int) else \
                        bank[6][:, col0 + r * 4 + j:col0 + r * 4 + j + 1]
                    for kc in range(KC):
                        last = mm(out, ring[:, j, kc], silu_c[:, kc:kc + 1], start=kc == 0, stop=kc == KC - 1)
                    last.then_inc(s_plain, 1)

            def project(name, src):
                for m in range(8):
                    arrived(name, m)
                    r = PROJ[name] + m
                    if r >= 2:
                        pe.wait_ge(s_evac, r - 1)
                    for kc in range(KC):
                        last = mm(bank[m % 2][:, 0:T], ring[:, m % 4, kc], src[:, kc], start=kc == 0,
                                  stop=kc == KC - 1)
                    last.then_inc(s_plain, 1)

            def mean_squares(k):
                for half in range(2):
                    pe.wait_ge(s_sq, 2 * k + half + 1)
                    for c in range(4):
                        kc = half * 4 + c
                        last = mm(bank[0][:, 0:T], ones[:], sq[:, kc], start=kc == 0, stop=kc == KC - 1)
                last.then_inc(s_ms, 1)

            pe.wait_ge(s_silu, 1)
            with pe.Fori(0, 4) as r:
                cond_round("cond_a", r)
            pe.wait_ge(s_bb, 2)
            for ch in range(KC):
                if ch >= 2:
                    pe.wait_ge(s_bbev, ch - 1)
                for i, b in enumerate((bb_re, bb_im)):
                    last = nc.tensor.transpose(bank[4 + ch % 2][:, i * P:i * P + P],
                                               b[:, 4 * ch:4 * ch + 4].rearrange("p a b -> p (a b)"), ident[:])
                last.then_inc(s_bbt, 1)
            pe.wait_ge(s_ones, 2)
            mean_squares(0)
            pe.wait_ge(s_h, 8)
            project("w_in", hT)
            pe.wait_ge(s_bbev, 8)
            pe.wait_ge(s_cneg, 2)
            pe.wait_ge(s_evac, 8)
            rb = 0

            def bu_of(pr):
                ch, q = pr // 4, pr % 4
                if pr >= 4:
                    pe.wait_ge(s_buev, pr - 3)
                rows = slice(32 * q, 32 * q + 32)
                for i in range(2):
                    last = mm(bank[2 + q][:, i * T:i * T + T], bbt[rows, ch, i], uT[rows, ch], start=True,
                              stop=True)
                last.then_inc(s_bu, 1)

            for pr in range(4):
                bu_of(pr)
            for ch in range(KC):
                for q in range(4):
                    pr = 4 * ch + q
                    if pr + 4 < PAIRS:
                        bu_of(pr + 4)
                    pe.wait_ge(s_p1, pr + 1)
                    pe.wait_ge(s_p2, pr + 1)
                    if q == 0 and ch >= 1:
                        pe.wait_ge(s_yev, ch)
                    out = bank[7][32 * q:32 * q + 32, 0:T]
                    k = q % 2
                    mm(out, c_re[:, pr], p1[:, k, 0], start=True, stop=False)
                    mm(out, c_nre[:, pr], p2[:, k, 1], start=False, stop=False)
                    mm(out, c_im[:, pr], p1[:, k, 1], start=False, stop=False)
                    mm(out, c_im[:, pr], p2[:, k, 0], start=False, stop=True).then_inc(s_y, 1)
                if ch < 7:
                    with pe.Fori(4 * ch, 4 * ch + 4) as r:
                        cond_round("cond_b", r)
            pe.wait_ge(s_gl, 1)
            project("w_glu", gl)
            pe.wait_ge(s_y2, 8)

            def project_x(name, src, x0):
                for m in range(8):
                    arrived(name, m)
                    if m >= 2:
                        pe.wait_ge(s_x, x0 + m - 1)
                    for kc in range(KC):
                        last = mm(bank[m % 2][:, 0:T], ring[:, m % 4, kc], src[:, kc], start=kc == 0,
                                  stop=kc == KC - 1)
                    last.then_inc(s_plain, 1)

            project_x("w_out", y2, 0)

            def peer(layer):
                n0, _, s0 = AT[f"u{layer}"]
                name = f"peer_q{layer}"
                pe.wait_ge(s_h, 8 * (2 + 3 * layer))
                for m in range(8):
                    arrived(name, m)
                    if m >= 2:
                        pe.wait_ge(s_evac, PROJ[name] - DONE_BY_X[name] + m - 1)
                    for kc in range(KC):
                        last = mm(bank[m % 2][:, 0:T], ring[:, m % 4, kc], hT[:, kc], start=kc == 0,
                                  stop=kc == KC - 1)
                    last.then_inc(s_plain, 1)
                pe.wait_ge(s_keys, 16 * (layer + 1))
                e0 = PROJ[name] - DONE_BY_X[name] + 8
                pe.wait_ge(s_evac, e0)
                for tb in range(TB):
                    for h in range(HEADS):
                        if tb == 1 and h % 2 == 0:
                            pe.wait_ge(s_scev, 8 * layer + h // 2 + 1)
                        last = mm(bank[2 + h // 2][:, (h % 2) * T:(h % 2) * T + T],
                                  qT[:, h, tb * P:tb * P + P], KEYS[:, h], start=True, stop=True)
                        if h % 2:
                            last.then_inc(s_sc, 1)

                pe.wait_ge(s_hlo, layer + 1)

                def u_block(r, j, half):
                    b = r * 4 + (s0 + half * HALF + j)
                    pe.wait_ge(s_hi, b + 1)
                    pe.wait_ge(s_evac, r * 4 + (e0 + half * HALF + j - 1))
                    out, k = bank[j % 2][:, 0:T], j % 2
                    for kc in range(KC):
                        mm(out, w_hi[:, k, kc], h_hi[:, kc], start=kc == 0, stop=False)
                        mm(out, w_hi[:, k, kc], h_lo[:, kc], start=False, stop=False)
                    pe.wait_ge(s_lo, b + 1)
                    for kc in range(KC):
                        last = mm(out, w_lo[:, k, kc], h_hi[:, kc], start=False, stop=kc == KC - 1)
                    last.then_inc(s_split, 1)

                def gate_group(group, j, first2):
                    pe.wait_ge(s_oneb, group + 1)
                    pe.wait_ge(s_onea, 2 * (group + 1))
                    if not first2:
                        pe.wait_ge(s_gev, group - 1)
                    k = j % 2
                    for t in range(4):
                        out = bank[6 + k][:, t * HALF:t * HALF + HALF]
                        mm(out, one_b[:, k, t], one_hi[:, k, t], start=True, stop=False)
                        last = mm(out, one_b[:, k, t], one_lo[:, k, t], start=False, stop=True)
                    last.then_inc(s_gmm, 1)

                with pe.Fori(0, HALF // SLOTS) as r:
                    for j in range(SLOTS):
                        u_block(r, j, 0)
                for tb in range(TB):
                    pe.wait_ge(s_route, 2 * layer + tb + 1)
                    for i in range(3):
                        last = nc.tensor.transpose(bank[6 + tb][:, i * P:i * P + P],
                                                   route[tb][:, i].rearrange("p a b -> p (a b)"), ident[:])
                    last.then_inc(s_rt, 1)
                pe.wait_ge(s_rtev, 2 * layer + 2)
                base = 2 * HALF * layer

                def u2(r, first, last):
                    for j in range(SLOTS):
                        u_block(r, j, 1)
                        gate_group(base + r * SLOTS + j, j, layer == 0 and first and j < 2)

                rounds(pe, HALF // SLOTS, u2)
                for b in range(4):
                    mm(bank[2 + b][:, :], zeros[:], ring0[:, 0:512], start=True, stop=False)

                def v_block(r, j, half, final):
                    b = r * 4 + (s0 + EB + half * HALF + j)
                    a = r * 4 + (EB * layer + half * HALF + j)
                    k = j % 2
                    pe.wait_ge(s_hi, b + 1)
                    pe.wait_ge(s_ahi, a + 1)
                    pe.wait_ge(s_alo, a + 1)
                    for ch in range(KC):
                        out = bank[2 + ch // 2][:, (ch % 2) * T:(ch % 2) * T + T]
                        mm(out, w_hi[:, k, ch], a_hi[:, k], start=False, stop=False)
                        mm(out, w_hi[:, k, ch], a_lo[:, k], start=False, stop=False)
                    pe.wait_ge(s_lo, b + 1)
                    for ch in range(KC):
                        out = bank[2 + ch // 2][:, (ch % 2) * T:(ch % 2) * T + T]
                        last = mm(out, w_lo[:, k, ch], a_hi[:, k], start=False, stop=final and ch % 2 == 1)
                    last.then_inc(s_split, 1)

                def v1(r, first, last):
                    for j in range(SLOTS):
                        v_block(r, j, 0, False)
                        gate_group(base + HALF + r * SLOTS + j, j, False)

                rounds(pe, HALF // SLOTS, v1)

                def v2(r, first, last):
                    for j in range(SLOTS):
                        v_block(r, j, 1, last and j == 3)

                rounds(pe, HALF // SLOTS, v2)

            DONE_BY_X = {"peer_q0": 8, "w_kv": 8, "attn_q": 8, "peer_q1": 16}
            ring0 = xT[:, 0:2].rearrange("p a b -> p (a b)")
            mean_squares(1)
            peer(0)

            mean_squares(2)
            pe.wait_ge(s_h, 24)
            e0 = PROJ["w_kv"] - 8
            for m in range(4):
                arrived("w_kv", m)
                if m >= 2:
                    pe.wait_ge(s_evac, e0 + m - 1)
                for kc in range(KC):
                    if m < 2:
                        last = mm(bank[m % 2][:, 0:T], ring[:, m, kc], hkv[:, kc], start=kc == 0,
                                  stop=kc == KC - 1)
                if m >= 2:
                    for tb in range(TB):
                        for kc in range(KC):
                            last = mm(bank[m % 2][:, tb * P:tb * P + P], hkv[:, kc, tb * P:tb * P + P],
                                      ring[:, m, kc], start=kc == 0, stop=kc == KC - 1)
                last.then_inc(s_plain, 1)
            pe.wait_ge(s_attin, 80)

            def rotate(m):
                if m >= 4:
                    pe.wait_ge(s_rope, m - 3)
                src = kraw[:, m] if m < 2 else qraw[:, m - 2]
                mm(bank[2 + m % 4][:, 0:T], rot, src, start=True, stop=True).then_inc(s_rmm, 1)

            pe.wait_ge(s_evac, e0 + 2)
            rotate(0)
            rotate(1)
            pe.wait_ge(s_h, 32)
            for m in range(8):
                arrived("attn_q", m)
                pe.wait_ge(s_evac, e0 + 4 + m - 1)
                for kc in range(KC):
                    last = mm(bank[m % 2][:, 0:T], ring[:, m % 4, kc], hT[:, kc], start=kc == 0,
                              stop=kc == KC - 1)
                last.then_inc(s_plain, 1)
                if m >= 1:
                    pe.wait_ge(s_evac, e0 + 4 + m)
                    rotate(m + 1)
            pe.wait_ge(s_evac, e0 + 12)
            rotate(9)
            pe.wait_ge(s_rope, 10)
            pe.wait_ge(s_kdup, 64)
            for s in range(9):
                if s < 8:
                    tb, kv = s // 4, s % 4
                    if s >= 2:
                        pe.wait_ge(s_sm, s - 1)
                    keys = slice(0, P) if tb == 0 else slice(0, T)
                    for r in range(2):
                        rows = slice(64 * r, 64 * r + 64)
                        for mh in range(2):
                            c0 = mh * T + (P if tb == 0 else 0)
                            last = mm(bank[2 + 2 * (s % 2) + r][:, c0:mh * T + T],
                                      qrot[rows, 2 * kv + mh, tb * P:tb * P + P], kdup[rows, kv, keys],
                                      start=True, stop=True)
                    last.then_inc(s_s, 1)
                if s >= 1:
                    ps = s - 1
                    tb, kv = ps // 4, ps % 4
                    pe.wait_ge(s_pn, ps + 1)
                    n_before = ps if ps < 4 else 4 + 2 * (ps - 4)
                    if n_before:
                        pe.wait_ge(s_ptev, n_before)
                    kbs = range(1 - tb, 2)
                    for kb in kbs:
                        for head in range(4):
                            last = nc.tensor.transpose(
                                bank[6 + kb][:, head * P:head * P + P],
                                s_sb[ps % 2][:, head // 2, head % 2, kb * P:kb * P + P], ident[:])
                        last.then_inc(s_pt, 1)
                    pe.wait_ge(s_ptev, n_before + len(kbs))
                    if ps >= 2:
                        pe.wait_ge(s_oev, ps - 1)
                    for r in range(2):
                        for kb in kbs:
                            vb = kb if tb == 1 else 0
                            last = mm(bank[ps % 2][64 * r:64 * r + 64, 256:512], vN[:, vb, kv * 64:kv * 64 + 64],
                                      pT[ps % 2][:, kb, 2 * r:2 * r + 2].rearrange("p a b -> p (a b)"),
                                      start=kb == kbs[0], stop=kb == kbs[-1])
                    last.then_inc(s_o, 1)
            pe.wait_ge(s_oev, 8)
            project_x("w_o", oT, 16)
            mean_squares(3)
            peer(1)
            mean_squares(4)


_INS = ["x_t", "c_col", "b_cond", "norms", "ident_d", "iota_d", "time_d", "w_cond", "w_in", "w_glu", "w_out",
        "s5_lam", "s5_b", "s5_c", "s5_d", "b_glu", "peer_wq", "keys_d", "u_tab", "v_tab", "w_kv", "attn_wq",
        "w_o", "sinks_d", "pos_d", "masks_d", "rot_d", "freq_d"]


def lay_out(x, c, positions, w_cond, b_cond, norm_mix, norm_ffn, s5_w_in, s5_a_re, s5_a_im, s5_log_dt,
            s5_b_re, s5_b_im, s5_c_re, s5_c_im, s5_d, s5_w_glu, s5_b_glu, s5_w_out, kv_norm, w_kv, attn_w_q,
            attn_sinks, attn_w_o, peer_w_q, peer_sub_keys, peer_u, peer_v, final_norm):
    f = np.float32

    def blocks(w):
        n = w.shape[-1] // P
        return np.ascontiguousarray(w.reshape(KC, P, n, P).transpose(2, 1, 0, 3)).reshape(n, P, D)

    def cols(v):
        return np.ascontiguousarray(v.reshape(-1, P).T)

    def pair(a):
        return a.reshape(PAIRS, 2, 64).transpose(1, 2, 0).reshape(P, PAIRS)

    def pad(a):
        out = np.zeros((2, 64, PAIRS, 2, 16), f)
        a = a.reshape(PAIRS, 2, 64, 16)
        for g in range(2):
            out[g, :, :, g, :] = a[:, g].transpose(1, 0, 2)
        return out.reshape(P, PAIRS, 32)

    keys = np.zeros((2, 2, 64, HEADS, 2, P), f)
    for half in range(2):
        keys[:, half, :, :, half, :] = peer_sub_keys[:, :, half].transpose(0, 3, 1, 2)
    qi = np.arange(P)[:, None]
    kj = np.arange(P)[None, :]
    masks = np.concatenate([np.where(kj > qi, 0.0, NEG), np.where(kj <= qi, 0.0, NEG)], axis=1).astype(f)
    rot = np.zeros((P, P), f)
    for h in range(2):
        for i in range(32):
            rot[64 * h + 32 + i, 64 * h + i] = -1.0
            rot[64 * h + i, 64 * h + 32 + i] = 1.0
    inv_freq = (f(10000.0) ** (-np.arange(0, 64, 2, dtype=f) / f(64))).astype(f)
    kv_cols = w_kv
    log_dt = np.broadcast_to(s5_log_dt[0][:, None], (64, 64))
    return {
        "x_t": np.ascontiguousarray(x[0].T.reshape(KC, P, T).transpose(1, 0, 2)),
        "c_col": cols(c[0]),
        "b_cond": cols(b_cond),
        "norms": np.ascontiguousarray(np.stack([cols(v) for v in (norm_mix[0], norm_ffn[0], kv_norm, norm_mix[1],
                                                                 norm_ffn[1], final_norm)], axis=1)),
        "ident_d": np.eye(P, dtype=f),
        "iota_d": np.ascontiguousarray(np.broadcast_to(np.arange(P, dtype=f), (P, P))),
        "time_d": np.ascontiguousarray(np.broadcast_to(np.arange(T, dtype=f), (P, T))),
        "w_cond": blocks(w_cond), "w_in": blocks(s5_w_in[0]), "w_glu": blocks(s5_w_glu[0]),
        "w_out": blocks(s5_w_out[0]),
        "s5_lam": np.ascontiguousarray(np.stack([pair(s5_a_re[0]), pair(s5_a_im[0]), pair(log_dt)], axis=1)),
        "s5_b": np.ascontiguousarray(np.stack([pad(s5_b_re[0]), pad(s5_b_im[0])], axis=1)),
        "s5_c": np.ascontiguousarray(np.stack([pad(s5_c_re[0].transpose(0, 2, 1)),
                                               pad(s5_c_im[0].transpose(0, 2, 1))], axis=1)),
        "s5_d": cols(s5_d[0].reshape(-1)), "b_glu": cols(s5_b_glu[0]),
        "peer_wq": np.stack([blocks(peer_w_q[i]) for i in range(2)]),
        "keys_d": keys.reshape(2, P, HEADS, 2 * P),
        "u_tab": np.ascontiguousarray(peer_u.reshape(2, EB, P, KC, P).transpose(0, 1, 4, 3, 2)).reshape(2, EB, P, D),
        "v_tab": peer_v.reshape(2, EB, P, D),
        "w_kv": blocks(kv_cols), "attn_wq": blocks(attn_w_q[0]), "w_o": blocks(attn_w_o[0]),
        "sinks_d": np.ascontiguousarray(np.broadcast_to(
            attn_sinks[0].reshape(4, 2, 2).transpose(0, 2, 1).reshape(1, 4, 4), (P, 4, 4))),
        "pos_d": np.ascontiguousarray(np.broadcast_to(positions[0][None, :], (P, T))),
        "masks_d": masks, "rot_d": rot,
        "freq_d": np.ascontiguousarray(np.tile(inv_freq, 4)[:, None]),
    }


def kernel(**inputs):
    import concourse.bacc as bacc
    from concourse.bass_utils import run_bass_kernel_spmd

    arrays = lay_out(**{k: np.asarray(a) for k, a in inputs.items()})
    nc = bacc.Bacc("TRN2", target_bir_lowering=False, num_devices=1)
    args = [nc.dram_tensor(n, arrays[n].shape, mybir.dt.from_np(arrays[n].dtype), kind="ExternalInput").ap()
            for n in _INS]
    out = nc.dram_tensor("out_t", (P, KC, T), F32, kind="ExternalOutput").ap()
    build(nc, *args, out)
    r = run_bass_kernel_spmd(nc, [arrays], core_ids=[0])
    got = r.results[0]["out_t"]
    return np.ascontiguousarray(got.transpose(2, 1, 0).reshape(1, T, D))
```

```python
from contextlib import ExitStack

import concourse.bass as bass
from concourse import mybir
import numpy as np

F32 = mybir.dt.float32
F32R = mybir.dt.float32r
BF16 = mybir.dt.bfloat16
I32 = mybir.dt.int32
U32 = mybir.dt.uint32
ALU = mybir.AluOpType
ACT = mybir.ActivationFunctionType
AX = mybir.AxisListType

P = 128
D = 1024
KC = D // P
T = 256
TB = T // P
EB = 128
HALF = EB // 2
HEADS = 8
TOPK = 16
PAIRS = 32
SLOTS = 4
STRIDE = 8
TWO_PI = 6.283185307179586
MAGIC = 12582912.0
MAGIC15 = 12582912.0 / 32768.0
NEG = -1e30

STREAM = [("w_in", 8, 0), ("w_glu", 8, 0), ("w_out", 8, 0),
          ("peer_q0", 8, 0), ("u0", 128, 1), ("v0", 128, 1),
          ("w_kv", 4, 0), ("attn_q", 8, 0), ("w_o", 8, 0),
          ("peer_q1", 8, 0), ("u1", 128, 1), ("v1", 128, 1)]


COND_GROUPS = [(0, 1), (2, 3, 4), (13, 8), (5, 6, 7, 12), (9, 10), (11, 14, 15)]
COND_AT = {}
for _group in COND_GROUPS:
    for _n in _group:
        COND_AT[_n] = len(COND_AT)
COND_U = [24, 88]
COND_V1 = COND_U[0] + 14
COND_V2 = [COND_V1 + 18, COND_U[1] + 14]
COND_FIRST = [sum(len(g) for g in COND_GROUPS[:k]) * KC for k in range(len(COND_GROUPS) + 1)]


def positions_in_stream():
    at, n, plain, split = {}, 0, 0, 0
    for name, count, is_split in STREAM:
        at[name] = (n, plain, split)
        n += count
        plain += 0 if is_split else count
        split += count if is_split else 0
    return at


AT = positions_in_stream()


class Steps:

    def __init__(self, eng, sem):
        self.eng, self.sem, self.n = eng, sem, 0

    def add(self, ins):
        ins.then_inc(self.sem, 1)
        self.n += 1

    def sync(self):
        self.eng.wait_ge(self.sem, self.n)


def rounds(eng, n, body):
    body(0, True, False)
    with eng.Fori(1, n - 1) as r:
        body(r, False, False)
    body(n - 1, False, True)


def build(nc, x_t, c_row_d, b_cond, norms, ident_d, iota_d, time_d, w_cond0, w_cond, w_in, w_glu, w_out,
          s5_lam, s5_b, s5_c, s5_d, b_glu, peer_wq, keys_d, u_tab, v_tab,
          w_kv, attn_wq, w_o, sinks_d, pos_d, masks_d, rot_d, freq_d, out_t):
    ctx = ExitStack()
    with ctx:
        def sb(name, shape, dt=F32, c=ctx):
            return c.enter_context(nc.sbuf_tensor(name, shape, dt))

        def sem(name):
            return ctx.enter_context(nc.semaphore(name))

        xT = sb("xT", [P, KC, T])
        ident = sb("ident", [P, P])
        ones = sb("ones", [P, P])
        zeros = sb("zeros", [P, P])
        iota = sb("iota", [P, P])
        cond = sb("cond", [P, P])
        bcond = sb("bcond", [P, P])
        norm_sb = sb("norm_sb", [P, 6, KC])
        gs = sb("gs", [P, 6, KC])
        c_row = sb("c_row", [P, D])
        cring = sb("cring", [P, 2, D])
        eps_sb = sb("eps_sb", [P, 2])
        big = sb("big", [P, EB * T])
        ring = sb("ring", [P, SLOTS, KC, P])
        HB = big[:, :].rearrange("p (i t) -> p i t", t=T)

        def area(at, *shape, dt=None):
            n = 1
            for s in shape:
                n *= s
            v = big[:, at:at + n]
            if dt is not None:
                v = v.bitcast(dt)
            if len(shape) == 2:
                return v.rearrange("p (a b) -> p a b", a=shape[0])
            if len(shape) == 3:
                return v.rearrange("p (a b c) -> p a b c", a=shape[0], b=shape[1])
            if len(shape) == 4:
                return v.rearrange("p (a b c d) -> p a b c d", a=shape[0], b=shape[1], c=shape[2])
            return v

        sq = area(0, KC, T)
        std = area(2048, T)
        rstd = area(2304, T)
        hT = area(16384, KC, T)
        FIRST_SLOTS = 6
        cond0 = [area(at, D) for at in (16384, 17408, 18432, 19456, 29696, 30720)]
        cosT = area(0, PAIRS, T)
        sinT = area(8192, PAIRS, T)
        uT = area(18432, KC, T)
        bbt = area(20480, KC, 2, P)
        c_re = area(22528, PAIRS, 32)
        c_im = area(23552, PAIRS, 32)
        c_nre = area(24576, PAIRS, 32)
        b_re = area(25600, PAIRS, 32)
        b_im = area(26624, PAIRS, 32)
        bb_re = area(27648, PAIRS, 32)
        bb_im = area(28672, PAIRS, 32)
        yT = area(29696, KC, T)
        gl = yT
        y2 = area(16384, KC, T)
        sig = area(18432, KC, T)
        SC = [area(18432, HEADS, 2, P), area(20480, HEADS, 2, P)]
        CAND = area(22528, HEADS, TOPK, TOPK)
        EQ = area(24576, HEADS, TOPK, TOPK)
        KEYS = area(26624, HEADS, 2 * P)
        qT = area(28672, KC, T)
        r_at = 30720
        v_top = area(r_at, HEADS, 2, TOPK)
        ix_u = area(r_at + 256, HEADS, 2, TOPK, dt=U32)
        ix_f = area(r_at + 512, HEADS, 2, TOPK)
        t_top = area(r_at + 768, HEADS, TOPK)
        pos_u = area(r_at + 896, HEADS, TOPK, dt=U32)
        ab_u = area(r_at + 1024, 2, HEADS, TOPK, dt=U32)
        ab_f = area(r_at + 1280, 2, HEADS, TOPK)
        route = [area(2560, 3, HEADS, TOPK), area(2944, 3, HEADS, TOPK)]
        route = [area(r_at + 1536, 3, HEADS, TOPK), None]
        gsum = sb("gsum", [P, HEADS])
        route[1] = sb("route1", [P, 3, HEADS, TOPK])
        hkv = area(4096, KC, T)
        rcos = area(6144, T)
        rsin = area(6400, T)
        rtmp = area(6656, 4, T)
        pos_i = area(7680, T, dt=I32)
        qraw = area(18432, KC, T)
        qrot = area(20480, KC, T)
        kraw = area(22528, 2, T)
        krot = area(23040, 2, T)
        kdup = area(23552, 4, T)
        vN = area(24576, TB, T)
        oT = area(25088, KC, T)
        s_sb = [area(at, 2, 2, T) for at in (27136, 28160, 2560)]
        pT = [area(29184, 2, 4, P), area(30208, 2, 4, P)]
        masks = area(31232, T)
        rot = area(31488, P)
        sinks = area(31616, 4, 4)
        freq = area(31632, 1)
        rowm, nrowm, rsum, esink = ([area(31648 + 8 * n + 4 * k, 4) for k in range(2)] for n in range(4))
        ropet = area(31744, 2, T)

        s5_mem = ExitStack()
        lam = sb("lam", [P, 3, PAIRS], c=s5_mem)
        dcol = sb("dcol", [P, KC], c=s5_mem)
        bglu = sb("bglu", [P, KC], c=s5_mem)
        tt = sb("tt", [P, T], c=s5_mem)
        sm = sb("sm", [P, 24, PAIRS], c=s5_mem)
        ang = sb("ang", [P, 4, T], c=s5_mem)
        bu = sb("bu", [P, 2, 2, T], c=s5_mem)
        m1 = sb("m1", [P, 2, 2, T], c=s5_mem)
        m2 = sb("m2", [P, 2, 2, T], c=s5_mem)
        wz = sb("wz", [P, 2, 2, T], c=s5_mem)
        zz = sb("zz", [P, 2, 2, T], c=s5_mem)
        p1 = sb("p1", [P, 2, 2, T], c=s5_mem)
        p2 = sb("p2", [P, 2, 2, T], c=s5_mem)
        bbtmp = sb("bbtmp", [P, PAIRS, 32], c=s5_mem)
        s5_mem.close()
        flat4 = "p a b t -> p (a b) t"
        NORM_MEM = [([bu[:].rearrange(flat4), m1[:].rearrange(flat4)], zz[:, 0, 0], p1[:, 0, 0])] + \
            [([sq[:, 0:4], sq[:, 4:8]], std, rstd)] * 4
        h_hi = sb("h_hi", [P, KC, T], F32R)
        h_lo = sb("h_lo", [P, KC, T], F32R)
        w_hi = sb("w_hi", [P, 2, KC, P], F32R)
        w_lo = sb("w_lo", [P, 2, KC, P], F32R)
        a_hi = sb("a_hi", [P, 2, T], F32R)
        a_lo = sb("a_lo", [P, 2, T], F32R)
        eq_a = sb("eq_a", [P, 2, 4, HALF], BF16)
        one_g = sb("one_g", [P, 2, 3, 4, HALF], BF16)
        one_b = sb("one_b", [P, 2, 4, P], BF16)
        i0T = sb("i0T", [P, T])
        i1T = sb("i1T", [P, T])
        g_rest = sb("g_rest", [P, T])
        g_part = sb("g_part", [P, 3, T], BF16)

        bank = [ctx.enter_context(nc.psum_tensor(f"bank{i}", [P, 512], F32)) for i in range(8)]

        s_const = sem("s_const")
        s_crow = sem("s_crow")
        s_lam = sem("s_lam")
        s_tt = sem("s_tt")
        s_disc = sem("s_disc")
        s_bbp = sem("s_bbp")
        s_s5in = sem("s_s5in")
        s_slot = [sem(f"s_slot{i}") for i in range(SLOTS)]
        s_plain = sem("s_plain")
        s_hi = sem("s_hi")
        s_lo = sem("s_lo")
        s_split = sem("s_split")
        s_evac = sem("s_evac")
        s_dve = sem("s_dve")
        s_act = sem("s_act")
        s_ones = sem("s_ones")
        s_silu = sem("s_silu")
        s_c0 = [sem(f"s_c0{i}") for i in range(FIRST_SLOTS)]
        s_cin = [sem(f"s_cin{i}") for i in range(2)]
        s_cdone = sem("s_cdone")
        s_sq = sem("s_sq")
        s_ms = sem("s_ms")
        s_var = sem("s_var")
        s_std = sem("s_std")
        s_hn = sem("s_hn")
        s_h = sem("s_h")
        s_x = sem("s_x")
        s_turns = sem("s_turns")
        s_trh = sem("s_trh")
        s_angc = sem("s_angc")
        s_angd = sem("s_angd")
        s_ang = sem("s_ang")
        s_wz = sem("s_wz")
        s_trig = sem("s_trig")
        s_trig0 = sem("s_trig0")
        s_rho = sem("s_rho")
        s_cneg = sem("s_cneg")
        s_bb = sem("s_bb")
        s_bbt = sem("s_bbt")
        s_bbev = sem("s_bbev")
        s_bu = sem("s_bu")
        s_buev = sem("s_buev")
        s_m1 = sem("s_m1")
        s_m2 = sem("s_m2")
        s_z = sem("s_z")
        s_p1 = sem("s_p1")
        s_p2 = sem("s_p2")
        s_y = sem("s_y")
        s_yev = sem("s_yev")
        s_gl = sem("s_gl")
        s_sig = sem("s_sig")
        s_y2 = sem("s_y2")
        s_keys = sem("s_keys")
        s_hhi = sem("s_hhi")
        s_hlo = sem("s_hlo")
        s_sc = sem("s_sc")
        s_scev = sem("s_scev")
        s_gsub = sem("s_gsub")
        s_gexp = sem("s_gexp")
        s_route = sem("s_route")
        s_rt = sem("s_rt")
        s_rtev = sem("s_rtev")
        s_eqa = sem("s_eqa")
        s_oneb = sem("s_oneb")
        s_onea = sem("s_onea")
        s_gmm = sem("s_gmm")
        s_gev = sem("s_gev")
        s_ahi = sem("s_ahi")
        s_alo = sem("s_alo")
        s_attin = sem("s_attin")
        s_rang = sem("s_rang")
        s_rtrig = sem("s_rtrig")
        s_rmm = sem("s_rmm")
        s_rope = sem("s_rope")
        s_kdup = sem("s_kdup")
        s_s = sem("s_s")
        s_sm = sem("s_sm")
        s_p = sem("s_p")
        s_pn = sem("s_pn")
        s_pt = sem("s_pt")
        s_ptev = sem("s_ptev")
        s_o = sem("s_o")
        s_oev = sem("s_oev")
        s_out = sem("s_out")

        SOURCE = {"w_in": w_in, "w_glu": w_glu, "w_out": w_out, "w_kv": w_kv, "attn_q": attn_wq,
                  "w_o": w_o, "peer_q0": peer_wq[0], "peer_q1": peer_wq[1],
                  "u0": u_tab[0], "v0": v_tab[0], "u1": u_tab[1], "v1": v_tab[1]}
        PROJ = {}
        made = 0
        for name, count, _ in STREAM:
            if name[0] != "v":
                PROJ[name] = made
                made += count

        NORM_STATS = 5
        MIX0, FFN0, KVN, MIX1, FFN1, FINAL = range(6)
        SCALE = [1, 4, 13, 7, 10, 15]
        SHIFT = [0, 3, 12, 6, 9, 14]

        def vec(n, ch):
            return cond[:, COND_AT[n] * KC + ch:COND_AT[n] * KC + ch + 1]

        def transposed(s):
            return s // 2 * 3 + s % 2

        block = ctx.enter_context(nc.Block())

        @block.sync
        def _(sp):
            sp.dma_start(lam[:], s5_lam).then_inc(s_lam, 16)
            sp.dma_start(c_row[:], c_row_d).then_inc(s_crow, 16)
            for i in range(16):
                k = i % FIRST_SLOTS
                if i == 2:
                    sp.dma_start(xT[:], x_t).then_inc(s_const, 16)
                if i >= FIRST_SLOTS:
                    sp.wait_ge(s_cdone, i - FIRST_SLOTS + 1)
                sp.dma_start(cond0[k], w_cond0[i]).then_inc(s_c0[k], 16)
            prev = None
            for name, count, is_split in STREAM:
                n0, plain0, split0 = AT[name]
                src = SOURCE[name]

                def load(r, j, freed, by_split):
                    if freed is not None:
                        sp.wait_ge(s_lo if by_split else s_plain, freed)
                    blk = src[r * SLOTS + j] if isinstance(r, int) else \
                        src[bass.ds(r * SLOTS + j, 1)].rearrange("a p n -> p (a n)")
                    sp.dma_start(ring[:, j].rearrange("p a b -> p (a b)"), blk).then_inc(s_slot[j], 16)

                for j in range(SLOTS):
                    if prev is None:
                        load(0, j, None, 0)
                    else:
                        before = split0 if prev[2] else plain0
                        load(0, j, before - SLOTS + j + 1, prev[2])
                first = split0 if is_split else plain0
                if count // SLOTS > 2:
                    with sp.Fori(1, count // SLOTS) as r:
                        for j in range(SLOTS):
                            load(r, j, r * SLOTS + (first - SLOTS + j + 1), is_split)
                else:
                    for r in range(1, count // SLOTS):
                        for j in range(SLOTS):
                            load(r, j, first + (r - 1) * SLOTS + j + 1, is_split)
                prev = (name, count, is_split)
            sp.wait_ge(s_h, 8 * 6)
            sp.dma_start(out_t, hT).then_inc(s_out, 16)
            sp.wait_ge(s_out, 16)

        @block.gpsimd
        def _(pool):
            nc.gpsimd.memset(ones[:], 1.0).then_inc(s_ones, 1)
            nc.gpsimd.memset(zeros[:], 0.0).then_inc(s_ones, 1)
            nc.gpsimd.memset(eps_sb[:, 0:1], TWO_PI / 4).then_inc(s_ones, 1)
            nc.gpsimd.memset(eps_sb[:, 1:2], MAGIC).then_inc(s_ones, 1)

            pool.wait_ge(s_rho, 3)
            pool.wait_ge(s_tt, 16)
            for i in range(0, PAIRS, 4):
                nc.gpsimd.tensor_tensor(cosT[:, i:i + 4], tt[:].unsqueeze(1).broadcast_to([P, 4, T]),
                                        sm[:, 13, i:i + 4].unsqueeze(2).broadcast_to([P, 4, T]), ALU.mult)\
                    .then_inc(s_trh, 1)

            pool.wait_ge(s_s5in, 96)
            pool.wait_ge(s_disc, 2)
            crb = sm[:, 19].unsqueeze(2).broadcast_to([P, PAIRS, 32])
            cib = sm[:, 20].unsqueeze(2).broadcast_to([P, PAIRS, 32])
            nc.gpsimd.tensor_tensor(bb_re, b_re, crb, ALU.mult).then_inc(s_bbp, 1)
            nc.gpsimd.tensor_tensor(bbtmp[:], b_im, cib, ALU.mult).then_inc(s_bbp, 1)
            pool.wait_ge(s_bbp, 2)
            nc.gpsimd.tensor_tensor(bb_re, bb_re, bbtmp[:], ALU.subtract).then_inc(s_bb, 1)
            nc.gpsimd.tensor_tensor(bb_im, b_im, crb, ALU.mult).then_inc(s_bbp, 1)
            pool.wait_ge(s_bb, 1)
            nc.gpsimd.tensor_tensor(bbtmp[:], b_re, cib, ALU.mult).then_inc(s_bbp, 1)
            pool.wait_ge(s_bbp, 4)
            nc.gpsimd.tensor_tensor(bb_im, bb_im, bbtmp[:], ALU.add).then_inc(s_bb, 1)

            def bc(table, pr):
                return table[:, pr:pr + 1, :].broadcast_to([P, 2, T])

            def m2_of(pr, k, first2):
                pool.wait_ge(s_buev, pr + 1)
                if not first2:
                    pool.wait_ge(s_wz, 2 * (pr - 1))
                nc.gpsimd.tensor_tensor(m2[:, k], bu[:, k], bc(sinT, pr), ALU.mult).then_inc(s_m2, 1)

            pool.wait_ge(s_trig, 6)
            m2_of(0, 0, True)

            def s5_round(ch, first, last):
                for q in range(4):
                    pr = ch * 4 + q
                    if not (last and q == 3):
                        m2_of(pr + 1, (q + 1) % 2, first and q == 0)
                    pool.wait_ge(s_z, pr + 1)
                    if not (first and q < 2):
                        pool.wait_ge(s_y, pr - 1)
                    nc.gpsimd.tensor_tensor(p2[:, q % 2], zz[:, q % 2], bc(sinT, pr), ALU.mult)\
                        .then_inc(s_p2, 1)

            for ch in range(KC):
                if ch == 1:
                    pool.wait_ge(s_trig, 8)
                s5_round(ch, ch == 0, ch == KC - 1)

            for layer in range(2):
                su = AT[f"u{layer}"][2]
                with pool.Fori(0, HALF // SLOTS) as r:
                    for j in range(SLOTS):
                        pool.wait_ge(s_hi, r * SLOTS + (su + j + 1))
                        nc.gpsimd.tensor_tensor(w_lo[:, j % 2], ring[:, j], w_hi[:, j % 2].bitcast(F32),
                                                ALU.subtract).then_inc(s_lo, 1)

                def gates(group, k, g, first2):
                    pool.wait_ge(s_eqa, group + 1)
                    if not first2:
                        pool.wait_ge(s_gmm, group - 1)
                    tok = g_part[:, :, g * 4:g * 4 + 4] if isinstance(g, int) else \
                        g_part[:, :, bass.ds(g * 4, 4)]
                    nc.gpsimd.tensor_tensor(one_g[:, k], eq_a[:, k].unsqueeze(1).broadcast_to([P, 3, 4, HALF]),
                                            tok.unsqueeze(3).broadcast_to([P, 3, 4, HALF]), ALU.mult)\
                        .then_inc(s_onea, 1)

                base = 2 * HALF * layer

                def u2(r, first, last):
                    for j in range(SLOTS):
                        g = r * SLOTS + j
                        gates(base + g, j % 2, g, first and j < 2 and layer == 0)

                rounds(pool, HALF // SLOTS, u2)

                def a_low(v, k):
                    pool.wait_ge(s_ahi, EB * layer + v + 1)
                    src = HB[:, v, :] if isinstance(v, int) else HB[:, bass.ds(v, 1), :].rearrange("p a t -> p (a t)")
                    nc.gpsimd.tensor_tensor(a_lo[:, k], src, a_hi[:, k].bitcast(F32), ALU.subtract)\
                        .then_inc(s_alo, 1)

                gates(base + HALF, 0, 0, False)

                def v1(r, first, last):
                    for j in range(SLOTS):
                        g = r * SLOTS + j
                        a_low(g, j % 2)
                        if not (last and j == 3):
                            gates(base + HALF + g + 1, (j + 1) % 2, g + 1, False)

                rounds(pool, HALF // SLOTS, v1)
                with pool.Fori(0, HALF // SLOTS) as r:
                    for j in range(SLOTS):
                        a_low(r * SLOTS + (HALF + j), j % 2)

        @block.scalar
        def _(act):
            act.dma_start(tt[:], time_d).then_inc(s_tt, 16)
            for dst, src in ((bcond[:], b_cond), (norm_sb[:], norms), (ident[:], ident_d), (iota[:], iota_d)):
                act.dma_start(dst, src).then_inc(s_const, 16)
            for dst, src in ((b_re, s5_b[:, 0]), (b_im, s5_b[:, 1]), (c_re, s5_c[:, 0]), (c_im, s5_c[:, 1]),
                             (dcol[:], s5_d), (bglu[:], b_glu)):
                act.dma_start(dst, src).then_inc(s_s5in, 16)

            def load_cond(i, k):
                if not (isinstance(i, int) and i < 2):
                    act.wait_ge(s_cdone, i + (16 - 1))
                blk = w_cond[i] if isinstance(i, int) else \
                    w_cond[bass.ds(i, 1)].rearrange("a p n -> p (a n)")
                act.dma_start(cring[:, k], blk).then_inc(s_cin[k], 16)

            load_cond(0, 0)
            load_cond(1, 1)
            act.wait_ge(s_lam, 16)
            nc.scalar.activation(sm[:, 0], lam[:, 2], ACT.Exp).then_inc(s_act, 1)
            act.wait_ge(s_rho, 1)
            nc.scalar.activation(sm[:, 2], sm[:, 1], ACT.Exp).then_inc(s_act, 1)
            act.wait_ge(s_crow, 16)
            nc.scalar.activation(c_row[:], c_row[:], ACT.Silu).then_inc(s_silu, 1)
            act.wait_ge(s_ones, 4)
            act.wait_ge(s_rho, 2)
            nc.scalar.activation(sm[:, 4], sm[:, 3], ACT.Sin, scale=TWO_PI).then_inc(s_trig0, 1)
            nc.scalar.activation(sm[:, 5], sm[:, 3], ACT.Abs).then_inc(s_act, 1)
            act.wait_ge(s_act, 3)
            nc.scalar.activation(sm[:, 6], sm[:, 5], ACT.Sin, scale=-TWO_PI, bias=eps_sb[:, 0:1])\
                .then_inc(s_trig0, 1)

            def square(k, ch):
                act.wait_ge(s_x, 8 * (k - 1) + ch + 1)
                nc.scalar.activation(sq[:, ch], xT[:, ch], ACT.Square).then_inc(s_sq, 1)

            def root(k):
                act.wait_ge(s_var, k + 1)
                _, root_k, var_k = NORM_MEM[k]
                nc.scalar.activation(root_k, var_k, ACT.Sqrt).then_inc(s_std, 1)

            def shifts(which, dst, n):
                for ch in range(KC):
                    act.wait_ge(s_hn, 8 * n + ch + 1)
                    nc.scalar.activation(dst[:, ch], dst[:, ch], ACT.Identity, bias=vec(SHIFT[which], ch))\
                        .then_inc(s_h, 1)

            def evacuate(name, m, dst):
                act.wait_ge(s_plain, AT[name][1] + m + 1)
                nc.scalar.copy(dst, bank[m % 2][:, 0:T]).then_inc(s_evac, 1)

            def turns(part):
                for pr in part:
                    nc.scalar.activation(sinT[:, pr], tt[:], ACT.Identity, scale=sm[:, 10, pr:pr + 1],
                                         bias=eps_sb[:, 1:2]).then_inc(s_turns, 1)

            def trig(g):
                act.wait_ge(s_ang, 2 * g + 2)
                part = slice(8 * g, 8 * g + 8)
                nc.scalar.activation(cosT[:, part], sinT[:, part], ACT.Abs).then_inc(s_act, 1)
                act.wait_ge(s_act, 4 + g)
                nc.scalar.activation(cosT[:, part], cosT[:, part], ACT.Sin, scale=-TWO_PI,
                                     bias=eps_sb[:, 0:1]).then_inc(s_trig, 1)
                nc.scalar.activation(sinT[:, part], sinT[:, part], ACT.Sin, scale=TWO_PI).then_inc(s_trig, 1)

            act.wait_ge(s_tt, 16)
            turns(range(0, 8))
            act.wait_ge(s_const, 80)
            for half in range(2):
                nc.scalar.activation(NORM_MEM[0][0][half], xT[:, half * 4:half * 4 + 4], ACT.Square)\
                    .then_inc(s_sq, 1)
            turns(range(8, PAIRS))
            root(0)
            act.wait_ge(s_s5in, 96)
            nc.scalar.mul(c_nre, c_re, -1.0).then_inc(s_cneg, 1)
            nc.scalar.mul(c_im, c_im, -1.0).then_inc(s_cneg, 1)
            trig(0)
            trig(1)
            for ch in range(KC):
                act.wait_ge(s_bbt, ch + 1)
                nc.scalar.copy(bbt[:, ch].rearrange("p a b -> p (a b)"),
                               bank[4 + ch % 2][:, 0:256]).then_inc(s_bbev, 1)
            trig(2)
            shifts(MIX0, hT, 0)
            trig(3)
            evacuate("w_in", 0, uT[:, 0])
            for ch in range(KC):
                for q in range(4):
                    pr = ch * 4 + q
                    act.wait_ge(s_bu, pr + 1)
                    if pr >= 2:
                        act.wait_ge(s_m1, pr - 1)
                        act.wait_ge(s_m2, pr - 1)
                    nc.scalar.copy(bu[:, q % 2].rearrange("p a b -> p (a b)"), bank[2 + q][:, :])\
                        .then_inc(s_buev, 1)
                if ch < KC - 1:
                    evacuate("w_in", ch + 1, uT[:, ch + 1])
                if ch >= 1:
                    act.wait_ge(s_yev, ch)
                    nc.scalar.activation(gl[:, ch - 1], yT[:, ch - 1], ACT.Gelu_apprx_tanh).then_inc(s_gl, 1)
            act.wait_ge(s_yev, 8)
            nc.scalar.activation(gl[:, KC - 1], yT[:, KC - 1], ACT.Gelu_apprx_tanh).then_inc(s_gl, 1)
            for m in range(8):
                load_cond(2 + m, m % 2)
                act.wait_ge(s_plain, AT["w_glu"][1] + m + 1)
                nc.scalar.activation(sig[:, m], bank[m % 2][:, 0:T], ACT.Sigmoid, bias=bglu[:, m:m + 1])\
                    .then_inc(s_evac, 1)

            def peer(layer):
                act.wait_ge(s_h, 8 * (2 + 3 * layer))
                act.dma_start(KEYS, keys_d[layer]).then_inc(s_keys, 16)
                nc.scalar.copy(h_hi[:], hT).then_inc(s_hhi, 1)
                for m in range(8):
                    evacuate(f"peer_q{layer}", m, qT[:, m])
                for tb in range(TB):
                    for b in range(4):
                        act.wait_ge(s_sc, 8 * layer + 4 * tb + b + 1)
                        nc.scalar.copy(SC[tb][:, 2 * b:2 * b + 2], bank[2 + b][:, :]
                                       .rearrange("p (a b c) -> p a b c", a=2, b=2)).then_inc(s_scev, 1)
                n0, _, s0 = AT[f"u{layer}"]

                def hi(r, j, off):
                    jj = (j + off) % 4
                    rr = (j + off) // 4
                    act.wait_ge(s_slot[jj], r * 16 + ((n0 // 4 + rr + 1) * 16))
                    if not (layer == 0 and isinstance(r, int) and r * 4 + j + off < 2):
                        act.wait_ge(s_split, r * 4 + (s0 + j + off - 1))
                    nc.scalar.copy(w_hi[:, jj % 2], ring[:, jj]).then_inc(s_hi, 1)

                hi(0, 0, 0)
                hi(0, 1, 0)
                ix = {0: None}

                def exp_gates(tb):
                    act.wait_ge(s_gsub, 2 * layer + tb + 1)
                    dst = route[tb][:, 2]
                    nc.scalar.activation(dst, dst, ACT.Exp).then_inc(s_gexp, 1)

                def gelu(r, j, half):
                    act.wait_ge(s_split, r * 4 + (s0 + half * HALF + j + 1))
                    row = r * 4 + (half * HALF + j)
                    dst = HB[:, row, :] if isinstance(row, int) else \
                        HB[:, bass.ds(row, 1), :].rearrange("p a t -> p (a t)")
                    nc.scalar.activation(dst, bank[j % 2][:, 0:T], ACT.Gelu_apprx_tanh).then_inc(s_evac, 1)

                def u_round(half):
                    def body(r, first, last):
                        for j in range(SLOTS):
                            hi(r + half * (HALF // 4), j, 2)
                            gelu(r, j, half)
                    return body

                n1 = HALF // SLOTS
                with act.Fori(0, 5) as r:
                    u_round(0)(r, False, False)
                exp_gates(0)
                with act.Fori(5, 10) as r:
                    u_round(0)(r, False, False)
                exp_gates(1)
                c0 = COND_U[layer]
                load_cond(c0 + 1, 1)
                with act.Fori(10, n1) as r:
                    for j in range(SLOTS):
                        if j % 2:
                            load_cond(r * 2 + (c0 + 2 - 20 + j // 2), j // 2)
                        hi(r, j, 2)
                        gelu(r, j, 0)
                with act.Fori(0, n1) as r:
                    u_round(1)(r, False, False)

                def a_high(v, k):
                    src = HB[:, v, :] if isinstance(v, int) else HB[:, bass.ds(v, 1), :].rearrange("p a t -> p (a t)")
                    nc.scalar.copy(a_hi[:, k], src).then_inc(s_ahi, 1)

                act.wait_ge(s_gev, 2 * HALF * layer + HALF)
                a_high(0, 0)
                a_high(1, 1)

                def v_round(half, cond_block=None):
                    def body(r, first, last):
                        for j in range(SLOTS):
                            if cond_block is not None and j == 0:
                                load_cond(r * 2 + (cond_block + 1), 1)
                            if cond_block is not None and j == 2:
                                load_cond(r * 2 + (cond_block + 2), 0)
                            final = last and half == 1 and j >= 2
                            if not final:
                                hi(r + (2 + half) * (HALF // 4), j, 2)
                                if half == 0 and last and j == 2:
                                    act.wait_ge(s_gev, 2 * HALF * layer + 2 * HALF)
                                act.wait_ge(s_alo, r * 4 + (EB * layer + half * HALF + j + 1))
                                a_high(r * 4 + (half * HALF + j + 2), j % 2)
                    return body

                if layer == 0:
                    load_cond(COND_V1, 0)
                    v_round(0)(0, True, False)
                    with act.Fori(1, 10) as r:
                        v_round(0, COND_V1 - 2)(r, False, False)
                    with act.Fori(10, n1 - 1) as r:
                        v_round(0)(r, False, False)
                    v_round(0)(n1 - 1, False, True)
                    rounds(act, n1, v_round(1, COND_V2[0]))
                else:
                    load_cond(COND_V2[1], 0)
                    rounds(act, n1, v_round(0))
                    with act.Fori(0, 4) as r:
                        v_round(1, COND_V2[1])(r, False, False)
                    load_cond(COND_V2[1] + 9, 1)
                    with act.Fori(4, n1 - 1) as r:
                        v_round(1)(r, False, False)
                    v_round(1)(n1 - 1, False, True)

            for i in range(10, 13):
                load_cond(i, i % 2)
            for m in range(8):
                square(1, m)
                for i in range(13, COND_U[0] + 1):
                    if (i - 13) * 8 // 12 == m:
                        load_cond(i, i % 2)
            root(1)
            shifts(FFN0, hT, 1)
            peer(0)

            for m in range(8):
                square(2, m)
            for dst, src in ((masks, masks_d), (rot, rot_d), (sinks, sinks_d), (freq, freq_d), (pos_i, pos_d)):
                act.dma_start(dst, src).then_inc(s_attin, 16)
            root(2)
            shifts(KVN, hkv, 2)
            shifts(MIX1, hT, 3)
            evacuate("w_kv", 0, kraw[:, 0])
            act.wait_ge(s_rang, 1)
            nc.scalar.activation(rsin, rtmp[:, 0], ACT.Sin).then_inc(s_rtrig, 1)
            nc.scalar.activation(rtmp[:, 1], rtmp[:, 0], ACT.Abs).then_inc(s_act, 1)
            act.wait_ge(s_act, 8)
            nc.scalar.activation(rcos, rtmp[:, 1], ACT.Sin, scale=-1.0, bias=eps_sb[:, 0:1]).then_inc(s_rtrig, 1)
            evacuate("w_kv", 1, kraw[:, 1])
            for m in range(2):
                act.wait_ge(s_plain, AT["w_kv"][1] + 2 + m + 1)
                nc.scalar.copy(vN[:, :, m * P:(m + 1) * P],
                               bank[m % 2][:, 0:T].rearrange("p (a b) -> p a b", a=2)).then_inc(s_evac, 1)
            for i in range(13):
                if i < 8:
                    evacuate("attn_q", i, qraw[:, i])
                if i == 1:
                    act.wait_ge(s_rope, 2)
                    for src in range(2):
                        for dst in range(2):
                            act.dma_start(kdup[64 * dst:64 * dst + 64, src::2, :],
                                          krot[64 * src:64 * src + 64, :, :]).then_inc(s_kdup, 16)
                if i >= 5:
                    s = i - 5
                    kv, tb = s // 2, s % 2
                    for n, kb in enumerate(range(1 - tb, 2)):
                        act.wait_ge(s_pt, transposed(s) + n + 1)
                        nc.scalar.copy(pT[s % 2][:, kb], bank[6 + kb][:, :]
                                       .rearrange("p (a b) -> p a b", a=4)).then_inc(s_ptev, 1)
                    act.wait_ge(s_o, s + 1)
                    nc.scalar.copy(oT[:, 2 * kv:2 * kv + 2, tb * P:tb * P + P],
                                   bank[5][:, 0:T].rearrange("p (a b) -> p a b", a=2)).then_inc(s_oev, 1)
                if 3 <= i < 11:
                    s = i - 3
                    k0, nk = (P, P) if s % 2 == 0 else (0, T)
                    act.wait_ge(s_sm, s + 1)
                    for r in range(2):
                        for mm in range(2):
                            head = 2 * r + mm
                            view = s_sb[s % 3][:, r, mm, k0:k0 + nk]
                            nc.scalar.activation(view, view, ACT.Exp, bias=nrowm[s % 2][:, head:head + 1],
                                                 accum_out=rsum[s % 2][:, head:head + 1]).then_inc(s_p, 1)
                    nc.scalar.activation(esink[s % 2], esink[s % 2], ACT.Exp).then_inc(s_p, 1)
            for m in range(8):
                square(3, m)
            root(3)
            shifts(FFN1, hT, 4)
            peer(1)
            for m in range(8):
                square(4, m)
            root(4)
            shifts(FINAL, hT, 5)

        @block.vector
        def _(dve):
            v = nc.vector
            st = Steps(dve, s_dve)

            def do(ins):
                st.add(ins)
                st.sync()

            def cond_column(col, blk):
                out = cond[:, col:col + 1] if isinstance(col, int) else cond[:, bass.ds(col, 1)]
                v.scalar_tensor_tensor(blk, blk, 1.0, c_row[:], ALU.mult, ALU.mult, accum_out=out)\
                    .then_inc(s_cdone, 1)

            def cond_ring(i, k):
                dve.wait_ge(s_cin[k], i * 8 + (16 - 8 * k))
                cond_column(i + 16, cring[:, k])

            def cond_bias(group):
                dve.wait_ge(s_cdone, COND_FIRST[group + 1])
                cols = slice(COND_FIRST[group], COND_FIRST[group + 1])
                do(v.tensor_tensor(cond[:, cols], cond[:, cols], bcond[:, cols], ALU.add))

            def scales(which):
                st.add(v.scalar_tensor_tensor(gs[:, which], cond[:, COND_AT[SCALE[which]] * KC:COND_AT[SCALE[which]] * KC + KC], 1.0,
                                              norm_sb[:, which], ALU.add, ALU.mult))

            def stats(k):
                _, root_k, rstd_k = NORM_MEM[k]
                dve.wait_ge(s_ms, k + 1)
                v.tensor_scalar(rstd_k, bank[6][:, 0:T], 1.0 / D, 1e-6, ALU.mult, ALU.add).then_inc(s_var, 1)
                dve.wait_ge(s_std, k + 1)
                do(v.reciprocal(rstd_k, root_k))

            def normalise(which, dst):
                rstd_k = NORM_MEM[0 if which == MIX0 else 1][2]
                for ch in range(KC):
                    v.scalar_tensor_tensor(dst[:, ch], xT[:, ch], gs[:, which, ch:ch + 1], rstd_k,
                                           ALU.mult, ALU.mult).then_inc(s_hn, 1)

            def residual(name, gate, m):
                dve.wait_ge(s_plain, AT[name][1] + m + 1)
                v.scalar_tensor_tensor(xT[:, m], bank[m % 2][:, 0:T], vec(gate, m), xT[:, m],
                                       ALU.mult, ALU.add).then_inc(s_x, 1)

            dve.wait_ge(s_lam, 16)
            dve.wait_ge(s_act, 1)
            a_re, a_im = lam[:, 0], lam[:, 1]
            v.tensor_tensor(sm[:, 1], a_re, sm[:, 0], ALU.mult).then_inc(s_rho, 1)
            theta, th, tl, acc, n, rl, rh = (sm[:, i] for i in range(7, 14))
            t1, t2 = sm[:, 14], sm[:, 15]
            do(v.tensor_tensor(theta, a_im, sm[:, 0], ALU.mult))
            inv = 1.0 / TWO_PI
            i1 = float(np.float32(np.round(inv * 2.0 ** 14) / 2.0 ** 14))
            i2 = float(np.float32(inv - i1))
            do(v.tensor_scalar(t1, theta, 4097.0, None, ALU.mult))
            do(v.tensor_tensor(t2, t1, theta, ALU.subtract))
            do(v.tensor_tensor(th, t1, t2, ALU.subtract))
            do(v.tensor_tensor(tl, theta, th, ALU.subtract))
            st.add(v.tensor_scalar(th, th, i1, None, ALU.mult))
            st.add(v.tensor_scalar(tl, tl, i1, None, ALU.mult))
            do(v.tensor_scalar(t1, theta, i2, None, ALU.mult))
            do(v.tensor_tensor(tl, tl, t1, ALU.add))
            do(v.tensor_tensor(acc, th, tl, ALU.add))
            do(v.tensor_scalar(n, acc, MAGIC, -MAGIC, ALU.add, ALU.add))
            do(v.tensor_tensor(th, th, n, ALU.subtract))
            do(v.tensor_tensor(acc, th, tl, ALU.add))
            v.tensor_scalar(sm[:, 3], acc, 0.49999997, -0.49999997, ALU.min, ALU.max).then_inc(s_rho, 1)
            v.tensor_scalar(rh, acc, MAGIC15, -MAGIC15, ALU.add, ALU.add).then_inc(s_rho, 1)
            dve.wait_ge(s_rho, 3)
            do(v.tensor_tensor(rl, th, rh, ALU.subtract))
            do(v.tensor_tensor(rl, rl, tl, ALU.add))
            mag, lre, lim, den, cr, ci = (sm[:, i] for i in (2, 16, 17, 18, 19, 20))
            dve.wait_ge(s_trig0, 2)
            dve.wait_ge(s_act, 2)
            do(v.tensor_tensor(lre, mag, sm[:, 6], ALU.mult))
            st.add(v.tensor_tensor(lim, mag, sm[:, 4], ALU.mult))
            st.add(v.tensor_tensor(den, a_re, a_re, ALU.mult))
            st.add(v.tensor_tensor(t1, a_im, a_im, ALU.mult))
            do(v.tensor_scalar(lre, lre, -1.0, None, ALU.add))
            do(v.tensor_tensor(den, den, t1, ALU.add))
            do(v.reciprocal(den, den))
            st.add(v.tensor_tensor(cr, lre, a_re, ALU.mult))
            st.add(v.tensor_tensor(t1, lim, a_im, ALU.mult))
            st.add(v.tensor_tensor(ci, lim, a_re, ALU.mult))
            do(v.tensor_tensor(t2, lre, a_im, ALU.mult))
            st.add(v.tensor_tensor(cr, cr, t1, ALU.add))
            do(v.tensor_tensor(ci, ci, t2, ALU.subtract))
            v.tensor_tensor(cr, cr, den, ALU.mult).then_inc(s_disc, 1)
            v.tensor_tensor(ci, ci, den, ALU.mult).then_inc(s_disc, 1)
            for g in range(0, PAIRS, 4):
                dve.wait_ge(s_turns, g + 4)
                dve.wait_ge(s_trh, g // 4 + 1)
                if g:
                    dve.wait_ge(s_angd, g)
                for pr in range(g, g + 4):
                    v.scalar_tensor_tensor(ang[:, pr % 4], sinT[:, pr], -MAGIC, cosT[:, pr], ALU.add,
                                           ALU.subtract).then_inc(s_angc, 1)
                for pr in range(g, g + 4):
                    dve.wait_ge(s_angc, pr + 1)
                    v.scalar_tensor_tensor(sinT[:, pr], tt[:], rl[:, pr:pr + 1], ang[:, pr % 4], ALU.mult,
                                           ALU.subtract).then_inc(s_angd, 1)
                dve.wait_ge(s_angd, g + 4)
                part = sinT[:, g:g + 4]
                v.tensor_scalar(part, part, 0.49999997, -0.49999997, ALU.min, ALU.max).then_inc(s_ang, 1)
                if g == 0:
                    dve.wait_ge(s_silu, 1)
                for i in range(g // 2, g // 2 + 2):
                    dve.wait_ge(s_c0[i % FIRST_SLOTS], 16 * (i // FIRST_SLOTS + 1))
                    cond_column(i, cond0[i % FIRST_SLOTS])
                if g == 8:
                    stats(0)
            dve.wait_ge(s_const, 80)
            cond_bias(0)
            scales(MIX0)
            st.sync()
            normalise(MIX0, hT)
            def bc(table, pr):
                return table[:, bass.ds(pr, 1), :].broadcast_to([P, 2, T]) if not isinstance(pr, int) \
                    else table[:, pr:pr + 1, :].broadcast_to([P, 2, T])

            def m1_of(pr, k):
                dve.wait_ge(s_buev, pr + 1)
                v.tensor_tensor(m1[:, k], bu[:, k], bc(cosT, pr), ALU.mult).then_inc(s_m1, 1)

            def p1_of(pr, k, first2):
                dve.wait_ge(s_z, pr + 1)
                if not first2:
                    dve.wait_ge(s_y, pr - 1)
                v.tensor_tensor(p1[:, k], zz[:, k], bc(cosT, pr), ALU.mult).then_inc(s_p1, 1)

            def y_of(ch, k):
                dve.wait_ge(s_y, ch * 4 + 4)
                chs = slice(ch, ch + 1) if isinstance(ch, int) else bass.ds(ch, 1)
                flat = "p a t -> p (a t)"
                v.scalar_tensor_tensor(yT[:, chs].rearrange(flat), uT[:, chs].rearrange(flat), dcol[:, chs],
                                       bank[6 + k][:, 0:T], ALU.mult, ALU.add).then_inc(s_yev, 1)

            dve.wait_ge(s_trig, 6)
            m1_of(0, 0)

            def s5_round(r, first, last):
                for q in range(8):
                    pr = r * 8 + q
                    k = q % 2
                    early = first and q < 2
                    dve.wait_ge(s_m1, pr + 1)
                    dve.wait_ge(s_m2, pr + 1)
                    if not early:
                        dve.wait_ge(s_z, pr - 1)
                    v.tensor_tensor(wz[:, k, 0], m1[:, k, 0], m2[:, k, 1], ALU.add).then_inc(s_wz, 1)
                    v.tensor_tensor(wz[:, k, 1], m1[:, k, 1], m2[:, k, 0], ALU.subtract).then_inc(s_wz, 1)
                    if not (first and q == 0):
                        p1_of(pr - 1, (q + 1) % 2, first and q < 3)
                    if not (last and q == 7):
                        if not (first and q == 0):
                            dve.wait_ge(s_wz, 2 * pr)
                        m1_of(pr + 1, (q + 1) % 2)
                    dve.wait_ge(s_wz, 2 * pr + 2)
                    if not early:
                        dve.wait_ge(s_p1, pr - 1)
                        dve.wait_ge(s_p2, pr - 1)
                    magp = mag[:, bass.ds(pr, 1)] if not isinstance(pr, int) else mag[:, pr:pr + 1]
                    magb = magp.broadcast_to([P, T])
                    v.tensor_tensor_scan(zz[:, k, 0], magb, wz[:, k, 0], 0.0, ALU.mult, ALU.add)
                    v.tensor_tensor_scan(zz[:, k, 1], magb, wz[:, k, 1], 0.0, ALU.mult, ALU.add).then_inc(s_z, 1)
                    if q == 1 and not first:
                        y_of(r * 2 - 1, 1)
                    if q == 5:
                        y_of(r * 2, 0)
                if first:
                    dve.wait_ge(s_trig, 8)

            rounds(dve, KC // 2, s5_round)
            p1_of(PAIRS - 1, 1, False)
            y_of(KC - 1, 1)
            for m in range(8):
                cond_ring(m, m % 2)
                dve.wait_ge(s_evac, PROJ["w_glu"] + m + 1)
                if m == 0:
                    dve.wait_ge(s_gl, KC)
                v.tensor_tensor(y2[:, m], gl[:, m], sig[:, m], ALU.mult).then_inc(s_y2, 1)
            for i in range(8, 12):
                cond_ring(i, i % 2)
            dve.wait_ge(s_cdone, 24)
            do(v.tensor_tensor(cond[:, 16:24], cond[:, 16:24], bcond[:, 16:24], ALU.add))
            for m in range(8):
                residual("w_out", 2, m)
                for i in range(12, 24):
                    if (i - 12) * 8 // 12 == m:
                        cond_ring(i, i % 2)
            dve.wait_ge(s_cdone, 40)
            do(v.tensor_tensor(cond[:, 24:40], cond[:, 24:40], bcond[:, 24:40], ALU.add))
            scales(FFN0)
            st.sync()

            def top16(src, vals, idx, n):
                for g in range(0, n, 4):
                    rows = range(g, g + 4)
                    for i in rows:
                        st.add(v.max(vals[i][:, 0:8], src[i]))
                    st.sync()
                    for i in rows:
                        st.add(v.max_index(idx[i][:, 0:8], vals[i][:, 0:8], src[i]))
                    st.sync()
                    for i in rows:
                        st.add(v.match_replace(src[i], vals[i][:, 0:8], src[i], -3.0e38))
                    st.sync()
                    for i in rows:
                        st.add(v.max(vals[i][:, 8:16], src[i]))
                    st.sync()
                    for i in rows:
                        st.add(v.max_index(idx[i][:, 8:16], vals[i][:, 8:16], src[i]))
                st.sync()

            def peer(layer):
                dve.wait_ge(s_hhi, layer + 1)
                v.tensor_tensor(h_lo[:], hT, h_hi[:].bitcast(F32), ALU.subtract).then_inc(s_hlo, 1)
                for tb in range(TB):
                    dve.wait_ge(s_scev, 8 * layer + 4 * tb + 4)
                    hp = [(h, p) for h in range(HEADS) for p in range(2)]
                    top16([SC[tb][:, h, p] for h, p in hp], [v_top[:, h, p] for h, p in hp],
                          [ix_u[:, h, p] for h, p in hp], 2 * HEADS)
                    full = [P, HEADS, TOPK, TOPK]
                    st.add(v.tensor_copy(ix_f, ix_u))
                    do(v.tensor_tensor(CAND, v_top[:, :, 0].unsqueeze(3).broadcast_to(full),
                                       v_top[:, :, 1].unsqueeze(2).broadcast_to(full), ALU.add))
                    top16([CAND[:, h].rearrange("p a b -> p (a b)") for h in range(HEADS)],
                          [t_top[:, h] for h in range(HEADS)], [pos_u[:, h] for h in range(HEADS)], HEADS)
                    st.add(v.tensor_scalar(ab_u[:, 0], pos_u, 4, None, ALU.logical_shift_right))
                    do(v.tensor_scalar(ab_u[:, 1], pos_u, 15, None, ALU.bitwise_and))
                    do(v.tensor_copy(ab_f, ab_u))
                    io = iota[:, 0:TOPK].unsqueeze(1).unsqueeze(1).broadcast_to(full)
                    for half in range(2):
                        do(v.tensor_tensor(EQ, ab_f[:, half].unsqueeze(3).broadcast_to(full), io, ALU.is_equal))
                        do(v.tensor_tensor(EQ, EQ, ix_f[:, :, half].unsqueeze(2).broadcast_to(full), ALU.mult))
                        do(v.tensor_reduce(route[tb][:, half], EQ, axis=AX.X, op=ALU.add))
                    v.tensor_tensor(route[tb][:, 2], t_top, t_top[:, :, 0:1].broadcast_to([P, HEADS, TOPK]),
                                    ALU.subtract).then_inc(s_gsub, 1)
                    dve.wait_ge(s_gexp, 2 * layer + tb + 1)
                    do(v.tensor_reduce(gsum[:], route[tb][:, 2], axis=AX.X, op=ALU.add))
                    do(v.reciprocal(gsum[:], gsum[:]))
                    v.tensor_tensor(route[tb][:, 2], route[tb][:, 2],
                                    gsum[:].unsqueeze(2).broadcast_to([P, HEADS, TOPK]), ALU.mult)\
                        .then_inc(s_route, 1)
                with dve.Fori(0, 7) as r:
                    for k in range(2):
                        cond_ring(r * 2 + (COND_U[layer] + k), k)
                for tb in range(TB):
                    dve.wait_ge(s_rt, 2 * layer + tb + 1)
                    cols = slice(tb * P, tb * P + P)
                    st.add(v.tensor_copy(i0T[:, cols], bank[6 + tb][:, 0:P]))
                    st.add(v.tensor_copy(i1T[:, cols], bank[6 + tb][:, P:2 * P]))
                    do(v.tensor_copy(g_part[:, 0, cols], bank[6 + tb][:, 2 * P:3 * P]))
                    do(v.tensor_tensor(g_rest[:, cols], bank[6 + tb][:, 2 * P:3 * P], g_part[:, 0, cols],
                                       ALU.subtract))
                    do(v.tensor_copy(g_part[:, 1, cols], g_rest[:, cols]))
                    v.tensor_tensor(g_part[:, 2, cols], g_rest[:, cols], g_part[:, 1, cols],
                                    ALU.subtract).then_inc(s_rtev, 1)
                dve.wait_ge(s_rtev, 2 * layer + 2)
                st.sync()
                base = 2 * HALF * layer
                su = AT[f"u{layer}"][2]

                def one_hots(group, k, g, half, first2):
                    for idx, out, first_key, width, s in ((i0T, eq_a, half * HALF, HALF, s_eqa),
                                                          (i1T, one_b, 0, P, s_oneb)):
                        tok = idx[:, g * 4:g * 4 + 4] if isinstance(g, int) else idx[:, bass.ds(g * 4, 4)]
                        if not first2:
                            dve.wait_ge(s_onea if s is s_eqa else s_gmm, group - 1)
                        v.tensor_tensor(out[:, k], tok.unsqueeze(2).broadcast_to([P, 4, width]),
                                        iota[:, first_key:first_key + width].unsqueeze(1)
                                        .broadcast_to([P, 4, width]), ALU.is_equal).then_inc(s, 1)

                def low(r, j, off):
                    dve.wait_ge(s_hi, r * 4 + (su + off + j + 1))
                    v.tensor_tensor(w_lo[:, j % 2], ring[:, j], w_hi[:, j % 2].bitcast(F32), ALU.subtract)\
                        .then_inc(s_lo, 1)

                def apply_gates(group, k, g, half):
                    if isinstance(g, int) and g == 0:
                        dve.wait_ge(s_evac, e_u + (half + 1) * HALF)
                    dve.wait_ge(s_gmm, group + 1)
                    rows = HB[:, half * HALF:half * HALF + HALF, :]
                    rows = rows[:, :, g * 4:g * 4 + 4] if isinstance(g, int) else rows[:, :, bass.ds(g * 4, 4)]
                    rows = rows.rearrange("p i t -> p t i")
                    v.tensor_tensor(rows, bank[6 + k][:, 0:4 * HALF].rearrange("p (t i) -> p t i", t=4),
                                    rows, ALU.mult).then_inc(s_gev, 1)

                def both(half, cond_block=None):
                    def body(r, first, last):
                        for j in range(SLOTS):
                            if cond_block is not None and j >= 2:
                                cond_ring(r * 2 + (cond_block + j - 2), j - 2)
                            g = r * SLOTS + j
                            low(r, j, HALF * (1 + half))
                            if not (last and j == 3):
                                one_hots(base + half * HALF + g + 1, (j + 1) % 2, g + 1, half,
                                         layer == 0 and half == 0 and first and j == 0)
                            elif half == 0:
                                one_hots(base + HALF, 0, 0, 1, False)
                            if not (first and j == 0):
                                apply_gates(base + half * HALF + g - 1, (j + 1) % 2, g - 1, half)
                            elif half == 1:
                                pass
                            if last and j == 3:
                                apply_gates(base + half * HALF + g, j % 2, g, half)
                    return body

                e_u = PROJ[f"u{layer}"] - 8 * (layer + 1)
                one_hots(base, 0, 0, 0, layer == 0)
                rounds(dve, HALF // SLOTS, both(0))
                def last_half(cond_block):
                    def body(r):
                        for j in range(SLOTS):
                            low(r, j, 3 * HALF)
                            if cond_block is not None and j % 2:
                                cond_ring(r * 2 + (cond_block + j // 2), j // 2)
                    return body

                n1 = HALF // SLOTS
                if layer == 0:
                    both(1)(0, True, False)
                    with dve.Fori(1, 10) as r:
                        both(1, COND_V1 - 2)(r, False, False)
                    with dve.Fori(10, n1 - 1) as r:
                        both(1)(r, False, False)
                    both(1)(n1 - 1, False, True)
                    with dve.Fori(0, n1) as r:
                        last_half(COND_V2[0])(r)
                    for group in (2, 3, 4):
                        cond_bias(group)
                    scales(FFN1)
                    scales(KVN)
                    scales(MIX1)
                else:
                    rounds(dve, n1, both(1))
                    with dve.Fori(0, 5) as r:
                        last_half(COND_V2[1])(r)
                    with dve.Fori(5, n1) as r:
                        last_half(None)(r)
                    cond_bias(5)
                    scales(FINAL)
                st.sync()
                dve.wait_ge(s_split, su + 2 * EB)
                for ch in range(KC):
                    v.scalar_tensor_tensor(xT[:, ch], bank[2 + ch // 2][:, (ch % 2) * T:(ch % 2) * T + T],
                                           vec(6 * layer + 5, ch), xT[:, ch], ALU.mult, ALU.add).then_inc(s_x, 1)

            stats(1)
            normalise(FFN0, hT)
            dve.wait_ge(s_h, 16)
            peer(0)

            stats(2)
            normalise(KVN, hkv)
            normalise(MIX1, hT)
            dve.wait_ge(s_attin, 80)
            c1 = 6.28125
            c2 = float(np.float32(round((TWO_PI - c1) * 2.0 ** 21) / 2.0 ** 21))
            c3 = float(np.float32(TWO_PI - c1 - c2))
            do(v.tensor_copy(rtmp[:, 1], pos_i))
            do(v.tensor_scalar(rtmp[:, 1], rtmp[:, 1], freq, None, ALU.mult))
            do(v.tensor_scalar(rtmp[:, 2], rtmp[:, 1], inv, MAGIC, ALU.mult, ALU.add))
            do(v.tensor_scalar(rtmp[:, 2], rtmp[:, 2], -MAGIC, None, ALU.add))
            for cc in (c1, c2, c3):
                do(v.scalar_tensor_tensor(rtmp[:, 1], rtmp[:, 2], -cc, rtmp[:, 1], ALU.mult, ALU.add))
            v.tensor_scalar(rtmp[:, 0], rtmp[:, 1], 3.1415925, -3.1415925, ALU.min, ALU.max).then_inc(s_rang, 1)
            dve.wait_ge(s_rtrig, 2)

            def rope(m):
                src, dst = (kraw[:, m], krot[:, m]) if m < 2 else (qraw[:, m - 2], qrot[:, m - 2])
                dve.wait_ge(s_evac, (PROJ["w_kv"] + m + 1 if m < 2 else PROJ["attn_q"] + m - 1) - 8)
                st.add(v.tensor_tensor(ropet[:, 0], src, rcos, ALU.mult))
                dve.wait_ge(s_rmm, m + 1)
                st.add(v.tensor_tensor(ropet[:, 1], bank[4][:, 0:T], rsin, ALU.mult))
                st.sync()
                v.tensor_tensor(dst, ropet[:, 0], ropet[:, 1], ALU.add).then_inc(s_rope, 1)
                dve.wait_ge(s_rope, m + 1)

            def masked(s):
                kv, tb = s // 2, s % 2
                k0, nk = (P, P) if tb == 0 else (0, T)
                own, k = s_sb[s % 3], s % 2
                dve.wait_ge(s_s, s + 1)
                if s >= 3:
                    dve.wait_ge(s_pt, transposed(s - 2))
                for r in range(2):
                    st.add(v.scalar_tensor_tensor(
                        own[:, r, :, k0:k0 + nk],
                        bank[2 + r][:, :].rearrange("p (a b) -> p a b", a=2)[:, :, k0:k0 + nk],
                        0.125, masks[:, k0:k0 + nk].unsqueeze(1).broadcast_to([P, 2, nk]), ALU.mult, ALU.add))
                st.sync()
                do(v.tensor_reduce(rowm[k], own[:, :, :, k0:k0 + nk], axis=AX.X, op=ALU.max))
                do(v.tensor_tensor(rowm[k], rowm[k], sinks[:, kv], ALU.max))
                st.add(v.tensor_scalar(nrowm[k], rowm[k], -1.0, None, ALU.mult))
                st.sync()
                v.tensor_tensor(esink[k], sinks[:, kv], rowm[k], ALU.subtract).then_inc(s_sm, 1)

            def probabilities(s):
                k0, nk = (P, P) if s % 2 == 0 else (0, T)
                flat, k = s_sb[s % 3][:, :, :, k0:k0 + nk], s % 2
                dve.wait_ge(s_p, 5 * (s + 1))
                do(v.tensor_tensor(rsum[k], rsum[k], esink[k], ALU.add))
                do(v.reciprocal(rsum[k], rsum[k]))
                v.tensor_tensor(flat, flat, rsum[k].rearrange("p (a b) -> p a b", a=2).unsqueeze(3)
                                .broadcast_to([P, 2, 2, nk]), ALU.mult).then_inc(s_pn, 1)
                dve.wait_ge(s_pn, s + 1)

            rope(0)
            rope(1)
            for i in range(1, 12):
                if i <= 8:
                    rope(i + 1)
                if 3 <= i < 11:
                    masked(i - 3)
                if i >= 4:
                    probabilities(i - 4)
            for m in range(8):
                residual("w_o", 8, m)
            stats(3)
            normalise(FFN1, hT)
            dve.wait_ge(s_h, 40)
            peer(1)
            stats(4)
            normalise(FINAL, hT)

        @block.tensor
        def _(pe):
            mm = nc.tensor.matmul

            def arrived(name, m):
                n = AT[name][0] + m
                pe.wait_ge(s_slot[n % 4], 16 * (n // 4 + 1))

            def project(name, src):
                for m in range(8):
                    arrived(name, m)
                    r = PROJ[name] + m
                    if r >= 2:
                        pe.wait_ge(s_evac, r - 1)
                    for kc in range(KC):
                        last = mm(bank[m % 2][:, 0:T], ring[:, m % 4, kc], src[:, kc], start=kc == 0,
                                  stop=kc == KC - 1)
                    last.then_inc(s_plain, 1)

            def sum_squares(k, ch):
                pe.wait_ge(s_sq, ch // 4 + 1 if k == 0 else 2 + 8 * (k - 1) + ch + 1)
                src = NORM_MEM[0][0][ch // 4][:, ch % 4] if k == 0 else sq[:, ch]
                last = mm(bank[6][:, 0:T], ones[:], src, start=ch == 0, stop=ch == KC - 1)
                if ch == KC - 1:
                    last.then_inc(s_ms, 1)

            pe.wait_ge(s_ones, 2)
            for ch in range(KC):
                sum_squares(0, ch)
            pe.wait_ge(s_bb, 2)
            for ch in range(KC):
                if ch >= 2:
                    pe.wait_ge(s_bbev, ch - 1)
                for i, b in enumerate((bb_re, bb_im)):
                    last = nc.tensor.transpose(bank[4 + ch % 2][:, i * P:i * P + P],
                                               b[:, 4 * ch:4 * ch + 4].rearrange("p a b -> p (a b)"), ident[:])
                last.then_inc(s_bbt, 1)

            def w_in_part(m, part):
                if part == 0:
                    arrived("w_in", m)
                    if m >= 2:
                        pe.wait_ge(s_evac, m - 1)
                for kc in (2 * part, 2 * part + 1):
                    if m == 0:
                        pe.wait_ge(s_h, kc + 1)
                    last = mm(bank[m % 2][:, 0:T], ring[:, m % 4, kc], hT[:, kc], start=kc == 0,
                              stop=kc == KC - 1)
                if part == 3:
                    last.then_inc(s_plain, 1)

            for m in range(2):
                for part in range(4):
                    w_in_part(m, part)
            pe.wait_ge(s_bbev, 8)
            pe.wait_ge(s_cneg, 2)

            def bu_of(pr):
                ch, q = pr // 4, pr % 4
                if q == 0:
                    pe.wait_ge(s_evac, ch + 1)
                if pr >= 4:
                    pe.wait_ge(s_buev, pr - 3)
                rows = slice(32 * q, 32 * q + 32)
                for i in range(2):
                    last = mm(bank[2 + q][:, i * T:i * T + T], bbt[rows, ch, i], uT[rows, ch], start=True,
                              stop=True)
                last.then_inc(s_bu, 1)

            for pr in range(4):
                bu_of(pr)
            for ch in range(KC):
                for q in range(4):
                    pr = 4 * ch + q
                    if pr + 4 < PAIRS:
                        bu_of(pr + 4)
                    if ch + 2 < KC:
                        w_in_part(ch + 2, q)
                    pe.wait_ge(s_p1, pr + 1)
                    pe.wait_ge(s_p2, pr + 1)
                    if q == 0 and ch >= 2:
                        pe.wait_ge(s_yev, ch - 1)
                    out = bank[6 + ch % 2][32 * q:32 * q + 32, 0:T]
                    k = q % 2
                    mm(out, c_re[:, pr], p1[:, k, 0], start=True, stop=False)
                    mm(out, c_nre[:, pr], p2[:, k, 1], start=False, stop=False)
                    mm(out, c_im[:, pr], p1[:, k, 1], start=False, stop=False)
                    mm(out, c_im[:, pr], p2[:, k, 0], start=False, stop=True).then_inc(s_y, 1)
            pe.wait_ge(s_gl, KC)
            project("w_glu", gl)
            pe.wait_ge(s_y2, 8)

            def project_x(name, src, x0, k):
                for m in range(8):
                    arrived(name, m)
                    if m >= 2:
                        pe.wait_ge(s_x, x0 + m - 1)
                    for kc in range(KC):
                        last = mm(bank[m % 2][:, 0:T], ring[:, m % 4, kc], src[:, kc], start=kc == 0,
                                  stop=kc == KC - 1)
                    last.then_inc(s_plain, 1)
                    if m >= 1:
                        sum_squares(k, m - 1)
                sum_squares(k, KC - 1)

            project_x("w_out", y2, 0, 1)

            def peer(layer):
                n0, _, s0 = AT[f"u{layer}"]
                name = f"peer_q{layer}"
                for m in range(8):
                    arrived(name, m)
                    if m >= 2:
                        pe.wait_ge(s_evac, PROJ[name] - DONE_BY_X[name] + m - 1)
                    for kc in range(KC):
                        if m == 0:
                            pe.wait_ge(s_h, 8 * (1 + 3 * layer) + kc + 1)
                        last = mm(bank[m % 2][:, 0:T], ring[:, m % 4, kc], hT[:, kc], start=kc == 0,
                                  stop=kc == KC - 1)
                    last.then_inc(s_plain, 1)
                pe.wait_ge(s_keys, 16 * (layer + 1))
                e0 = PROJ[name] - DONE_BY_X[name] + 8
                pe.wait_ge(s_evac, e0)
                for tb in range(TB):
                    for h in range(HEADS):
                        if tb == 1 and h % 2 == 0:
                            pe.wait_ge(s_scev, 8 * layer + h // 2 + 1)
                        last = mm(bank[2 + h // 2][:, (h % 2) * T:(h % 2) * T + T],
                                  qT[:, h, tb * P:tb * P + P], KEYS[:, h], start=True, stop=True)
                        if h % 2:
                            last.then_inc(s_sc, 1)

                pe.wait_ge(s_hlo, layer + 1)

                def u_block(r, j, half):
                    b = r * STRIDE + (s0 + half * HALF + j)
                    pe.wait_ge(s_hi, b + 1)
                    pe.wait_ge(s_evac, r * STRIDE + (e0 + half * HALF + j - 1))
                    out, k = bank[j % 2][:, 0:T], j % 2
                    for kc in range(KC):
                        mm(out, w_hi[:, k, kc], h_hi[:, kc], start=kc == 0, stop=False)
                        mm(out, w_hi[:, k, kc], h_lo[:, kc], start=False, stop=False)
                    pe.wait_ge(s_lo, b + 1)
                    for kc in range(KC):
                        last = mm(out, w_lo[:, k, kc], h_hi[:, kc], start=False, stop=kc == KC - 1)
                    last.then_inc(s_split, 1)

                def gate_group(group, j, first2):
                    pe.wait_ge(s_oneb, group + 1)
                    pe.wait_ge(s_onea, group + 1)
                    if not first2:
                        pe.wait_ge(s_gev, group - 1)
                    k = j % 2
                    for t in range(4):
                        out = bank[6 + k][:, t * HALF:t * HALF + HALF]
                        for part in range(3):
                            last = mm(out, one_b[:, k, t], one_g[:, k, part, t], start=part == 0,
                                      stop=part == 2)
                    last.then_inc(s_gmm, 1)

                with pe.Fori(0, HALF // STRIDE) as r:
                    for j in range(STRIDE):
                        u_block(r, j, 0)
                for tb in range(TB):
                    pe.wait_ge(s_route, 2 * layer + tb + 1)
                    for i in range(3):
                        last = nc.tensor.transpose(bank[6 + tb][:, i * P:i * P + P],
                                                   route[tb][:, i].rearrange("p a b -> p (a b)"), ident[:])
                    last.then_inc(s_rt, 1)
                pe.wait_ge(s_rtev, 2 * layer + 2)
                base = 2 * HALF * layer

                def u2(r, first, last):
                    for j in range(STRIDE):
                        u_block(r, j, 1)
                        gate_group(base + r * STRIDE + j, j, layer == 0 and first and j < 2)

                rounds(pe, HALF // STRIDE, u2)
                for b in range(4):
                    mm(bank[2 + b][:, :], zeros[:], ring0[:, 0:512], start=True, stop=False)

                def v_block(r, j, half, final):
                    b = r * STRIDE + (s0 + EB + half * HALF + j)
                    a = r * STRIDE + (EB * layer + half * HALF + j)
                    k = j % 2
                    pe.wait_ge(s_hi, b + 1)
                    pe.wait_ge(s_ahi, a + 1)
                    pe.wait_ge(s_alo, a + 1)
                    for ch in range(KC):
                        out = bank[2 + ch // 2][:, (ch % 2) * T:(ch % 2) * T + T]
                        mm(out, w_hi[:, k, ch], a_hi[:, k], start=False, stop=False)
                        mm(out, w_hi[:, k, ch], a_lo[:, k], start=False, stop=False)
                    pe.wait_ge(s_lo, b + 1)
                    for ch in range(KC):
                        out = bank[2 + ch // 2][:, (ch % 2) * T:(ch % 2) * T + T]
                        last = mm(out, w_lo[:, k, ch], a_hi[:, k], start=False, stop=final and ch % 2 == 1)
                    last.then_inc(s_split, 1)

                def v1(r, first, last):
                    for j in range(STRIDE):
                        v_block(r, j, 0, False)
                        gate_group(base + HALF + r * STRIDE + j, j, False)

                rounds(pe, HALF // STRIDE, v1)

                def v2(r, first, last):
                    for j in range(STRIDE):
                        v_block(r, j, 1, last and j == STRIDE - 1)

                rounds(pe, HALF // STRIDE, v2)

            DONE_BY_X = {"peer_q0": 8, "w_kv": 8, "attn_q": 8, "peer_q1": 16}
            ring0 = xT[:, 0:2].rearrange("p a b -> p (a b)")
            peer(0)

            for ch in range(KC):
                sum_squares(2, ch)
            e0 = PROJ["w_kv"] - 8

            def rotate(m):
                if m == 0:
                    pe.wait_ge(s_attin, 80)
                pe.wait_ge(s_evac, e0 + (m + 1 if m < 2 else m + 3))
                if m:
                    pe.wait_ge(s_rope, m)
                src = kraw[:, m] if m < 2 else qraw[:, m - 2]
                mm(bank[4][:, 0:T], rot, src, start=True, stop=True).then_inc(s_rmm, 1)

            for m in range(4):
                arrived("w_kv", m)
                if m >= 2:
                    pe.wait_ge(s_evac, e0 + m - 1)
                for kc in range(KC):
                    if m == 0:
                        pe.wait_ge(s_h, 16 + kc + 1)
                    if m < 2:
                        last = mm(bank[m % 2][:, 0:T], ring[:, m, kc], hkv[:, kc], start=kc == 0,
                                  stop=kc == KC - 1)
                if m >= 2:
                    for tb in range(TB):
                        for kc in range(KC):
                            last = mm(bank[m % 2][:, tb * P:tb * P + P], hkv[:, kc, tb * P:tb * P + P],
                                      ring[:, m, kc], start=kc == 0, stop=kc == KC - 1)
                last.then_inc(s_plain, 1)
                if m >= 2:
                    rotate(m - 2)

            pe.wait_ge(s_h, 32)
            for i in range(13):
                if i < 8:
                    arrived("attn_q", i)
                    pe.wait_ge(s_evac, e0 + 4 + i - 1)
                    for kc in range(KC):
                        last = mm(bank[i % 2][:, 0:T], ring[:, i % 4, kc], hT[:, kc], start=kc == 0,
                                  stop=kc == KC - 1)
                    last.then_inc(s_plain, 1)
                if 1 <= i <= 8:
                    rotate(i + 1)
                if 3 <= i < 11:
                    s = i - 3
                    kv, tb = s // 2, s % 2
                    pe.wait_ge(s_rope, 2 * kv + 4)
                    if s == 0:
                        pe.wait_ge(s_kdup, 64)
                    else:
                        pe.wait_ge(s_sm, s)
                    keys = slice(0, P) if tb == 0 else slice(0, T)
                    for r in range(2):
                        rows = slice(64 * r, 64 * r + 64)
                        for mh in range(2):
                            c0 = mh * T + (P if tb == 0 else 0)
                            last = mm(bank[2 + r][:, c0:mh * T + T], qrot[rows, 2 * kv + mh, tb * P:tb * P + P],
                                      kdup[rows, kv, keys], start=True, stop=True)
                    last.then_inc(s_s, 1)
                if i >= 5:
                    s = i - 5
                    kv, tb = s // 2, s % 2
                    n = transposed(s)
                    kbs = range(1 - tb, 2)
                    pe.wait_ge(s_pn, s + 1)
                    if n:
                        pe.wait_ge(s_ptev, n)
                    for kb in kbs:
                        for head in range(4):
                            last = nc.tensor.transpose(
                                bank[6 + kb][:, head * P:head * P + P],
                                s_sb[s % 3][:, head // 2, head % 2, kb * P:kb * P + P], ident[:])
                        last.then_inc(s_pt, 1)
                    pe.wait_ge(s_ptev, n + len(kbs))
                    if s:
                        pe.wait_ge(s_oev, s)
                    for r in range(2):
                        for kb in kbs:
                            vb = kb if tb == 1 else 0
                            last = mm(bank[5][64 * r:64 * r + 64, 0:T], vN[:, vb, kv * 64:kv * 64 + 64],
                                      pT[s % 2][:, kb, 2 * r:2 * r + 2].rearrange("p a b -> p (a b)"),
                                      start=kb == kbs[0], stop=kb == kbs[-1])
                    last.then_inc(s_o, 1)
            pe.wait_ge(s_oev, 8)
            project_x("w_o", oT, 16, 3)
            peer(1)
            for ch in range(KC):
                sum_squares(4, ch)


_INS = ["x_t", "c_row_d", "b_cond", "norms", "ident_d", "iota_d", "time_d", "w_cond0", "w_cond", "w_in", "w_glu", "w_out",
        "s5_lam", "s5_b", "s5_c", "s5_d", "b_glu", "peer_wq", "keys_d", "u_tab", "v_tab", "w_kv", "attn_wq",
        "w_o", "sinks_d", "pos_d", "masks_d", "rot_d", "freq_d"]


def lay_out(x, c, positions, w_cond, b_cond, norm_mix, norm_ffn, s5_w_in, s5_a_re, s5_a_im, s5_log_dt,
            s5_b_re, s5_b_im, s5_c_re, s5_c_im, s5_d, s5_w_glu, s5_b_glu, s5_w_out, kv_norm, w_kv, attn_w_q,
            attn_sinks, attn_w_o, peer_w_q, peer_sub_keys, peer_u, peer_v, final_norm):
    f = np.float32

    def blocks(w):
        n = w.shape[-1] // P
        return np.ascontiguousarray(w.reshape(KC, P, n, P).transpose(2, 1, 0, 3)).reshape(n, P, D)

    def cols(v):
        return np.ascontiguousarray(v.reshape(-1, P).T)

    def pair(a):
        return a.reshape(PAIRS, 2, 64).transpose(1, 2, 0).reshape(P, PAIRS)

    def pad(a):
        out = np.zeros((2, 64, PAIRS, 2, 16), f)
        a = a.reshape(PAIRS, 2, 64, 16)
        for g in range(2):
            out[g, :, :, g, :] = a[:, g].transpose(1, 0, 2)
        return out.reshape(P, PAIRS, 32)

    keys = np.zeros((2, 2, 64, HEADS, 2, P), f)
    for half in range(2):
        keys[:, half, :, :, half, :] = peer_sub_keys[:, :, half].transpose(0, 3, 1, 2)
    qi = np.arange(P)[:, None]
    kj = np.arange(P)[None, :]
    masks = np.concatenate([np.where(kj > qi, 0.0, NEG), np.where(kj <= qi, 0.0, NEG)], axis=1).astype(f)
    rot = np.zeros((P, P), f)
    for h in range(2):
        for i in range(32):
            rot[64 * h + 32 + i, 64 * h + i] = -1.0
            rot[64 * h + i, 64 * h + 32 + i] = 1.0
    inv_freq = (f(10000.0) ** (-np.arange(0, 64, 2, dtype=f) / f(64))).astype(f)
    order = list(COND_AT)
    cond_rows = w_cond.T.reshape(16, KC, P, D)[order].reshape(P, P, D)
    log_dt = np.broadcast_to(s5_log_dt[0][:, None], (64, 64))
    return {
        "x_t": np.ascontiguousarray(x[0].T.reshape(KC, P, T).transpose(1, 0, 2)),
        "c_row_d": np.ascontiguousarray(np.broadcast_to(c[0], (P, D))),
        "b_cond": np.ascontiguousarray(cols(b_cond).reshape(P, 16, KC)[:, order].reshape(P, P)),
        "norms": np.ascontiguousarray(np.stack([cols(v) for v in (norm_mix[0], norm_ffn[0], kv_norm, norm_mix[1],
                                                                 norm_ffn[1], final_norm)], axis=1)),
        "ident_d": np.eye(P, dtype=f),
        "iota_d": np.ascontiguousarray(np.broadcast_to(np.arange(P, dtype=f), (P, P))),
        "time_d": np.ascontiguousarray(np.broadcast_to(np.arange(T, dtype=f), (P, T))),
        "w_cond0": np.ascontiguousarray(cond_rows[0:16]),
        "w_cond": np.ascontiguousarray(cond_rows[16:]), "w_in": blocks(s5_w_in[0]), "w_glu": blocks(s5_w_glu[0]),
        "w_out": blocks(s5_w_out[0]),
        "s5_lam": np.ascontiguousarray(np.stack([pair(s5_a_re[0]), pair(s5_a_im[0]), pair(log_dt)], axis=1)),
        "s5_b": np.ascontiguousarray(np.stack([pad(s5_b_re[0]), pad(s5_b_im[0])], axis=1)),
        "s5_c": np.ascontiguousarray(np.stack([pad(s5_c_re[0].transpose(0, 2, 1)),
                                               pad(s5_c_im[0].transpose(0, 2, 1))], axis=1)),
        "s5_d": cols(s5_d[0].reshape(-1)), "b_glu": cols(s5_b_glu[0]),
        "peer_wq": np.stack([blocks(peer_w_q[i]) for i in range(2)]),
        "keys_d": keys.reshape(2, P, HEADS, 2 * P),
        "u_tab": np.ascontiguousarray(peer_u.reshape(2, EB, P, KC, P).transpose(0, 1, 4, 3, 2)).reshape(2, EB, P, D),
        "v_tab": peer_v.reshape(2, EB, P, D),
        "w_kv": blocks(w_kv), "attn_wq": blocks(attn_w_q[0]), "w_o": blocks(attn_w_o[0]),
        "sinks_d": np.ascontiguousarray(np.broadcast_to(
            attn_sinks[0].reshape(4, 2, 2).transpose(0, 2, 1).reshape(1, 4, 4), (P, 4, 4))),
        "pos_d": np.ascontiguousarray(np.broadcast_to(positions[0][None, :], (P, T))),
        "masks_d": masks, "rot_d": rot,
        "freq_d": np.ascontiguousarray(np.tile(inv_freq, 4)[:, None]),
    }


def kernel(**inputs):
    import concourse.bacc as bacc
    from concourse.bass_utils import run_bass_kernel_spmd

    arrays = lay_out(**{k: np.asarray(a) for k, a in inputs.items()})
    nc = bacc.Bacc("TRN2", target_bir_lowering=False, num_devices=1, dynamic_dma_scratch_size=1024)
    args = [nc.dram_tensor(n, arrays[n].shape, mybir.dt.from_np(arrays[n].dtype), kind="ExternalInput").ap()
            for n in _INS]
    out = nc.dram_tensor("out_t", (P, KC, T), F32, kind="ExternalOutput").ap()
    build(nc, *args, out)
    r = run_bass_kernel_spmd(nc, [arrays], core_ids=[0])
    got = r.results[0]["out_t"]
    return np.ascontiguousarray(got.transpose(2, 1, 0).reshape(1, T, D))
```

```python
from contextlib import ExitStack

import concourse.bass as bass
from concourse import mybir
import numpy as np

F32 = mybir.dt.float32
F32R = mybir.dt.float32r
BF16 = mybir.dt.bfloat16
I32 = mybir.dt.int32
U32 = mybir.dt.uint32
ALU = mybir.AluOpType
ACT = mybir.ActivationFunctionType
AX = mybir.AxisListType

P = 128
D = 1024
KC = D // P
T = 256
TB = T // P
EB = 128
HALF = EB // 2
HEADS = 8
TOPK = 16
PAIRS = 32
SLOTS = 4
STRIDE = 8
TWO_PI = 6.283185307179586
MAGIC = 12582912.0
MAGIC15 = 12582912.0 / 32768.0
NEG = -1e30

STREAM = [("w_in", 8, 0), ("w_glu", 8, 1), ("w_out", 8, 1),
          ("peer_q0", 8, 1), ("u0", 128, 1), ("v0", 128, 1),
          ("w_kv", 4, 1), ("attn_q", 8, 1), ("w_o", 8, 1),
          ("peer_q1", 8, 1), ("u1", 128, 1), ("v1", 128, 1)]


COND_GROUPS = [(0, 1), (2, 3, 4), (13, 8), (5, 6, 7, 12), (9, 10), (11, 14, 15)]
PE_COLS = 10
FIRST_COLS = 22
COND_AT = {}
for _group in COND_GROUPS:
    for _n in _group:
        COND_AT[_n] = len(COND_AT)
COND_U = [40 - FIRST_COLS, 104 - FIRST_COLS]
COND_V1 = COND_U[0] + 14
COND_V2 = [COND_V1 + 18, COND_U[1] + 14]
COND_FIRST = [sum(len(g) for g in COND_GROUPS[:k]) * KC for k in range(len(COND_GROUPS) + 1)]


def positions_in_stream():
    at, n, plain, split = {}, 0, 0, 0
    for name, count, is_split in STREAM:
        at[name] = (n, plain, split)
        n += count
        plain += 0 if is_split else count
        split += count if is_split else 0
    return at


AT = positions_in_stream()


class Steps:

    def __init__(self, eng, sem):
        self.eng, self.sem, self.n = eng, sem, 0

    def add(self, ins):
        ins.then_inc(self.sem, 1)
        self.n += 1

    def sync(self):
        self.eng.wait_ge(self.sem, self.n)


def middle(eng, a, b, body):
    with eng.Fori(0, (b - a) // 2) as r:
        for k in range(2):
            body(r * 2 + (a + k), False, False)
    if (b - a) % 2:
        body(b - 1, False, False)


def rounds(eng, n, body):
    body(0, True, False)
    middle(eng, 1, n - 1, body)
    body(n - 1, False, True)


def build(nc, x_t, c_col_d, c_row_d, b_cond, norms, ident_d, iota_d, time_d, w_cond0, w_cond, w_in, w_glu, w_out,
          s5_lam, s5_b, s5_c, s5_d, b_glu, peer_wq, keys_d, u_tab, v_tab,
          w_kv, attn_wq, w_o, sinks_d, pos_d, masks_d, rot_d, freq_d, out_t):
    ctx = ExitStack()
    with ctx:
        def sb(name, shape, dt=F32, c=ctx):
            return c.enter_context(nc.sbuf_tensor(name, shape, dt))

        def sem(name):
            return ctx.enter_context(nc.semaphore(name))

        xT = sb("xT", [P, KC, T])
        ident = sb("ident", [P, P])
        ones = sb("ones", [P, P])
        zeros = sb("zeros", [P, P])
        iota = sb("iota", [P, P])
        cond = sb("cond", [P, P])
        bcond = sb("bcond", [P, P])
        norm_sb = sb("norm_sb", [P, 6, KC])
        gs = sb("gs", [P, 6, KC])
        c_row = sb("c_row", [P, D])
        c_col = sb("c_col", [P, KC])
        cring = sb("cring", [P, 2, D])
        eps_sb = sb("eps_sb", [P, 3])
        bglu = sb("bglu", [P, KC])
        warm = sb("warm", [P, 1])
        over = ExitStack()
        sb("below_hq", [P, 8192], c=over)
        hq_hi = sb("hq_hi", [P, KC, T], F32R, c=over)
        hq_lo = sb("hq_lo", [P, KC, T], F32R, c=over)
        sb("below_gl", [P, 25600 - 12288], c=over)
        gl_hi = sb("gl_hi", [P, KC, T], F32R, c=over)
        gl_lo = sb("gl_lo", [P, KC, T], F32R, c=over)
        over.close()
        big = sb("big", [P, EB * T])
        ring = sb("ring", [P, SLOTS, KC, P])
        HB = big[:, :].rearrange("p (i t) -> p i t", t=T)

        def area(at, *shape, dt=None):
            n = 1
            for s in shape:
                n *= s
            v = big[:, at:at + n]
            if dt is not None:
                v = v.bitcast(dt)
            if len(shape) == 2:
                return v.rearrange("p (a b) -> p a b", a=shape[0])
            if len(shape) == 3:
                return v.rearrange("p (a b c) -> p a b c", a=shape[0], b=shape[1])
            if len(shape) == 4:
                return v.rearrange("p (a b c d) -> p a b c d", a=shape[0], b=shape[1], c=shape[2])
            return v

        sq = area(0, KC, T)
        std = area(2048, T)
        rstd = area(2304, T)
        hT = area(16384, KC, T)
        cond0 = [area(at, D) for at in (16384, 17408, 18432, 19456, 29696, 30720)]

        def first_slot(i):
            return i % 4 if i < PE_COLS else 4 + (i - PE_COLS) % 2

        def first_use(i):
            return i // 4 + 1 if i < PE_COLS else (i - PE_COLS) // 2 + 1
        cosT = area(0, PAIRS, T)
        sinT = area(8192, PAIRS, T)
        uT = area(18432, KC, T)
        bbt = area(20480, KC, 2, P)
        c_re = area(22528, PAIRS, 32)
        c_im = area(23552, PAIRS, 32)
        c_nre = area(24576, PAIRS, 32)
        b_re = area(25600, PAIRS, 32)
        b_im = area(26624, PAIRS, 32)
        bb_re = area(27648, PAIRS, 32)
        bb_im = area(28672, PAIRS, 32)
        yT = area(29696, KC, T)
        gl = yT
        y2 = area(16384, KC, T)
        sig = area(18432, KC, T)
        SC = [area(18432, HEADS, 2, P), area(20480, HEADS, 2, P)]
        CAND = area(22528, HEADS, TOPK, TOPK)
        EQ = area(24576, HEADS, TOPK, TOPK)
        KEYS = area(26624, HEADS, 2 * P)
        qT = area(28672, KC, T)
        r_at = 30720
        v_top = area(r_at, HEADS, 2, TOPK)
        ix_u = area(r_at + 256, HEADS, 2, TOPK, dt=U32)
        ix_f = area(r_at + 512, HEADS, 2, TOPK)
        t_top = area(r_at + 768, HEADS, TOPK)
        pos_u = area(r_at + 896, HEADS, TOPK, dt=U32)
        ab_u = area(r_at + 1024, 2, HEADS, TOPK, dt=U32)
        ab_f = area(r_at + 1280, 2, HEADS, TOPK)
        route = [area(r_at + 1536, 3, HEADS, TOPK), sb("route1", [P, 3, HEADS, TOPK])]
        gsum = sb("gsum", [P, 2, HEADS])
        vT = area(12288, 2, T)
        hkv = area(4096, KC, T)
        rcos = area(6144, T)
        rsin = area(6400, T)
        rtmp = area(6656, 4, T)
        pos_i = area(7680, T, dt=I32)
        qraw = area(18432, KC, T)
        qrot = area(20480, KC, T)
        kraw = area(22528, 2, T)
        krot = area(23040, 2, T)
        kdup = area(23552, 4, T)
        vN = area(24576, TB, T)
        s_sb = [area(at, 2, 2, T) for at in (27136, 28160, 2560)]
        pT = [area(29184, 2, 4, P), area(30208, 2, 4, P)]
        masks = area(31232, T)
        rot = area(31488, P)
        sinks = area(31616, 4, 4)
        freq = area(31632, 1)
        rowm, nrowm, rsum, esink = ([area(31648 + 8 * n + 4 * k, 4) for k in range(2)] for n in range(4))
        ropet = area(31744, 2, T)

        s5_mem = ExitStack()
        lam = sb("lam", [P, 3, PAIRS], c=s5_mem)
        dcol = sb("dcol", [P, KC], c=s5_mem)
        tt = sb("tt", [P, T], c=s5_mem)
        sm = sb("sm", [P, 24, PAIRS], c=s5_mem)
        ang = sb("ang", [P, 4, T], c=s5_mem)
        bu = sb("bu", [P, 2, 2, T], c=s5_mem)
        m1 = sb("m1", [P, 2, 2, T], c=s5_mem)
        m2 = sb("m2", [P, 2, 2, T], c=s5_mem)
        wz = sb("wz", [P, 2, 2, T], c=s5_mem)
        zz = sb("zz", [P, 2, 2, T], c=s5_mem)
        p1 = sb("p1", [P, 2, 2, T], c=s5_mem)
        p2 = sb("p2", [P, 2, 2, T], c=s5_mem)
        bbtmp = sb("bbtmp", [P, PAIRS, 32], c=s5_mem)
        s5_mem.close()
        flat4 = "p a b t -> p (a b) t"
        NORM_MEM = [([bu[:].rearrange(flat4), m1[:].rearrange(flat4)], zz[:, 0, 0], p1[:, 0, 0])] + \
            [([sq[:, 0:4], sq[:, 4:8]], std, rstd)] * 4
        h_hi = sb("h_hi", [P, KC, T], F32R)
        h_lo = sb("h_lo", [P, KC, T], F32R)
        w_hi = sb("w_hi", [P, 2, KC, P], F32R)
        w_lo = sb("w_lo", [P, 2, KC, P], F32R)
        a_hi = sb("a_hi", [P, 2, T], F32R)
        a_lo = sb("a_lo", [P, 2, T], F32R)
        eq_a = sb("eq_a", [P, 2, 4, HALF], BF16)
        one_g = sb("one_g", [P, 2, 3, 4, HALF], BF16)
        one_b = sb("one_b", [P, 2, 4, P], BF16)
        i0T = sb("i0T", [P, T])
        i1T = sb("i1T", [P, T])
        g_rest = sb("g_rest", [P, T])
        g_part = sb("g_part", [P, 3, T], BF16)

        bank = [ctx.enter_context(nc.psum_tensor(f"bank{i}", [P, 512], F32)) for i in range(8)]

        s_const = sem("s_const")
        s_ccol = sem("s_ccol")
        s_crow = sem("s_crow")
        s_lam = sem("s_lam")
        s_tt = sem("s_tt")
        s_disc = sem("s_disc")
        s_bbp = sem("s_bbp")
        s_s5in = sem("s_s5in")
        s_slot = [sem(f"s_slot{i}") for i in range(SLOTS)]
        s_plain = sem("s_plain")
        s_hi = sem("s_hi")
        s_lo = sem("s_lo")
        s_split = sem("s_split")
        s_evac = sem("s_evac")
        s_dve = sem("s_dve")
        s_act = sem("s_act")
        s_ones = sem("s_ones")
        s_silu = sem("s_silu")
        s_c0 = [sem(f"s_c0{i}") for i in range(6)]
        s_cin = [sem(f"s_cin{i}") for i in range(2)]
        s_cpe = sem("s_cpe")
        s_cdone = sem("s_cdone")
        s_sq = sem("s_sq")
        s_ms = sem("s_ms")
        s_std = sem("s_std")
        s_hn = sem("s_hn")
        s_h = sem("s_h")
        s_x = sem("s_x")
        s_turns = sem("s_turns")
        s_trh = sem("s_trh")
        s_angc = sem("s_angc")
        s_angd = sem("s_angd")
        s_ang = sem("s_ang")
        s_wz = sem("s_wz")
        s_trig = sem("s_trig")
        s_trig0 = sem("s_trig0")
        s_rho = sem("s_rho")
        s_cneg = sem("s_cneg")
        s_bb = sem("s_bb")
        s_bbt = sem("s_bbt")
        s_bbev = sem("s_bbev")
        s_bu = sem("s_bu")
        s_buev = sem("s_buev")
        s_m1 = sem("s_m1")
        s_m2 = sem("s_m2")
        s_z = sem("s_z")
        s_p1 = sem("s_p1")
        s_p2 = sem("s_p2")
        s_y = sem("s_y")
        s_yev = sem("s_yev")
        s_gl = sem("s_gl")
        s_gelu = sem("s_gelu")
        s_y2 = sem("s_y2")
        s_y2hi = sem("s_y2hi")
        s_keys = sem("s_keys")
        s_hlo = sem("s_hlo")
        s_sc = sem("s_sc")
        s_scev = sem("s_scev")
        s_gsub = sem("s_gsub")
        s_gexp = sem("s_gexp")
        s_route = sem("s_route")
        s_rt = sem("s_rt")
        s_rtev = sem("s_rtev")
        s_eqa = sem("s_eqa")
        s_oneb = sem("s_oneb")
        s_onea = sem("s_onea")
        s_gmm = sem("s_gmm")
        s_gev = sem("s_gev")
        s_ahi = sem("s_ahi")
        s_alo = sem("s_alo")
        s_attin = sem("s_attin")
        s_rang = sem("s_rang")
        s_rtrig = sem("s_rtrig")
        s_rmm = sem("s_rmm")
        s_rope = sem("s_rope")
        s_kdup = sem("s_kdup")
        s_s = sem("s_s")
        s_sm = sem("s_sm")
        s_p = sem("s_p")
        s_pn = sem("s_pn")
        s_pt = sem("s_pt")
        s_ptev = sem("s_ptev")
        s_o = sem("s_o")
        s_vt = sem("s_vt")
        s_vtev = sem("s_vtev")
        s_oev = sem("s_oev")
        s_olo = sem("s_olo")
        s_out = sem("s_out")

        SOURCE = {"w_in": w_in, "w_glu": w_glu, "w_out": w_out, "w_kv": w_kv, "attn_q": attn_wq,
                  "w_o": w_o, "peer_q0": peer_wq[0], "peer_q1": peer_wq[1],
                  "u0": u_tab[0], "v0": v_tab[0], "u1": u_tab[1], "v1": v_tab[1]}
        SCORE_BANKS = [(2, 3, 4, 5), (6, 7, 2, 3)]
        PROJ = {}
        made = 0
        for name, count, _ in STREAM:
            if name[0] != "v":
                PROJ[name] = made
                made += count

        LOW_AT = {name: KC * i for i, name in enumerate(("gl", "y2", "ffn0", "kv", "mix1", "ffn1"))}
        MIX0, FFN0, KVN, MIX1, FFN1, FINAL = range(6)
        SCALE = [1, 4, 13, 7, 10, 15]
        SHIFT = [0, 3, 12, 6, 9, 14]

        def vec(n, ch):
            return cond[:, COND_AT[n] * KC + ch:COND_AT[n] * KC + ch + 1]

        def transposed(s):
            return s // 2 * 3 + s % 2

        block = ctx.enter_context(nc.Block())

        @block.sync
        def _(sp):
            sp.dma_start(lam[:], s5_lam).then_inc(s_lam, 16)
            sp.dma_start(c_col[:], c_col_d).then_inc(s_ccol, 16)
            sp.dma_start(xT[:], x_t).then_inc(s_const, 16)

            def load_first(i):
                k = first_slot(i)
                if first_use(i) > 1:
                    sp.wait_ge(*((s_cpe, i - 3) if i < PE_COLS else (s_cdone, i - PE_COLS - 1)))
                sp.dma_start(cond0[k], w_cond0[i]).then_inc(s_c0[k], 16)

            for i in (*range(4), PE_COLS, PE_COLS + 1, *range(4, PE_COLS), *range(PE_COLS + 2, 16)):
                load_first(i)
            prev = None
            for name, count, is_split in STREAM:
                n0, plain0, split0 = AT[name]
                src = SOURCE[name]

                def load(r, j, freed, by_split):
                    if freed is not None:
                        sp.wait_ge(s_lo if by_split else s_plain, freed)
                    blk = src[r * SLOTS + j] if isinstance(r, int) else \
                        src[bass.ds(r * SLOTS + j, 1)].rearrange("a p n -> p (a n)")
                    sp.dma_start(ring[:, j].rearrange("p a b -> p (a b)"), blk).then_inc(s_slot[j], 16)

                for j in range(SLOTS):
                    if prev is None:
                        load(0, j, None, 0)
                    else:
                        before = split0 if prev[2] else plain0
                        load(0, j, before - SLOTS + j + 1, prev[2])
                if prev is None:
                    for i in range(16, FIRST_COLS):
                        load_first(i)
                first = split0 if is_split else plain0
                if count // SLOTS > 2:
                    with sp.Fori(1, count // SLOTS) as r:
                        for j in range(SLOTS):
                            load(r, j, r * SLOTS + (first - SLOTS + j + 1), is_split)
                else:
                    for r in range(1, count // SLOTS):
                        for j in range(SLOTS):
                            load(r, j, first + (r - 1) * SLOTS + j + 1, is_split)
                prev = (name, count, is_split)
            sp.wait_ge(s_h, 8 * 6)
            sp.dma_start(out_t, hT).then_inc(s_out, 16)
            sp.wait_ge(s_out, 16)

        @block.gpsimd
        def _(pool):
            nc.gpsimd.memset(ones[:], 1.0).then_inc(s_ones, 1)
            nc.gpsimd.memset(zeros[:], 0.0).then_inc(s_ones, 1)
            nc.gpsimd.memset(eps_sb[:, 0:1], TWO_PI / 4).then_inc(s_ones, 1)
            nc.gpsimd.memset(eps_sb[:, 1:2], MAGIC).then_inc(s_ones, 1)
            nc.gpsimd.memset(eps_sb[:, 2:3], 1e-6).then_inc(s_ones, 1)

            pool.wait_ge(s_rho, 3)
            pool.wait_ge(s_tt, 16)
            for i in range(0, PAIRS, 4):
                nc.gpsimd.tensor_tensor(cosT[:, i:i + 4], tt[:].unsqueeze(1).broadcast_to([P, 4, T]),
                                        sm[:, 13, i:i + 4].unsqueeze(2).broadcast_to([P, 4, T]), ALU.mult)\
                    .then_inc(s_trh, 1)

            pool.wait_ge(s_s5in, 96)
            pool.wait_ge(s_disc, 2)
            crb = sm[:, 19].unsqueeze(2).broadcast_to([P, PAIRS, 32])
            cib = sm[:, 20].unsqueeze(2).broadcast_to([P, PAIRS, 32])
            nc.gpsimd.tensor_tensor(bb_re, b_re, crb, ALU.mult).then_inc(s_bbp, 1)
            nc.gpsimd.tensor_tensor(bbtmp[:], b_im, cib, ALU.mult).then_inc(s_bbp, 1)
            pool.wait_ge(s_bbp, 2)
            nc.gpsimd.tensor_tensor(bb_re, bb_re, bbtmp[:], ALU.subtract).then_inc(s_bb, 1)
            nc.gpsimd.tensor_tensor(bb_im, b_im, crb, ALU.mult).then_inc(s_bbp, 1)
            pool.wait_ge(s_bb, 1)
            nc.gpsimd.tensor_tensor(bbtmp[:], b_re, cib, ALU.mult).then_inc(s_bbp, 1)
            pool.wait_ge(s_bbp, 4)
            nc.gpsimd.tensor_tensor(bb_im, bb_im, bbtmp[:], ALU.add).then_inc(s_bb, 1)

            def bc(table, pr):
                return table[:, pr:pr + 1, :].broadcast_to([P, 2, T])

            def m2_of(pr, k, first2):
                pool.wait_ge(s_buev, pr + 1)
                if not first2:
                    pool.wait_ge(s_wz, 2 * (pr - 1))
                nc.gpsimd.tensor_tensor(m2[:, k], bu[:, k], bc(sinT, pr), ALU.mult).then_inc(s_m2, 1)

            pool.wait_ge(s_trig, 6)
            m2_of(0, 0, True)

            def s5_round(ch, first, last):
                for q in range(4):
                    pr = ch * 4 + q
                    if not (last and q == 3):
                        m2_of(pr + 1, (q + 1) % 2, first and q == 0)
                    pool.wait_ge(s_z, pr + 1)
                    if not (first and q < 2):
                        pool.wait_ge(s_y, pr - 1)
                    nc.gpsimd.tensor_tensor(p2[:, q % 2], zz[:, q % 2], bc(sinT, pr), ALU.mult)\
                        .then_inc(s_p2, 1)

            for ch in range(KC):
                if ch == 1:
                    pool.wait_ge(s_trig, 8)
                s5_round(ch, ch == 0, ch == KC - 1)

            def lows(*names):
                for name in names:
                    for m in range(dict((n, c) for n, c, _ in STREAM)[name]):
                        n, b = AT[name][0] + m, AT[name][2] + m
                        pool.wait_ge(s_hi, b + 1)
                        nc.gpsimd.tensor_tensor(w_lo[:, b % 2], ring[:, n % 4], w_hi[:, b % 2].bitcast(F32),
                                                ALU.subtract).then_inc(s_lo, 1)

            lows("w_glu", "w_out")
            for layer in range(2):
                if layer == 1:
                    pool.wait_ge(s_lo, AT["w_kv"][2])
                    lows("w_kv", "attn_q", "w_o")
                lows(f"peer_q{layer}")
                su = AT[f"u{layer}"][2]
                with pool.Fori(0, HALF // SLOTS) as r:
                    for j in range(SLOTS):
                        pool.wait_ge(s_hi, r * SLOTS + (su + j + 1))
                        nc.gpsimd.tensor_tensor(w_lo[:, j % 2], ring[:, j], w_hi[:, j % 2].bitcast(F32),
                                                ALU.subtract).then_inc(s_lo, 1)
                pool.wait_ge(s_hi, su + HALF + 1)
                nc.gpsimd.tensor_tensor(w_lo[:, 0], ring[:, 0], w_hi[:, 0].bitcast(F32),
                                        ALU.subtract).then_inc(s_lo, 1)

                def gates(group, k, g, first2):
                    pool.wait_ge(s_eqa, group + 1)
                    if not first2:
                        pool.wait_ge(s_gmm, group - 1)
                    tok = g_part[:, :, g * 4:g * 4 + 4] if isinstance(g, int) else \
                        g_part[:, :, bass.ds(g * 4, 4)]
                    nc.gpsimd.tensor_tensor(one_g[:, k], eq_a[:, k].unsqueeze(1).broadcast_to([P, 3, 4, HALF]),
                                            tok.unsqueeze(3).broadcast_to([P, 3, 4, HALF]), ALU.mult)\
                        .then_inc(s_onea, 1)

                base = 2 * HALF * layer

                def u2(r, first, last):
                    for j in range(SLOTS):
                        g = r * SLOTS + j
                        gates(base + g, j % 2, g, first and j < 2 and layer == 0)

                rounds(pool, HALF // SLOTS, u2)

                def a_low(v, k):
                    pool.wait_ge(s_ahi, EB * layer + v + 1)
                    src = HB[:, v, :] if isinstance(v, int) else HB[:, bass.ds(v, 1), :].rearrange("p a t -> p (a t)")
                    nc.gpsimd.tensor_tensor(a_lo[:, k], src, a_hi[:, k].bitcast(F32), ALU.subtract)\
                        .then_inc(s_alo, 1)

                gates(base + HALF, 0, 0, False)

                def v1(r, first, last):
                    for j in range(SLOTS):
                        g = r * SLOTS + j
                        a_low(g, j % 2)
                        if not (last and j == 3):
                            gates(base + HALF + g + 1, (j + 1) % 2, g + 1, False)

                rounds(pool, HALF // SLOTS, v1)
                with pool.Fori(0, HALF // SLOTS) as r:
                    for j in range(SLOTS):
                        a_low(r * SLOTS + (HALF + j), j % 2)

        @block.scalar
        def _(act):
            act.dma_start(tt[:], time_d).then_inc(s_tt, 16)
            act.dma_start(c_row[:], c_row_d).then_inc(s_crow, 16)
            act.wait_ge(s_lam, 16)
            nc.scalar.activation(sm[:, 0], lam[:, 2], ACT.Exp).then_inc(s_act, 1)
            act.wait_ge(s_rho, 1)
            nc.scalar.activation(sm[:, 2], sm[:, 1], ACT.Exp).then_inc(s_act, 1)
            act.wait_ge(s_ccol, 16)
            nc.scalar.activation(c_col[:], c_col[:], ACT.Silu).then_inc(s_silu, 1)
            act.wait_ge(s_ones, 5)
            act.wait_ge(s_rho, 2)
            nc.scalar.activation(sm[:, 4], sm[:, 3], ACT.Sin, scale=TWO_PI).then_inc(s_trig0, 1)
            nc.scalar.activation(sm[:, 5], sm[:, 3], ACT.Abs).then_inc(s_act, 1)
            act.wait_ge(s_act, 3)
            nc.scalar.activation(sm[:, 6], sm[:, 5], ACT.Sin, scale=-TWO_PI, bias=eps_sb[:, 0:1])\
                .then_inc(s_trig0, 1)
            for dst, src in ((bcond[:], b_cond), (norm_sb[:], norms), (ident[:], ident_d), (iota[:], iota_d)):
                act.dma_start(dst, src).then_inc(s_const, 16)
            for dst, src in ((b_re, s5_b[:, 0]), (b_im, s5_b[:, 1]), (c_re, s5_c[:, 0]), (c_im, s5_c[:, 1]),
                             (dcol[:], s5_d), (bglu[:], b_glu)):
                act.dma_start(dst, src).then_inc(s_s5in, 16)

            def load_cond(i, k):
                if not (isinstance(i, int) and i < 2):
                    act.wait_ge(s_cdone, i + (FIRST_COLS - PE_COLS - 1))
                blk = w_cond[i] if isinstance(i, int) else \
                    w_cond[bass.ds(i, 1)].rearrange("a p n -> p (a n)")
                act.dma_start(cring[:, k], blk).then_inc(s_cin[k], 16)

            load_cond(0, 0)
            load_cond(1, 1)
            def square(k, ch):
                if ch == KC - 1:
                    nc.scalar.activation(warm[:], eps_sb[:, 2:3], ACT.Sqrt)
                act.wait_ge(s_x, 8 * (k - 1) + ch + 1)
                nc.scalar.activation(sq[:, ch], xT[:, ch], ACT.Square).then_inc(s_sq, 1)

            def root(k):
                act.wait_ge(s_ms, k + 1)
                nc.scalar.activation(NORM_MEM[k][1], bank[6][:, 0:T], ACT.Sqrt, scale=1.0 / D,
                                     bias=eps_sb[:, 2:3]).then_inc(s_std, 1)

            def hi_block(name, m):
                n, b = AT[name][0] + m, AT[name][2] + m
                act.wait_ge(s_slot[n % 4], 16 * (n // 4 + 1))
                if b >= 2:
                    act.wait_ge(s_split, b - 1)
                nc.scalar.copy(w_hi[:, b % 2], ring[:, n % 4]).then_inc(s_hi, 1)

            def shifts(which, dst, n, out=None):
                for ch in range(KC):
                    act.wait_ge(s_hn, 8 * n + ch + 1)
                    nc.scalar.activation((dst if out is None else out)[:, ch], dst[:, ch], ACT.Identity,
                                         bias=vec(SHIFT[which], ch))\
                        .then_inc(s_h, 1)

            def evacuate(name, m, dst):
                act.wait_ge(*((s_split, AT[name][2] + m + 1) if name != "w_in" else (s_plain, m + 1)))
                nc.scalar.copy(dst, bank[m % 2][:, 0:T]).then_inc(s_evac, 1)

            def gelu_of(ch):
                act.wait_ge(s_yev, ch + 1)
                nc.scalar.activation(gl[:, ch], yT[:, ch], ACT.Gelu_apprx_tanh).then_inc(s_gelu, 1)
                act.wait_ge(s_gelu, ch + 1)
                nc.scalar.copy(gl_hi[:, ch], gl[:, ch]).then_inc(s_gl, 1)

            def turns(part):
                for pr in part:
                    nc.scalar.activation(sinT[:, pr], tt[:], ACT.Identity, scale=sm[:, 10, pr:pr + 1],
                                         bias=eps_sb[:, 1:2]).then_inc(s_turns, 1)

            def trig(g):
                act.wait_ge(s_ang, 2 * g + 2)
                part = slice(8 * g, 8 * g + 8)
                nc.scalar.activation(cosT[:, part], sinT[:, part], ACT.Abs).then_inc(s_act, 1)
                act.wait_ge(s_act, 4 + g)
                nc.scalar.activation(cosT[:, part], cosT[:, part], ACT.Sin, scale=-TWO_PI,
                                     bias=eps_sb[:, 0:1]).then_inc(s_trig, 1)
                nc.scalar.activation(sinT[:, part], sinT[:, part], ACT.Sin, scale=TWO_PI).then_inc(s_trig, 1)

            act.wait_ge(s_tt, 16)
            turns(range(0, 8))
            act.wait_ge(s_const, 80)
            for half in range(2):
                nc.scalar.activation(NORM_MEM[0][0][half], xT[:, half * 4:half * 4 + 4], ACT.Square)\
                    .then_inc(s_sq, 1)
            turns(range(8, 16))
            act.wait_ge(s_crow, 16)
            nc.scalar.activation(c_row[:], c_row[:], ACT.Silu).then_inc(s_silu, 1)
            turns(range(16, 24))
            root(0)
            turns(range(24, PAIRS))
            act.wait_ge(s_s5in, 96)
            nc.scalar.mul(c_nre, c_re, -1.0).then_inc(s_cneg, 1)
            nc.scalar.mul(c_im, c_im, -1.0).then_inc(s_cneg, 1)
            trig(0)
            trig(1)
            for ch in range(KC):
                act.wait_ge(s_bbt, ch + 1)
                nc.scalar.copy(bbt[:, ch].rearrange("p a b -> p (a b)"),
                               bank[4 + ch % 2][:, 0:256]).then_inc(s_bbev, 1)
            trig(2)
            shifts(MIX0, hT, 0)
            trig(3)
            evacuate("w_in", 0, uT[:, 0])
            for ch in range(KC):
                for q in range(4):
                    pr = ch * 4 + q
                    if q == 3 and ch < KC - 1:
                        evacuate("w_in", ch + 1, uT[:, ch + 1])
                    act.wait_ge(s_bu, pr + 1)
                    if pr >= 2:
                        act.wait_ge(s_m1, pr - 1)
                        act.wait_ge(s_m2, pr - 1)
                    nc.scalar.copy(bu[:, q % 2].rearrange("p a b -> p (a b)"), bank[2 + q][:, :])\
                        .then_inc(s_buev, 1)
                if ch >= 1:
                    gelu_of(ch - 1)
                if ch in (1, 2):
                    load_cond(ch + 1, (ch + 1) % 2)
            gelu_of(KC - 1)
            hi_block("w_glu", 0)
            hi_block("w_glu", 1)

            def y2_high(m):
                act.wait_ge(s_y2, m + 1)
                nc.scalar.copy(h_hi[:, m], y2[:, m]).then_inc(s_y2hi, 1)

            for m in range(8):
                hi_block(*(("w_glu", m + 2) if m < 6 else ("w_out", m - 6)))
                act.wait_ge(s_split, AT["w_glu"][2] + m + 1)
                nc.scalar.activation(sig[:, m], bank[m % 2][:, 0:T], ACT.Sigmoid, bias=bglu[:, m:m + 1])\
                    .then_inc(s_evac, 1)
                if m:
                    y2_high(m - 1)
                load_cond(4 + m, m % 2)
            y2_high(7)

            def peer(layer):
                act.wait_ge(s_h, 8 * (2 + 3 * layer))
                act.dma_start(KEYS, keys_d[layer]).then_inc(s_keys, 16)
                n0, _, s0 = AT[f"u{layer}"]

                def hi(r, j, off):
                    jj = (j + off) % 4
                    rr = (j + off) // 4
                    act.wait_ge(s_slot[jj], r * 16 + ((n0 // 4 + rr + 1) * 16))
                    act.wait_ge(s_split, r * 4 + (s0 + j + off - 1))
                    nc.scalar.copy(w_hi[:, jj % 2], ring[:, jj]).then_inc(s_hi, 1)

                for m in range(8):
                    if m < 6:
                        hi_block(f"peer_q{layer}", m + 2)
                    evacuate(f"peer_q{layer}", m, qT[:, m])
                    if m >= 6:
                        hi(0, m - 6, 0)
                for tb in range(TB):
                    for b in range(4):
                        act.wait_ge(s_sc, 8 * layer + 4 * tb + b + 1)
                        nc.scalar.copy(SC[tb][:, 2 * b:2 * b + 2], bank[SCORE_BANKS[tb][b]][:, :]
                                       .rearrange("p (a b c) -> p a b c", a=2, b=2)).then_inc(s_scev, 1)

                def exp_gates(tb):
                    act.wait_ge(s_gsub, 2 * layer + tb + 1)
                    dst = route[tb][:, 2]
                    nc.scalar.activation(dst, dst, ACT.Exp).then_inc(s_gexp, 1)

                def gelu(r, j, half):
                    act.wait_ge(s_split, r * 4 + (s0 + half * HALF + j + 1))
                    row = r * 4 + (half * HALF + j)
                    dst = HB[:, row, :] if isinstance(row, int) else \
                        HB[:, bass.ds(row, 1), :].rearrange("p a t -> p (a t)")
                    nc.scalar.activation(dst, bank[j % 2][:, 0:T], ACT.Gelu_apprx_tanh).then_inc(s_evac, 1)

                def u_round(half):
                    def body(r, first, last):
                        for j in range(SLOTS):
                            hi(r + half * (HALF // 4), j, 2)
                            gelu(r, j, half)
                    return body

                n1 = HALF // SLOTS
                middle(act, 0, 10, u_round(0))
                for tb in range(TB):
                    exp_gates(tb)
                c0 = COND_U[layer]
                load_cond(c0 + 1, 1)

                def u_cond_round(r, first, last):
                    for j in range(SLOTS):
                        if j % 2:
                            load_cond(r * 2 + (c0 + 2 - 20 + j // 2), j // 2)
                        hi(r, j, 2)
                        gelu(r, j, 0)

                middle(act, 10, n1, u_cond_round)
                middle(act, 0, n1, u_round(1))

                def a_high(v, k):
                    src = HB[:, v, :] if isinstance(v, int) else HB[:, bass.ds(v, 1), :].rearrange("p a t -> p (a t)")
                    nc.scalar.copy(a_hi[:, k], src).then_inc(s_ahi, 1)

                act.wait_ge(s_gev, 2 * HALF * layer + HALF)
                a_high(0, 0)
                a_high(1, 1)

                def v_round(half, cond_block=None):
                    def body(r, first, last):
                        for j in range(SLOTS):
                            if cond_block is not None and j == 0:
                                load_cond(r * 2 + (cond_block + 1), 1)
                            if cond_block is not None and j == 2:
                                load_cond(r * 2 + (cond_block + 2), 0)
                            final = last and half == 1 and j >= 2
                            if not final:
                                hi(r + (2 + half) * (HALF // 4), j, 2)
                                if half == 0 and last and j == 2:
                                    act.wait_ge(s_gev, 2 * HALF * layer + 2 * HALF)
                                act.wait_ge(s_alo, r * 4 + (EB * layer + half * HALF + j + 1))
                                a_high(r * 4 + (half * HALF + j + 2), j % 2)
                    return body

                if layer == 0:
                    load_cond(COND_V1, 0)
                    v_round(0)(0, True, False)
                    middle(act, 1, 10, v_round(0, COND_V1 - 2))
                    middle(act, 10, n1 - 1, v_round(0))
                    v_round(0)(n1 - 1, False, True)
                    rounds(act, n1, v_round(1, COND_V2[0]))
                else:
                    load_cond(COND_V2[1], 0)
                    rounds(act, n1, v_round(0))
                    middle(act, 0, 4, v_round(1, COND_V2[1]))
                    load_cond(COND_V2[1] + 9, 1)
                    middle(act, 4, n1 - 1, v_round(1))
                    v_round(1)(n1 - 1, False, True)

            for m in range(8):
                if m < 6:
                    hi_block("w_out", m + 2)
                square(1, m)
                if m >= 6:
                    hi_block("peer_q0", m - 6)
                if m < 7:
                    load_cond(12 + m, m % 2)
            root(1)
            shifts(FFN0, hT, 1, h_hi)
            peer(0)

            for m in range(8):
                square(2, m)
            for m in range(2):
                hi_block("w_kv", m)
            for dst, src in ((masks, masks_d), (rot, rot_d), (sinks, sinks_d), (freq, freq_d), (pos_i, pos_d)):
                act.dma_start(dst, src).then_inc(s_attin, 16)
            root(2)
            shifts(KVN, hkv, 2, h_hi)
            for m in range(4):
                hi_block(*(("w_kv", m + 2) if m < 2 else ("attn_q", m - 2)))
                evacuate("w_kv", m, kraw[:, m] if m < 2 else vT[:, m - 2])
                if m == 0:
                    shifts(MIX1, hT, 3, hq_hi)
            act.wait_ge(s_rang, 1)
            nc.scalar.activation(rsin, rtmp[:, 0], ACT.Sin).then_inc(s_rtrig, 1)
            nc.scalar.activation(rtmp[:, 1], rtmp[:, 0], ACT.Abs).then_inc(s_act, 1)
            act.wait_ge(s_act, 8)
            nc.scalar.activation(rcos, rtmp[:, 1], ACT.Sin, scale=-1.0, bias=eps_sb[:, 0:1]).then_inc(s_rtrig, 1)
            for i in range(13):
                if i < 8:
                    hi_block(*(("attn_q", i + 2) if i < 6 else ("w_o", i - 6)))
                    evacuate("attn_q", i, qraw[:, i])
                if i == 1:
                    act.wait_ge(s_vt, 1)
                    nc.scalar.copy(vN.rearrange("p b (m d) -> p m b d", m=2),
                                   bank[7][:, :].rearrange("p (m b d) -> p m b d", m=2, b=2)).then_inc(s_vtev, 1)
                    act.wait_ge(s_rope, 2)
                    for src in range(2):
                        for dst in range(2):
                            act.dma_start(kdup[64 * dst:64 * dst + 64, src::2, :],
                                          krot[64 * src:64 * src + 64, :, :]).then_inc(s_kdup, 16)
                if i >= 5:
                    s = i - 5
                    kv, tb = s // 2, s % 2
                    for n, kb in enumerate(range(1 - tb, 2)):
                        act.wait_ge(s_pt, transposed(s) + n + 1)
                        nc.scalar.copy(pT[s % 2][:, kb], bank[6 + kb][:, :]
                                       .rearrange("p (a b) -> p a b", a=4)).then_inc(s_ptev, 1)
                    act.wait_ge(s_o, s + 1)
                    nc.scalar.copy(h_hi[:, 2 * kv:2 * kv + 2, tb * P:tb * P + P],
                                   bank[5][:, 0:T].rearrange("p (a b) -> p a b", a=2)).then_inc(s_oev, 1)
                if 3 <= i < 11:
                    s = i - 3
                    k0, nk = (P, P) if s % 2 == 0 else (0, T)
                    act.wait_ge(s_sm, s + 1)
                    for r in range(2):
                        for mm in range(2):
                            head = 2 * r + mm
                            view = s_sb[s % 3][:, r, mm, k0:k0 + nk]
                            nc.scalar.activation(view, view, ACT.Exp, bias=nrowm[s % 2][:, head:head + 1],
                                                 accum_out=rsum[s % 2][:, head:head + 1]).then_inc(s_p, 1)
                    nc.scalar.activation(esink[s % 2], esink[s % 2], ACT.Exp).then_inc(s_p, 1)
            for m in range(8):
                if m < 6:
                    hi_block("w_o", m + 2)
                square(3, m)
                if m >= 6:
                    hi_block("peer_q1", m - 6)
            root(3)
            shifts(FFN1, hT, 4, h_hi)
            peer(1)
            for m in range(8):
                square(4, m)
            root(4)
            shifts(FINAL, hT, 5)

        @block.vector
        def _(dve):
            v = nc.vector
            st = Steps(dve, s_dve)

            def do(ins):
                st.add(ins)
                st.sync()

            def cond_column(col, blk):
                out = cond[:, col:col + 1] if isinstance(col, int) else cond[:, bass.ds(col, 1)]
                v.scalar_tensor_tensor(blk, blk, 1.0, c_row[:], ALU.mult, ALU.mult, accum_out=out)\
                    .then_inc(s_cdone, 1)

            def cond_ring(i, k):
                dve.wait_ge(s_cin[k], i * 8 + (16 - 8 * k))
                cond_column(i + FIRST_COLS, cring[:, k])

            def cond_bias(group):
                dve.wait_ge(s_cdone, COND_FIRST[group + 1] - PE_COLS)
                cols = slice(COND_FIRST[group], COND_FIRST[group + 1])
                do(v.tensor_tensor(cond[:, cols], cond[:, cols], bcond[:, cols], ALU.add))

            def scales(which):
                st.add(v.scalar_tensor_tensor(gs[:, which], cond[:, COND_AT[SCALE[which]] * KC:COND_AT[SCALE[which]] * KC + KC], 1.0,
                                              norm_sb[:, which], ALU.add, ALU.mult))

            def inverse_root(k):
                _, root_k, rstd_k = NORM_MEM[k]
                dve.wait_ge(s_std, k + 1)
                do(v.reciprocal(rstd_k, root_k))

            def stats(k):
                inverse_root(k)

            def normalise(which, dst):
                rstd_k = NORM_MEM[0 if which == MIX0 else 1][2]
                for ch in range(KC):
                    v.scalar_tensor_tensor(dst[:, ch], xT[:, ch], gs[:, which, ch:ch + 1], rstd_k,
                                           ALU.mult, ALU.mult).then_inc(s_hn, 1)

            def low_halves(which, src, hi_, lo_, n):
                for ch in range(KC):
                    dve.wait_ge(s_h, n + ch + 1)
                    v.scalar_tensor_tensor(lo_[:, ch], src[:, ch], vec(SHIFT[which], ch), hi_[:, ch].bitcast(F32),
                                           ALU.add, ALU.subtract).then_inc(s_hlo, 1)

            def residual(name, gate, m):
                dve.wait_ge(s_split, AT[name][2] + m + 1)
                v.scalar_tensor_tensor(xT[:, m], bank[m % 2][:, 0:T], vec(gate, m), xT[:, m],
                                       ALU.mult, ALU.add).then_inc(s_x, 1)

            dve.wait_ge(s_lam, 16)
            dve.wait_ge(s_act, 1)
            a_re, a_im = lam[:, 0], lam[:, 1]
            v.tensor_tensor(sm[:, 1], a_re, sm[:, 0], ALU.mult).then_inc(s_rho, 1)
            theta, th, tl, acc, n, rl, rh = (sm[:, i] for i in range(7, 14))
            t1, t2 = sm[:, 14], sm[:, 15]
            do(v.tensor_tensor(theta, a_im, sm[:, 0], ALU.mult))
            inv = 1.0 / TWO_PI
            i1 = float(np.float32(np.round(inv * 2.0 ** 14) / 2.0 ** 14))
            i2 = float(np.float32(inv - i1))
            do(v.tensor_scalar(t1, theta, 4097.0, None, ALU.mult))
            do(v.tensor_tensor(t2, t1, theta, ALU.subtract))
            do(v.tensor_tensor(th, t1, t2, ALU.subtract))
            do(v.tensor_tensor(tl, theta, th, ALU.subtract))
            st.add(v.tensor_scalar(th, th, i1, None, ALU.mult))
            st.add(v.tensor_scalar(tl, tl, i1, None, ALU.mult))
            do(v.tensor_scalar(t1, theta, i2, None, ALU.mult))
            do(v.tensor_tensor(tl, tl, t1, ALU.add))
            do(v.tensor_tensor(acc, th, tl, ALU.add))
            do(v.tensor_scalar(n, acc, MAGIC, -MAGIC, ALU.add, ALU.add))
            do(v.tensor_tensor(th, th, n, ALU.subtract))
            do(v.tensor_tensor(acc, th, tl, ALU.add))
            v.tensor_scalar(sm[:, 3], acc, 0.49999997, -0.49999997, ALU.min, ALU.max).then_inc(s_rho, 1)
            v.tensor_scalar(rh, acc, MAGIC15, -MAGIC15, ALU.add, ALU.add).then_inc(s_rho, 1)
            dve.wait_ge(s_rho, 3)
            do(v.tensor_tensor(rl, th, rh, ALU.subtract))
            do(v.tensor_tensor(rl, rl, tl, ALU.add))
            mag, lre, lim, den, cr, ci = (sm[:, i] for i in (2, 16, 17, 18, 19, 20))
            dve.wait_ge(s_trig0, 2)
            dve.wait_ge(s_act, 2)
            do(v.tensor_tensor(lre, mag, sm[:, 6], ALU.mult))
            st.add(v.tensor_tensor(lim, mag, sm[:, 4], ALU.mult))
            st.add(v.tensor_tensor(den, a_re, a_re, ALU.mult))
            st.add(v.tensor_tensor(t1, a_im, a_im, ALU.mult))
            do(v.tensor_scalar(lre, lre, -1.0, None, ALU.add))
            do(v.tensor_tensor(den, den, t1, ALU.add))
            do(v.reciprocal(den, den))
            st.add(v.tensor_tensor(cr, lre, a_re, ALU.mult))
            st.add(v.tensor_tensor(t1, lim, a_im, ALU.mult))
            st.add(v.tensor_tensor(ci, lim, a_re, ALU.mult))
            do(v.tensor_tensor(t2, lre, a_im, ALU.mult))
            st.add(v.tensor_tensor(cr, cr, t1, ALU.add))
            do(v.tensor_tensor(ci, ci, t2, ALU.subtract))
            v.tensor_tensor(cr, cr, den, ALU.mult).then_inc(s_disc, 1)
            v.tensor_tensor(ci, ci, den, ALU.mult).then_inc(s_disc, 1)
            for g in range(0, PAIRS, 4):
                dve.wait_ge(s_turns, g + 4)
                dve.wait_ge(s_trh, g // 4 + 1)
                if g:
                    dve.wait_ge(s_angd, g)
                for pr in range(g, g + 4):
                    v.scalar_tensor_tensor(ang[:, pr % 4], sinT[:, pr], -MAGIC, cosT[:, pr], ALU.add,
                                           ALU.subtract).then_inc(s_angc, 1)
                for pr in range(g, g + 4):
                    dve.wait_ge(s_angc, pr + 1)
                    v.scalar_tensor_tensor(sinT[:, pr], tt[:], rl[:, pr:pr + 1], ang[:, pr % 4], ALU.mult,
                                           ALU.subtract).then_inc(s_angd, 1)
                dve.wait_ge(s_angd, g + 4)
                part = sinT[:, g:g + 4]
                v.tensor_scalar(part, part, 0.49999997, -0.49999997, ALU.min, ALU.max).then_inc(s_ang, 1)
                if g == 20:
                    inverse_root(0)
                if g >= 8:
                    i = PE_COLS + g // 4 - 2
                    if g == 8:
                        dve.wait_ge(s_silu, 2)
                    dve.wait_ge(s_c0[first_slot(i)], 16 * first_use(i))
                    cond_column(i, cond0[first_slot(i)])
            dve.wait_ge(s_const, 80)
            dve.wait_ge(s_cpe, PE_COLS)
            dve.wait_ge(s_cdone, 16 - PE_COLS)
            st.add(v.tensor_tensor(cond[:, 0:PE_COLS], bank[7][:, 0:PE_COLS], bcond[:, 0:PE_COLS], ALU.add))
            do(v.tensor_tensor(cond[:, PE_COLS:16], cond[:, PE_COLS:16], bcond[:, PE_COLS:16], ALU.add))
            scales(MIX0)
            st.sync()
            normalise(MIX0, hT)
            def bc(table, pr):
                return table[:, bass.ds(pr, 1), :].broadcast_to([P, 2, T]) if not isinstance(pr, int) \
                    else table[:, pr:pr + 1, :].broadcast_to([P, 2, T])

            def m1_of(pr, k):
                dve.wait_ge(s_buev, pr + 1)
                v.tensor_tensor(m1[:, k], bu[:, k], bc(cosT, pr), ALU.mult).then_inc(s_m1, 1)

            def p1_of(pr, k, first2):
                dve.wait_ge(s_z, pr + 1)
                if not first2:
                    dve.wait_ge(s_y, pr - 1)
                v.tensor_tensor(p1[:, k], zz[:, k], bc(cosT, pr), ALU.mult).then_inc(s_p1, 1)

            def y_of(ch, k):
                dve.wait_ge(s_y, ch * 4 + 4)
                chs = slice(ch, ch + 1) if isinstance(ch, int) else bass.ds(ch, 1)
                flat = "p a t -> p (a t)"
                v.scalar_tensor_tensor(yT[:, chs].rearrange(flat), uT[:, chs].rearrange(flat), dcol[:, chs],
                                       bank[6 + k][:, 0:T], ALU.mult, ALU.add).then_inc(s_yev, 1)

            def gl_low(ch, k):
                dve.wait_ge(s_gl, ch + 1)
                chs = slice(ch, ch + 1) if isinstance(ch, int) else bass.ds(ch, 1)
                v.tensor_tensor(gl_lo[:, chs], gl[:, chs], gl_hi[:, chs].bitcast(F32), ALU.subtract)\
                    .then_inc(s_hlo, 1)

            for i in range(16, FIRST_COLS):
                dve.wait_ge(s_c0[first_slot(i)], 16 * first_use(i))
                cond_column(i, cond0[first_slot(i)])
            for i in range(2):
                cond_ring(i, i)
            dve.wait_ge(s_trig, 6)
            m1_of(0, 0)

            def s5_round(r, first, last):
                for q in range(8):
                    pr = r * 8 + q
                    k = q % 2
                    early = first and q < 2
                    dve.wait_ge(s_m1, pr + 1)
                    dve.wait_ge(s_m2, pr + 1)
                    if not early:
                        dve.wait_ge(s_z, pr - 1)
                    v.tensor_tensor(wz[:, k, 0], m1[:, k, 0], m2[:, k, 1], ALU.add).then_inc(s_wz, 1)
                    v.tensor_tensor(wz[:, k, 1], m1[:, k, 1], m2[:, k, 0], ALU.subtract).then_inc(s_wz, 1)
                    if not (first and q == 0):
                        p1_of(pr - 1, (q + 1) % 2, first and q < 3)
                    if not (last and q == 7):
                        if not (first and q == 0):
                            dve.wait_ge(s_wz, 2 * pr)
                        m1_of(pr + 1, (q + 1) % 2)
                    dve.wait_ge(s_wz, 2 * pr + 2)
                    if not early:
                        dve.wait_ge(s_p1, pr - 1)
                        dve.wait_ge(s_p2, pr - 1)
                    magp = mag[:, bass.ds(pr, 1)] if not isinstance(pr, int) else mag[:, pr:pr + 1]
                    magb = magp.broadcast_to([P, T])
                    v.tensor_tensor_scan(zz[:, k, 0], magb, wz[:, k, 0], 0.0, ALU.mult, ALU.add)
                    v.tensor_tensor_scan(zz[:, k, 1], magb, wz[:, k, 1], 0.0, ALU.mult, ALU.add).then_inc(s_z, 1)
                    if q == 1 and not first:
                        y_of(r * 2 - 1, 1)
                    if q == 5:
                        y_of(r * 2, 0)
                if first:
                    dve.wait_ge(s_trig, 8)

            rounds(dve, KC // 2, s5_round)
            p1_of(PAIRS - 1, 1, False)
            y_of(KC - 1, 1)
            for ch in range(KC):
                gl_low(ch, 0)

            def y2_low(m):
                dve.wait_ge(s_y2hi, m + 1)
                v.tensor_tensor(h_lo[:, m], y2[:, m], h_hi[:, m].bitcast(F32), ALU.subtract).then_inc(s_hlo, 1)

            for m in range(8):
                cond_ring(2 + m, m % 2)
                dve.wait_ge(s_evac, PROJ["w_glu"] + m + 1)
                v.tensor_tensor(y2[:, m], gl[:, m], sig[:, m], ALU.mult).then_inc(s_y2, 1)
                if m:
                    y2_low(m - 1)
            y2_low(7)
            dve.wait_ge(s_cdone, 24 - PE_COLS)
            do(v.tensor_tensor(cond[:, 16:24], cond[:, 16:24], bcond[:, 16:24], ALU.add))
            for m in range(8):
                residual("w_out", 2, m)
                cond_ring(10 + m, m % 2)
            dve.wait_ge(s_cdone, 40 - PE_COLS)
            do(v.tensor_tensor(cond[:, 24:40], cond[:, 24:40], bcond[:, 24:40], ALU.add))
            scales(FFN0)
            st.sync()

            def top16(src, vals, idx, n):
                for g in range(0, n, 4):
                    rows = range(g, g + 4)
                    for i in rows:
                        st.add(v.max(vals[i][:, 0:8], src[i]))
                    st.sync()
                    for i in rows:
                        st.add(v.max_index(idx[i][:, 0:8], vals[i][:, 0:8], src[i]))
                    st.sync()
                    for i in rows:
                        st.add(v.match_replace(src[i], vals[i][:, 0:8], src[i], -3.0e38))
                    st.sync()
                    for i in rows:
                        st.add(v.max(vals[i][:, 8:16], src[i]))
                    st.sync()
                    for i in rows:
                        st.add(v.max_index(idx[i][:, 8:16], vals[i][:, 8:16], src[i]))
                st.sync()

            def peer(layer):
                for tb in range(TB):
                    dve.wait_ge(s_scev, 8 * layer + 4 * tb + 4)
                    hp = [(h, p) for h in range(HEADS) for p in range(2)]
                    top16([SC[tb][:, h, p] for h, p in hp], [v_top[:, h, p] for h, p in hp],
                          [ix_u[:, h, p] for h, p in hp], 2 * HEADS)
                    full = [P, HEADS, TOPK, TOPK]
                    st.add(v.tensor_copy(ix_f, ix_u))
                    do(v.tensor_tensor(CAND, v_top[:, :, 0].unsqueeze(3).broadcast_to(full),
                                       v_top[:, :, 1].unsqueeze(2).broadcast_to(full), ALU.add))
                    top16([CAND[:, h].rearrange("p a b -> p (a b)") for h in range(HEADS)],
                          [t_top[:, h] for h in range(HEADS)], [pos_u[:, h] for h in range(HEADS)], HEADS)
                    st.add(v.tensor_scalar(ab_u[:, 0], pos_u, 4, None, ALU.logical_shift_right))
                    do(v.tensor_scalar(ab_u[:, 1], pos_u, 15, None, ALU.bitwise_and))
                    do(v.tensor_copy(ab_f, ab_u))
                    io = iota[:, 0:TOPK].unsqueeze(1).unsqueeze(1).broadcast_to(full)
                    for half in range(2):
                        do(v.tensor_tensor(EQ, ab_f[:, half].unsqueeze(3).broadcast_to(full), io, ALU.is_equal))
                        do(v.tensor_tensor(EQ, EQ, ix_f[:, :, half].unsqueeze(2).broadcast_to(full), ALU.mult))
                        do(v.tensor_reduce(route[tb][:, half], EQ, axis=AX.X, op=ALU.add))
                    v.tensor_tensor(route[tb][:, 2], t_top, t_top[:, :, 0:1].broadcast_to([P, HEADS, TOPK]),
                                    ALU.subtract).then_inc(s_gsub, 1)
                for tb in range(TB):
                    dve.wait_ge(s_gexp, 2 * layer + tb + 1)
                    do(v.tensor_reduce(gsum[:, tb], route[tb][:, 2], axis=AX.X, op=ALU.add))
                    do(v.reciprocal(gsum[:, tb], gsum[:, tb]))
                    v.tensor_tensor(route[tb][:, 2], route[tb][:, 2],
                                    gsum[:, tb].unsqueeze(2).broadcast_to([P, HEADS, TOPK]), ALU.mult)\
                        .then_inc(s_route, 1)
                with dve.Fori(0, 6) as r:
                    for k in range(2):
                        cond_ring(r * 2 + (COND_U[layer] + k), k)
                for tb in range(TB):
                    dve.wait_ge(s_rt, 2 * layer + tb + 1)
                    cols = slice(tb * P, tb * P + P)
                    st.add(v.tensor_copy(i0T[:, cols], bank[6 + tb][:, 0:P]))
                    st.add(v.tensor_copy(i1T[:, cols], bank[6 + tb][:, P:2 * P]))
                    do(v.tensor_copy(g_part[:, 0, cols], bank[6 + tb][:, 2 * P:3 * P]))
                    do(v.tensor_tensor(g_rest[:, cols], bank[6 + tb][:, 2 * P:3 * P], g_part[:, 0, cols],
                                       ALU.subtract))
                    do(v.tensor_copy(g_part[:, 1, cols], g_rest[:, cols]))
                    v.tensor_tensor(g_part[:, 2, cols], g_rest[:, cols], g_part[:, 1, cols],
                                    ALU.subtract).then_inc(s_rtev, 1)
                dve.wait_ge(s_rtev, 2 * layer + 2)
                st.sync()
                base = 2 * HALF * layer
                su = AT[f"u{layer}"][2]

                def one_hots(group, k, g, half, first2):
                    for idx, out, first_key, width, s in ((i0T, eq_a, half * HALF, HALF, s_eqa),
                                                          (i1T, one_b, 0, P, s_oneb)):
                        tok = idx[:, g * 4:g * 4 + 4] if isinstance(g, int) else idx[:, bass.ds(g * 4, 4)]
                        if not first2:
                            dve.wait_ge(s_onea if s is s_eqa else s_gmm, group - 1)
                        v.tensor_tensor(out[:, k], tok.unsqueeze(2).broadcast_to([P, 4, width]),
                                        iota[:, first_key:first_key + width].unsqueeze(1)
                                        .broadcast_to([P, 4, width]), ALU.is_equal).then_inc(s, 1)

                def low(r, j, off):
                    dve.wait_ge(s_hi, r * 4 + (su + off + j + 1))
                    v.tensor_tensor(w_lo[:, j % 2], ring[:, j], w_hi[:, j % 2].bitcast(F32), ALU.subtract)\
                        .then_inc(s_lo, 1)

                def apply_gates(group, k, g, half):
                    if isinstance(g, int) and g == 0:
                        dve.wait_ge(s_evac, e_u + (half + 1) * HALF)
                    dve.wait_ge(s_gmm, group + 1)
                    rows = HB[:, half * HALF:half * HALF + HALF, :]
                    rows = rows[:, :, g * 4:g * 4 + 4] if isinstance(g, int) else rows[:, :, bass.ds(g * 4, 4)]
                    rows = rows.rearrange("p i t -> p t i")
                    v.tensor_tensor(rows, bank[6 + k][:, 0:4 * HALF].rearrange("p (t i) -> p t i", t=4),
                                    rows, ALU.mult).then_inc(s_gev, 1)

                def both(half, cond_block=None):
                    def body(r, first, last):
                        for j in range(SLOTS):
                            if cond_block is not None and j >= 2:
                                cond_ring(r * 2 + (cond_block + j - 2), j - 2)
                            g = r * SLOTS + j
                            if half == 0 and first and j == 0:
                                dve.wait_ge(s_lo, su + HALF + 1)
                            else:
                                low(r, j, HALF * (1 + half))
                            if not (last and j == 3):
                                one_hots(base + half * HALF + g + 1, (j + 1) % 2, g + 1, half,
                                         layer == 0 and half == 0 and first and j == 0)
                            elif half == 0:
                                one_hots(base + HALF, 0, 0, 1, False)
                            if not (first and j == 0):
                                apply_gates(base + half * HALF + g - 1, (j + 1) % 2, g - 1, half)
                            elif half == 1:
                                pass
                            if last and j == 3:
                                apply_gates(base + half * HALF + g, j % 2, g, half)
                    return body

                e_u = PROJ[f"u{layer}"] - 8 * (layer + 1)
                one_hots(base, 0, 0, 0, layer == 0)
                for k in range(2):
                    cond_ring(COND_U[layer] + 12 + k, k)
                rounds(dve, HALF // SLOTS, both(0))
                def last_half(cond_block):
                    def body(r, first, last):
                        for j in range(SLOTS):
                            low(r, j, 3 * HALF)
                            if cond_block is not None and j % 2:
                                cond_ring(r * 2 + (cond_block + j // 2), j // 2)
                    return body

                n1 = HALF // SLOTS
                if layer == 0:
                    both(1)(0, True, False)
                    middle(dve, 1, 10, both(1, COND_V1 - 2))
                    middle(dve, 10, n1 - 1, both(1))
                    both(1)(n1 - 1, False, True)
                    middle(dve, 0, n1, last_half(COND_V2[0]))
                    for group in (2, 3, 4):
                        cond_bias(group)
                    scales(FFN1)
                    scales(KVN)
                    scales(MIX1)
                else:
                    rounds(dve, n1, both(1))
                    middle(dve, 0, 5, last_half(COND_V2[1]))
                    middle(dve, 5, n1, last_half(None))
                    cond_bias(5)
                    scales(FINAL)
                st.sync()
                dve.wait_ge(s_split, su + 2 * EB)
                for ch in range(KC):
                    v.scalar_tensor_tensor(xT[:, ch], bank[2 + ch // 2][:, (ch % 2) * T:(ch % 2) * T + T],
                                           vec(6 * layer + 5, ch), xT[:, ch], ALU.mult, ALU.add).then_inc(s_x, 1)

            stats(1)
            normalise(FFN0, hT)
            low_halves(FFN0, hT, h_hi, h_lo, 8)
            peer(0)

            stats(2)
            normalise(KVN, hkv)
            low_halves(KVN, hkv, h_hi, h_lo, 16)
            normalise(MIX1, hT)
            low_halves(MIX1, hT, hq_hi, hq_lo, 24)
            dve.wait_ge(s_attin, 80)
            c1 = 6.28125
            c2 = float(np.float32(round((TWO_PI - c1) * 2.0 ** 21) / 2.0 ** 21))
            c3 = float(np.float32(TWO_PI - c1 - c2))
            do(v.tensor_copy(rtmp[:, 1], pos_i))
            do(v.tensor_scalar(rtmp[:, 1], rtmp[:, 1], freq, None, ALU.mult))
            do(v.tensor_scalar(rtmp[:, 2], rtmp[:, 1], inv, MAGIC, ALU.mult, ALU.add))
            do(v.tensor_scalar(rtmp[:, 2], rtmp[:, 2], -MAGIC, None, ALU.add))
            for cc in (c1, c2, c3):
                do(v.scalar_tensor_tensor(rtmp[:, 1], rtmp[:, 2], -cc, rtmp[:, 1], ALU.mult, ALU.add))
            v.tensor_scalar(rtmp[:, 0], rtmp[:, 1], 3.1415925, -3.1415925, ALU.min, ALU.max).then_inc(s_rang, 1)
            dve.wait_ge(s_rtrig, 2)

            def rope(m):
                src, dst = (kraw[:, m], krot[:, m]) if m < 2 else (qraw[:, m - 2], qrot[:, m - 2])
                dve.wait_ge(s_evac, (PROJ["w_kv"] + m + 1 if m < 2 else PROJ["attn_q"] + m - 1) - 8)
                st.add(v.tensor_tensor(ropet[:, 0], src, rcos, ALU.mult))
                dve.wait_ge(s_rmm, m + 1)
                st.add(v.tensor_tensor(ropet[:, 1], bank[4][:, 0:T], rsin, ALU.mult))
                st.sync()
                v.tensor_tensor(dst, ropet[:, 0], ropet[:, 1], ALU.add).then_inc(s_rope, 1)
                dve.wait_ge(s_rope, m + 1)

            def masked(s):
                kv, tb = s // 2, s % 2
                k0, nk = (P, P) if tb == 0 else (0, T)
                own, k = s_sb[s % 3], s % 2
                dve.wait_ge(s_s, s + 1)
                if s >= 3:
                    dve.wait_ge(s_pt, transposed(s - 2))
                for r in range(2):
                    st.add(v.scalar_tensor_tensor(
                        own[:, r, :, k0:k0 + nk],
                        bank[2 + r][:, :].rearrange("p (a b) -> p a b", a=2)[:, :, k0:k0 + nk],
                        0.125, masks[:, k0:k0 + nk].unsqueeze(1).broadcast_to([P, 2, nk]), ALU.mult, ALU.add))
                st.sync()
                do(v.tensor_reduce(rowm[k], own[:, :, :, k0:k0 + nk], axis=AX.X, op=ALU.max))
                do(v.tensor_tensor(rowm[k], rowm[k], sinks[:, kv], ALU.max))
                st.add(v.tensor_scalar(nrowm[k], rowm[k], -1.0, None, ALU.mult))
                st.sync()
                v.tensor_tensor(esink[k], sinks[:, kv], rowm[k], ALU.subtract).then_inc(s_sm, 1)

            def probabilities(s):
                k0, nk = (P, P) if s % 2 == 0 else (0, T)
                flat, k = s_sb[s % 3][:, :, :, k0:k0 + nk], s % 2
                dve.wait_ge(s_p, 5 * (s + 1))
                do(v.tensor_tensor(rsum[k], rsum[k], esink[k], ALU.add))
                do(v.reciprocal(rsum[k], rsum[k]))
                v.tensor_tensor(flat, flat, rsum[k].rearrange("p (a b) -> p a b", a=2).unsqueeze(3)
                                .broadcast_to([P, 2, 2, nk]), ALU.mult).then_inc(s_pn, 1)
                dve.wait_ge(s_pn, s + 1)

            def output_low(s):
                kv, tb = s // 2, s % 2
                dve.wait_ge(s_oev, s + 1)
                part = (slice(None), slice(2 * kv, 2 * kv + 2), slice(tb * P, tb * P + P))
                v.tensor_tensor(h_lo[part], bank[5][:, 0:T].rearrange("p (a b) -> p a b", a=2),
                                h_hi[part].bitcast(F32), ALU.subtract).then_inc(s_olo, 1)

            rope(0)
            rope(1)
            for i in range(1, 14):
                if i >= 6:
                    output_low(i - 6)
                if i <= 8:
                    rope(i + 1)
                if 3 <= i < 11:
                    masked(i - 3)
                if 4 <= i < 12:
                    probabilities(i - 4)
            for m in range(8):
                residual("w_o", 8, m)
            stats(3)
            normalise(FFN1, hT)
            low_halves(FFN1, hT, h_hi, h_lo, 32)
            peer(1)
            stats(4)
            normalise(FINAL, hT)

        @block.tensor
        def _(pe):
            mm = nc.tensor.matmul

            def arrived(name, m):
                n = AT[name][0] + m
                pe.wait_ge(s_slot[n % 4], 16 * (n // 4 + 1))

            def split_product(name, m, hi_, lo_, chunk_hi=None, chunk_lo=None):
                b, out = AT[name][2] + m, bank[m % 2][:, 0:T]
                pe.wait_ge(s_hi, b + 1)
                if chunk_hi is None:
                    for kc in range(KC):
                        mm(out, w_hi[:, b % 2, kc], hi_[:, kc], start=kc == 0, stop=False)
                        mm(out, w_hi[:, b % 2, kc], lo_[:, kc], start=False, stop=False)
                else:
                    for kc in range(KC):
                        pe.wait_ge(chunk_hi[0], chunk_hi[1] + kc + 1)
                        mm(out, w_hi[:, b % 2, kc], hi_[:, kc], start=kc == 0, stop=False)
                    for kc in range(KC):
                        pe.wait_ge(chunk_lo[0], chunk_lo[1] + kc + 1)
                        mm(out, w_hi[:, b % 2, kc], lo_[:, kc], start=False, stop=False)
                pe.wait_ge(s_lo, b + 1)
                for kc in range(KC):
                    last = mm(out, w_lo[:, b % 2, kc], hi_[:, kc], start=False, stop=kc == KC - 1)
                last.then_inc(s_split, 1)

            def sum_squares(k, ch):
                pe.wait_ge(s_sq, ch // 4 + 1 if k == 0 else 2 + 8 * (k - 1) + ch + 1)
                src = NORM_MEM[0][0][ch // 4][:, ch % 4] if k == 0 else sq[:, ch]
                last = mm(bank[6][:, 0:T], ones[:], src, start=ch == 0, stop=ch == KC - 1)
                if ch == KC - 1:
                    last.then_inc(s_ms, 1)

            pe.wait_ge(s_ones, 2)
            def first_column(i):
                k = first_slot(i)
                pe.wait_ge(s_c0[k], 16 * first_use(i))
                for kc in range(KC):
                    last = mm(bank[7][:, i:i + 1], cond0[k][:, kc * P:kc * P + P], c_col[:, kc:kc + 1],
                              start=kc == 0, stop=kc == KC - 1)
                last.then_inc(s_cpe, 1)

            pe.wait_ge(s_silu, 1)
            for i in range(3):
                first_column(i)
            for ch in range(KC):
                sum_squares(0, ch)
            for i in range(3, PE_COLS):
                first_column(i)
            pe.wait_ge(s_bb, 2)
            for ch in range(KC):
                if ch >= 2:
                    pe.wait_ge(s_bbev, ch - 1)
                for i, b in enumerate((bb_re, bb_im)):
                    last = nc.tensor.transpose(bank[4 + ch % 2][:, i * P:i * P + P],
                                               b[:, 4 * ch:4 * ch + 4].rearrange("p a b -> p (a b)"), ident[:])
                last.then_inc(s_bbt, 1)

            def w_in_part(m, part):
                if part == 0:
                    arrived("w_in", m)
                    if m >= 2:
                        pe.wait_ge(s_evac, m - 1)
                for kc in (2 * part, 2 * part + 1):
                    if m == 0:
                        pe.wait_ge(s_h, kc + 1)
                    last = mm(bank[m % 2][:, 0:T], ring[:, m % 4, kc], hT[:, kc], start=kc == 0,
                              stop=kc == KC - 1)
                if part == 3:
                    last.then_inc(s_plain, 1)

            for m in range(2):
                for part in range(4):
                    w_in_part(m, part)
            pe.wait_ge(s_bbev, 8)
            pe.wait_ge(s_cneg, 2)

            def bu_of(pr):
                ch, q = pr // 4, pr % 4
                if q == 0:
                    pe.wait_ge(s_evac, ch + 1)
                if pr >= 4:
                    pe.wait_ge(s_buev, pr - 3)
                rows = slice(32 * q, 32 * q + 32)
                for i in range(2):
                    last = mm(bank[2 + q][:, i * T:i * T + T], bbt[rows, ch, i], uT[rows, ch], start=True,
                              stop=True)
                last.then_inc(s_bu, 1)

            for pr in range(4):
                bu_of(pr)
            for ch in range(KC):
                for q in range(4):
                    pr = 4 * ch + q
                    if pr + 4 < PAIRS:
                        bu_of(pr + 4)
                    if ch + 2 < KC:
                        w_in_part(ch + 2, q)
                    pe.wait_ge(s_p1, pr + 1)
                    pe.wait_ge(s_p2, pr + 1)
                    if q == 0 and ch >= 2:
                        pe.wait_ge(s_yev, ch - 1)
                    out = bank[6 + ch % 2][32 * q:32 * q + 32, 0:T]
                    k = q % 2
                    mm(out, c_re[:, pr], p1[:, k, 0], start=True, stop=False)
                    mm(out, c_nre[:, pr], p2[:, k, 1], start=False, stop=False)
                    mm(out, c_im[:, pr], p1[:, k, 1], start=False, stop=False)
                    mm(out, c_im[:, pr], p2[:, k, 0], start=False, stop=True).then_inc(s_y, 1)
            for m in range(8):
                if m >= 2:
                    pe.wait_ge(s_evac, PROJ["w_glu"] + m - 1)
                fresh = m == 0
                split_product("w_glu", m, gl_hi, gl_lo, (s_gl, 0) if fresh else None,
                              (s_hlo, LOW_AT["gl"]) if fresh else None)

            def project_x(name, x0, k, chunk_hi=None, chunk_lo=None):
                for m in range(8):
                    if m >= 2:
                        pe.wait_ge(s_x, x0 + m - 1)
                    split_product(name, m, h_hi, h_lo, *((chunk_hi, chunk_lo) if m == 0 else (None, None)))
                    if m >= 1:
                        sum_squares(k, m - 1)
                sum_squares(k, KC - 1)

            pe.wait_ge(s_evac, PROJ["w_glu"] + 8)
            project_x("w_out", 0, 1, (s_y2hi, 0), (s_hlo, LOW_AT["y2"]))

            def peer(layer):
                n0, _, s0 = AT[f"u{layer}"]
                name = f"peer_q{layer}"
                for m in range(8):
                    if m >= 2:
                        pe.wait_ge(s_evac, PROJ[name] - DONE_BY_X[name] + m - 1)
                    split_product(name, m, h_hi, h_lo, (s_h, 8 * (1 + 3 * layer)) if m == 0 else None,
                                  (s_hlo, LOW_AT[f"ffn{layer}"]) if m == 0 else None)
                pe.wait_ge(s_keys, 16 * (layer + 1))
                e0 = PROJ[name] - DONE_BY_X[name] + 8
                pe.wait_ge(s_evac, e0)
                for tb in range(TB):
                    for h in range(HEADS):
                        if tb == 1 and h in (4, 6):
                            pe.wait_ge(s_scev, 8 * layer + h // 2 - 1)
                        last = mm(bank[SCORE_BANKS[tb][h // 2]][:, (h % 2) * T:(h % 2) * T + T],
                                  qT[:, h, tb * P:tb * P + P], KEYS[:, h], start=True, stop=True)
                        if h % 2:
                            last.then_inc(s_sc, 1)

                def u_block(r, j, half):
                    b = r * STRIDE + (s0 + half * HALF + j)
                    pe.wait_ge(s_hi, b + 1)
                    pe.wait_ge(s_evac, r * STRIDE + (e0 + half * HALF + j - 1))
                    out, k = bank[j % 2][:, 0:T], j % 2
                    for kc in range(KC):
                        mm(out, w_hi[:, k, kc], h_hi[:, kc], start=kc == 0, stop=False)
                        mm(out, w_hi[:, k, kc], h_lo[:, kc], start=False, stop=False)
                    pe.wait_ge(s_lo, b + 1)
                    for kc in range(KC):
                        last = mm(out, w_lo[:, k, kc], h_hi[:, kc], start=False, stop=kc == KC - 1)
                    last.then_inc(s_split, 1)

                def gate_group(group, j, first2):
                    pe.wait_ge(s_oneb, group + 1)
                    pe.wait_ge(s_onea, group + 1)
                    if not first2:
                        pe.wait_ge(s_gev, group - 1)
                    k = j % 2
                    for t in range(4):
                        out = bank[6 + k][:, t * HALF:t * HALF + HALF]
                        for part in range(3):
                            last = mm(out, one_b[:, k, t], one_g[:, k, part, t], start=part == 0,
                                      stop=part == 2)
                    last.then_inc(s_gmm, 1)

                n1 = HALF // STRIDE

                def u1(r, first, last):
                    for j in range(STRIDE):
                        u_block(r, j, 0)

                middle(pe, 0, n1 - 1, u1)
                for tb in range(TB):
                    pe.wait_ge(s_route, 2 * layer + tb + 1)
                    for i in range(3):
                        last = nc.tensor.transpose(bank[6 + tb][:, i * P:i * P + P],
                                                   route[tb][:, i].rearrange("p a b -> p (a b)"), ident[:])
                    last.then_inc(s_rt, 1)
                u1(n1 - 1, False, True)
                base = 2 * HALF * layer

                def u2(r, first, last):
                    for j in range(STRIDE):
                        u_block(r, j, 1)
                        gate_group(base + r * STRIDE + j, j, layer == 0 and first and j < 2)

                rounds(pe, HALF // STRIDE, u2)
                for b in range(4):
                    mm(bank[2 + b][:, :], zeros[:], ring0[:, 0:512], start=True, stop=False)

                def v_block(r, j, half, final):
                    b = r * STRIDE + (s0 + EB + half * HALF + j)
                    a = r * STRIDE + (EB * layer + half * HALF + j)
                    k = j % 2
                    pe.wait_ge(s_hi, b + 1)
                    pe.wait_ge(s_ahi, a + 1)
                    pe.wait_ge(s_alo, a + 1)
                    for ch in range(KC):
                        out = bank[2 + ch // 2][:, (ch % 2) * T:(ch % 2) * T + T]
                        mm(out, w_hi[:, k, ch], a_hi[:, k], start=False, stop=False)
                        mm(out, w_hi[:, k, ch], a_lo[:, k], start=False, stop=False)
                    pe.wait_ge(s_lo, b + 1)
                    for ch in range(KC):
                        out = bank[2 + ch // 2][:, (ch % 2) * T:(ch % 2) * T + T]
                        last = mm(out, w_lo[:, k, ch], a_hi[:, k], start=False, stop=final and ch % 2 == 1)
                    last.then_inc(s_split, 1)

                def v1(r, first, last):
                    for j in range(STRIDE):
                        gate_group(base + HALF + r * STRIDE + j, j, False)
                        v_block(r, j, 0, False)

                rounds(pe, HALF // STRIDE, v1)

                def v2(r, first, last):
                    for j in range(STRIDE):
                        v_block(r, j, 1, last and j == STRIDE - 1)

                rounds(pe, HALF // STRIDE, v2)

            DONE_BY_X = {"peer_q0": 8, "w_kv": 8, "attn_q": 8, "peer_q1": 16}
            ring0 = xT[:, 0:2].rearrange("p a b -> p (a b)")
            peer(0)

            for ch in range(KC):
                sum_squares(2, ch)
            e0 = PROJ["w_kv"] - 8

            def rotate(m):
                if m == 0:
                    pe.wait_ge(s_attin, 80)
                pe.wait_ge(s_evac, e0 + (m + 1 if m < 2 else m + 3))
                if m:
                    pe.wait_ge(s_rope, m)
                src = kraw[:, m] if m < 2 else qraw[:, m - 2]
                mm(bank[4][:, 0:T], rot, src, start=True, stop=True).then_inc(s_rmm, 1)

            for m in range(4):
                if m >= 2:
                    pe.wait_ge(s_evac, e0 + m - 1)
                split_product("w_kv", m, h_hi, h_lo, (s_h, 16) if m == 0 else None,
                              (s_hlo, LOW_AT["kv"]) if m == 0 else None)
            rotate(0)

            def scores(s):
                kv, tb = s // 2, s % 2
                pe.wait_ge(s_rope, 2 * kv + 4)
                if s == 0:
                    pe.wait_ge(s_kdup, 64)
                else:
                    pe.wait_ge(s_sm, s)
                keys = slice(0, P) if tb == 0 else slice(0, T)
                for r in range(2):
                    rows = slice(64 * r, 64 * r + 64)
                    for mh in range(2):
                        c0 = mh * T + (P if tb == 0 else 0)
                        last = mm(bank[2 + r][:, c0:mh * T + T], qrot[rows, 2 * kv + mh, tb * P:tb * P + P],
                                  kdup[rows, kv, keys], start=True, stop=True)
                last.then_inc(s_s, 1)

            for i in range(13):
                if i < 8:
                    pe.wait_ge(s_evac, e0 + 4 + i - 1)
                    split_product("attn_q", i, hq_hi, hq_lo, (s_h, 24) if i == 0 else None,
                                  (s_hlo, LOW_AT["mix1"]) if i == 0 else None)
                if i == 0:
                    rotate(1)
                    pe.wait_ge(s_evac, e0 + 4)
                    for m in range(2):
                        for tb in range(TB):
                            last = nc.tensor.transpose(bank[7][:, (m * 2 + tb) * P:(m * 2 + tb + 1) * P],
                                                       vT[:, m, tb * P:tb * P + P], ident[:])
                    last.then_inc(s_vt, 1)
                if 8 <= i < 11:
                    scores(i - 3)
                if i >= 5:
                    s = i - 5
                    n = transposed(s)
                    kbs = range(1 - s % 2, 2)
                    pe.wait_ge(s_pn, s + 1)
                    if n:
                        pe.wait_ge(s_ptev, n)
                    for kb in kbs:
                        for head in range(4):
                            last = nc.tensor.transpose(
                                bank[6 + kb][:, head * P:head * P + P],
                                s_sb[s % 3][:, head // 2, head % 2, kb * P:kb * P + P], ident[:])
                        last.then_inc(s_pt, 1)
                if 1 <= i <= 8:
                    rotate(i + 1)
                if 3 <= i < 8:
                    scores(i - 3)
                if i >= 5:
                    s = i - 5
                    kv, tb = s // 2, s % 2
                    n = transposed(s)
                    kbs = range(1 - tb, 2)
                    pe.wait_ge(s_ptev, n + len(kbs))
                    if s:
                        pe.wait_ge(s_olo, s)
                    else:
                        pe.wait_ge(s_vtev, 1)
                    for r in range(2):
                        for kb in kbs:
                            vb = kb if tb == 1 else 0
                            last = mm(bank[5][64 * r:64 * r + 64, 0:T], vN[:, vb, kv * 64:kv * 64 + 64],
                                      pT[s % 2][:, kb, 2 * r:2 * r + 2].rearrange("p a b -> p (a b)"),
                                      start=kb == kbs[0], stop=kb == kbs[-1])
                    last.then_inc(s_o, 1)
            pe.wait_ge(s_olo, 8)
            project_x("w_o", 16, 3)
            peer(1)
            for ch in range(KC):
                sum_squares(4, ch)


_INS = ["x_t", "c_col_d", "c_row_d", "b_cond", "norms", "ident_d", "iota_d", "time_d", "w_cond0", "w_cond", "w_in", "w_glu", "w_out",
        "s5_lam", "s5_b", "s5_c", "s5_d", "b_glu", "peer_wq", "keys_d", "u_tab", "v_tab", "w_kv", "attn_wq",
        "w_o", "sinks_d", "pos_d", "masks_d", "rot_d", "freq_d"]


def lay_out(x, c, positions, w_cond, b_cond, norm_mix, norm_ffn, s5_w_in, s5_a_re, s5_a_im, s5_log_dt,
            s5_b_re, s5_b_im, s5_c_re, s5_c_im, s5_d, s5_w_glu, s5_b_glu, s5_w_out, kv_norm, w_kv, attn_w_q,
            attn_sinks, attn_w_o, peer_w_q, peer_sub_keys, peer_u, peer_v, final_norm):
    f = np.float32

    def blocks(w):
        n = w.shape[-1] // P
        return np.ascontiguousarray(w.reshape(KC, P, n, P).transpose(2, 1, 0, 3)).reshape(n, P, D)

    def cols(v):
        return np.ascontiguousarray(v.reshape(-1, P).T)

    def pair(a):
        return a.reshape(PAIRS, 2, 64).transpose(1, 2, 0).reshape(P, PAIRS)

    def pad(a):
        out = np.zeros((2, 64, PAIRS, 2, 16), f)
        a = a.reshape(PAIRS, 2, 64, 16)
        for g in range(2):
            out[g, :, :, g, :] = a[:, g].transpose(1, 0, 2)
        return out.reshape(P, PAIRS, 32)

    keys = np.zeros((2, 2, 64, HEADS, 2, P), f)
    for half in range(2):
        keys[:, half, :, :, half, :] = peer_sub_keys[:, :, half].transpose(0, 3, 1, 2)
    qi = np.arange(P)[:, None]
    kj = np.arange(P)[None, :]
    masks = np.concatenate([np.where(kj > qi, 0.0, NEG), np.where(kj <= qi, 0.0, NEG)], axis=1).astype(f)
    rot = np.zeros((P, P), f)
    for h in range(2):
        for i in range(32):
            rot[64 * h + 32 + i, 64 * h + i] = -1.0
            rot[64 * h + i, 64 * h + 32 + i] = 1.0
    inv_freq = (f(10000.0) ** (-np.arange(0, 64, 2, dtype=f) / f(64))).astype(f)
    order = list(COND_AT)
    cond_rows = w_cond.T.reshape(16, KC, P, D)[order].reshape(P, P, D)
    log_dt = np.broadcast_to(s5_log_dt[0][:, None], (64, 64))
    return {
        "x_t": np.ascontiguousarray(x[0].T.reshape(KC, P, T).transpose(1, 0, 2)),
        "c_col_d": cols(c[0]),
        "c_row_d": np.ascontiguousarray(np.broadcast_to(c[0], (P, D))),
        "b_cond": np.ascontiguousarray(cols(b_cond).reshape(P, 16, KC)[:, order].reshape(P, P)),
        "norms": np.ascontiguousarray(np.stack([cols(v) for v in (norm_mix[0], norm_ffn[0], kv_norm, norm_mix[1],
                                                                 norm_ffn[1], final_norm)], axis=1)),
        "ident_d": np.eye(P, dtype=f),
        "iota_d": np.ascontiguousarray(np.broadcast_to(np.arange(P, dtype=f), (P, P))),
        "time_d": np.ascontiguousarray(np.broadcast_to(np.arange(T, dtype=f), (P, T))),
        "w_cond0": np.concatenate([cond_rows[0:PE_COLS].reshape(PE_COLS, P, KC, P).transpose(0, 3, 2, 1)
                                   .reshape(PE_COLS, P, D), cond_rows[PE_COLS:FIRST_COLS]]),
        "w_cond": np.ascontiguousarray(cond_rows[FIRST_COLS:]), "w_in": blocks(s5_w_in[0]), "w_glu": blocks(s5_w_glu[0]),
        "w_out": blocks(s5_w_out[0]),
        "s5_lam": np.ascontiguousarray(np.stack([pair(s5_a_re[0]), pair(s5_a_im[0]), pair(log_dt)], axis=1)),
        "s5_b": np.ascontiguousarray(np.stack([pad(s5_b_re[0]), pad(s5_b_im[0])], axis=1)),
        "s5_c": np.ascontiguousarray(np.stack([pad(s5_c_re[0].transpose(0, 2, 1)),
                                               pad(s5_c_im[0].transpose(0, 2, 1))], axis=1)),
        "s5_d": cols(s5_d[0].reshape(-1)), "b_glu": cols(s5_b_glu[0]),
        "peer_wq": np.stack([blocks(peer_w_q[i]) for i in range(2)]),
        "keys_d": keys.reshape(2, P, HEADS, 2 * P),
        "u_tab": np.ascontiguousarray(peer_u.reshape(2, EB, P, KC, P).transpose(0, 1, 4, 3, 2)).reshape(2, EB, P, D),
        "v_tab": peer_v.reshape(2, EB, P, D),
        "w_kv": blocks(w_kv), "attn_wq": blocks(attn_w_q[0]), "w_o": blocks(attn_w_o[0]),
        "sinks_d": np.ascontiguousarray(np.broadcast_to(
            attn_sinks[0].reshape(4, 2, 2).transpose(0, 2, 1).reshape(1, 4, 4), (P, 4, 4))),
        "pos_d": np.ascontiguousarray(np.broadcast_to(positions[0][None, :], (P, T))),
        "masks_d": masks, "rot_d": rot,
        "freq_d": np.ascontiguousarray(np.tile(inv_freq, 4)[:, None]),
    }


def kernel(**inputs):
    import concourse.bacc as bacc
    from concourse.bass_utils import run_bass_kernel_spmd

    arrays = lay_out(**{k: np.asarray(a) for k, a in inputs.items()})
    nc = bacc.Bacc("TRN2", target_bir_lowering=False, num_devices=1, dynamic_dma_scratch_size=1024)
    args = [nc.dram_tensor(n, arrays[n].shape, mybir.dt.from_np(arrays[n].dtype), kind="ExternalInput").ap()
            for n in _INS]
    out = nc.dram_tensor("out_t", (P, KC, T), F32, kind="ExternalOutput").ap()
    build(nc, *args, out)
    r = run_bass_kernel_spmd(nc, [arrays], core_ids=[0])
    got = r.results[0]["out_t"]
    return np.ascontiguousarray(got.transpose(2, 1, 0).reshape(1, T, D))
```
